# Optimizing a Trainium2 kernel written in Bass

```python
import jax
import jax.numpy as jnp
from jax import lax
import numpy as np

D_MODEL = 2048
BATCH = 1
SEQ = 1024
DEPTH = 1
DEC_BATCH = 8
DEC_SEQ = 1
PAST_LEN = 1024
PAGE_SIZE = 128

N_META = 16
POOL_WINDOWS = (2, 4, 8, 16)
N_POOL_GROUPS = len(POOL_WINDOWS)
POOL_W = D_MODEL // 2
POOL_GROUP = POOL_W // N_POOL_GROUPS
POOL_PAD = max(POOL_WINDOWS) - 1
ATTN_W = D_MODEL // 2
HEAD_DIM = 128
N_HEADS = ATTN_W // HEAD_DIM
N_KV_HEADS = 2
GQA_GROUP = N_HEADS // N_KV_HEADS
N_IDX_HEADS = 16
IDX_DIM = 64
TOPK_MAX = 256
Q_BLOCK = 128
D_MIX = POOL_W + ATTN_W
SPLIT_WIDTHS = (POOL_W, POOL_W, N_HEADS * HEAD_DIM, N_KV_HEADS * HEAD_DIM, N_KV_HEADS * HEAD_DIM,
                ATTN_W, N_IDX_HEADS * IDX_DIM, IDX_DIM, N_IDX_HEADS)
D_IN_PROJ = sum(SPLIT_WIDTHS)
RMS_EPS = 1e-6

kernel_name = 'hymba_pool_dsa_alibi_step'

def rmsnorm(x, g):
    xf = x.astype(jnp.float32)
    y = xf * lax.rsqrt(jnp.mean(xf * xf, axis=-1, keepdims=True) + RMS_EPS)
    return (y * g.astype(jnp.float32)).astype(x.dtype)

def alibi_slopes():
    i = jnp.arange(1, N_HEADS + 1, dtype=jnp.float32)
    return jnp.exp2(-8.0 * i / N_HEADS).reshape(N_KV_HEADS, GQA_GROUP)

def topk_count(n_keys):
    return max(1, min(TOPK_MAX, n_keys // 4))

def in_projection(h, norm_g, w_in):
    B, T, _ = h.shape
    hn = rmsnorm(h, norm_g)
    cuts = np.cumsum(SPLIT_WIDTHS)[:-1].tolist()
    u, z_pool, q, k, v, z_attn, qi, ki, wi = jnp.split(hn @ w_in, cuts, axis=-1)
    q = q.reshape(B, T, N_KV_HEADS, GQA_GROUP, HEAD_DIM)
    k = k.reshape(B, T, N_KV_HEADS, HEAD_DIM)
    v = v.reshape(B, T, N_KV_HEADS, HEAD_DIM)
    qi = qi.reshape(B, T, N_IDX_HEADS, IDX_DIM)
    return u, z_pool, q, k, v, z_attn, qi, ki, wi

def pool_branch(u_prefix, u, z, pos, w_pool, pool_scale):
    B, T, _ = u.shape
    u_ext = jnp.concatenate([u_prefix.astype(u.dtype), u], axis=1)
    cs = jnp.cumsum(u_ext.astype(jnp.float32), axis=1)
    cs = jnp.concatenate([jnp.zeros((B, 1, POOL_W), jnp.float32), cs], axis=1)
    end = cs[:, POOL_PAD + 1:]
    means = []
    for g, w in enumerate(POOL_WINDOWS):
        sl = slice(g * POOL_GROUP, (g + 1) * POOL_GROUP)
        start = cs[:, POOL_PAD + 1 - w: POOL_PAD + 1 - w + T, sl]
        cnt = jnp.minimum(pos + 1, w).astype(jnp.float32)[None, :, None]
        means.append((end[..., sl] - start) / cnt)
    mixed = (jnp.concatenate(means, axis=-1) - u.astype(jnp.float32)).astype(u.dtype)
    mixed = jnp.einsum('btgc,gcd->btgd', mixed.reshape(B, T, N_POOL_GROUPS, POOL_GROUP), w_pool)
    out = mixed.reshape(B, T, POOL_W) * pool_scale * jax.nn.silu(z)
    return out, u_ext[:, -POOL_PAD:]

def indexer_select(qi, wi, ki, q_pos, n_sel):
    S = ki.shape[1]
    logits = jnp.einsum('bthd,bsd->bths', qi, ki).astype(jnp.float32) * IDX_DIM ** -0.5
    score = jnp.einsum('bth,bths->bts', wi.astype(jnp.float32) * N_IDX_HEADS ** -0.5, jax.nn.relu(logits))
    visible = jnp.arange(S)[None, :] <= q_pos[:, None]
    score = jnp.where(visible[None], score, -jnp.inf)
    vals, idx = lax.top_k(score, n_sel)
    return idx, jnp.isfinite(vals)

def sparse_attend(q, k_sel, v_sel, q_pos, idx, valid):
    B, T = q.shape[:2]
    s = jnp.einsum('btgrd,btkgd->btgrk', q, k_sel).astype(jnp.float32) * HEAD_DIM ** -0.5
    dist = (q_pos[None, :, None] - idx).astype(jnp.float32)
    s = s - alibi_slopes()[None, None, :, :, None] * dist[:, :, None, None, :]
    s = jnp.where(valid[:, :, None, None, :], s, -jnp.inf)
    p = jax.nn.softmax(s, axis=-1).astype(v_sel.dtype)
    o = jnp.einsum('btgrk,btkgd->btgrd', p, v_sel)
    return o.reshape(B, T, ATTN_W)

def prompt_attention(q, k, v, qi, ki, wi):
    B, L = k.shape[:2]
    n_sel = topk_count(L)
    n_blk = -(-L // Q_BLOCK)
    pad = n_blk * Q_BLOCK - L

    def blocks(a):
        a = jnp.pad(a, [(0, 0), (0, pad)] + [(0, 0)] * (a.ndim - 2))
        return jnp.moveaxis(a.reshape((B, n_blk, Q_BLOCK) + a.shape[2:]), 1, 0)

    pos_blocks = jnp.arange(n_blk * Q_BLOCK).reshape(n_blk, Q_BLOCK)
    bidx = jnp.arange(B)[:, None, None]

    def one_block(args):
        qb, qib, wib, pb = args
        idx, valid = indexer_select(qib, wib, ki, pb, n_sel)
        return sparse_attend(qb, k[bidx, idx], v[bidx, idx], pb, idx, valid)

    o = lax.map(one_block, (blocks(q), blocks(qi), blocks(wi), pos_blocks))
    return jnp.moveaxis(o, 0, 1).reshape(B, n_blk * Q_BLOCK, ATTN_W)[:, :L]

def sample_attention(q, k, v, qi, ki, wi, q_pos, cache_k, cache_v, cache_idx_k, page_table):
    B, T = k.shape[:2]
    past = page_table.shape[1] * PAGE_SIZE
    ki_past = cache_idx_k[page_table].reshape(B, past, IDX_DIM).astype(ki.dtype)
    ki_all = jnp.concatenate([ki_past, ki], axis=1)
    idx, valid = indexer_select(qi, wi, ki_all, q_pos, topk_count(past + T))
    bidx = jnp.arange(B)[:, None, None]
    in_past = idx < past
    pidx = jnp.minimum(idx, past - 1)
    phys = page_table[bidx, pidx // PAGE_SIZE]
    off = pidx % PAGE_SIZE
    nidx = jnp.clip(idx - past, 0, T - 1)

    def pick(cache, new):
        return jnp.where(in_past[..., None, None], cache[phys, off].astype(new.dtype), new[bidx, nidx])

    return sparse_attend(q, pick(cache_k, k), pick(cache_v, v), q_pos, idx, valid)

def merge_residual(h, o_pool, o_attn, z_attn, w_out):
    return h + jnp.concatenate([o_pool, o_attn * jax.nn.silu(z_attn)], axis=-1) @ w_out

def setup_inputs(seed: int = 0) -> dict:
    key = jax.random.key(seed)
    ks = jax.random.split(key, 14)
    n_pages = PAST_LEN // PAGE_SIZE
    n_used = DEC_BATCH * n_pages
    n_phys = n_used + max(1, n_used // 4)
    nrm = jax.random.normal
    page_table = jax.random.permutation(ks[0], n_phys)[:n_used].reshape(DEC_BATCH, n_pages).astype(jnp.int32)
    return {
        'x_prompt': nrm(ks[1], (BATCH, SEQ, D_MODEL), jnp.float32),
        'x_sample': nrm(ks[2], (DEC_BATCH, DEC_SEQ, D_MODEL), jnp.float32),
        'cache_k': nrm(ks[3], (DEPTH, n_phys, PAGE_SIZE, N_KV_HEADS, HEAD_DIM), jnp.float32),
        'cache_v': nrm(ks[4], (DEPTH, n_phys, PAGE_SIZE, N_KV_HEADS, HEAD_DIM), jnp.float32),
        'cache_idx_k': nrm(ks[5], (DEPTH, n_phys, PAGE_SIZE, IDX_DIM), jnp.float32),
        'state_pool': nrm(ks[6], (DEPTH, DEC_BATCH, POOL_PAD, POOL_W), jnp.float32),
        'page_table': page_table,
        'meta_tokens': nrm(ks[7], (N_META, D_MODEL), jnp.float32),
        'norm_g': 1.0 + 0.1 * nrm(ks[8], (DEPTH, D_MODEL), jnp.float32),
        'w_in': nrm(ks[9], (DEPTH, D_MODEL, D_IN_PROJ), jnp.float32) * D_MODEL ** -0.5,
        'w_pool': nrm(ks[10], (DEPTH, N_POOL_GROUPS, POOL_GROUP, POOL_GROUP), jnp.float32) * POOL_GROUP ** -0.5,
        'pool_scale': 1.0 + 0.1 * nrm(ks[11], (DEPTH, POOL_W), jnp.float32),
        'w_out': nrm(ks[12], (DEPTH, D_MIX, D_MODEL), jnp.float32) * D_MIX ** -0.5,
        'final_norm_g': 1.0 + 0.1 * nrm(ks[13], (D_MODEL,), jnp.float32),
    }

def reference(x_prompt, x_sample, cache_k, cache_v, cache_idx_k, state_pool, page_table,
              meta_tokens, norm_g, w_in, w_pool, pool_scale, w_out, final_norm_g):
    B, S, _ = x_prompt.shape
    T = x_sample.shape[1]
    past = page_table.shape[1] * PAGE_SIZE
    meta = jnp.broadcast_to(meta_tokens.astype(x_prompt.dtype)[None], (B, N_META, D_MODEL))
    hp = jnp.concatenate([meta, x_prompt], axis=1)
    hs = x_sample
    pos_p = jnp.arange(N_META + S)
    pos_s = past + jnp.arange(T)
    kp, vp, kip, pp, ksm, vsm, kism, psm = ([] for _ in range(8))
    for l in range(DEPTH):
        u, zp, q, k, v, za, qi, ki, wi = in_projection(hp, norm_g[l], w_in[l])
        o_pool, st = pool_branch(jnp.zeros((B, POOL_PAD, POOL_W), u.dtype), u, zp, pos_p, w_pool[l], pool_scale[l])
        o_attn = prompt_attention(q, k, v, qi, ki, wi)
        hp = merge_residual(hp, o_pool, o_attn, za, w_out[l])
        kp.append(k)
        vp.append(v)
        kip.append(ki)
        pp.append(st)
        u, zp, q, k, v, za, qi, ki, wi = in_projection(hs, norm_g[l], w_in[l])
        o_pool, st = pool_branch(state_pool[l], u, zp, pos_s, w_pool[l], pool_scale[l])
        o_attn = sample_attention(q, k, v, qi, ki, wi, pos_s, cache_k[l], cache_v[l], cache_idx_k[l], page_table)
        hs = merge_residual(hs, o_pool, o_attn, za, w_out[l])
        ksm.append(k)
        vsm.append(v)
        kism.append(ki)
        psm.append(st)
    y_prompt = rmsnorm(hp, final_norm_g)[:, N_META:]
    y_sample = rmsnorm(hs, final_norm_g)
    return (y_prompt, y_sample, jnp.stack(kp), jnp.stack(vp), jnp.stack(kip), jnp.stack(pp),
            jnp.stack(ksm), jnp.stack(vsm), jnp.stack(kism), jnp.stack(psm))


_drawn_inputs = setup_inputs


def setup_inputs(seed=0):
    import zlib

    import numpy as np

    out = dict(_drawn_inputs(seed))
    spreads = {}
    factors = {}
    for name, (base, spread) in spreads.items():
        noise = np.random.default_rng([zlib.crc32(name.encode()), seed]).standard_normal(out[name].shape)
        drawn = base * np.exp(spread * noise) if base else spread * noise
        out[name] = jnp.asarray(drawn.astype(out[name].dtype))
    for name, factor in factors.items():
        out[name] = (out[name] * factor).astype(out[name].dtype)
    return out
```

```python
from contextlib import ExitStack

import concourse.bass as bass
import numpy as np
from concourse import mybir

F32 = mybir.dt.float32
F32R = mybir.dt.float32r
I32 = mybir.dt.int32
ALU = mybir.AluOpType
ACT = mybir.ActivationFunctionType
AX = mybir.AxisListType

D = 2048
META, SEQ, NSAMP = 16, 1024, 8
L = META + SEQ
T = L + NSAMP
NTILE = -(-T // 128)
TAIL = L - 128 * (NTILE - 1)
POOLW, GROUP, PAD = 1024, 256, 15
HEADS, KVH, HD = 8, 2, 128
IH, ID = 16, 64
PAST, PAGE, NPAGES = 1024, 128, 8
NPHYS = 80
TOPK = 256
EPS = 1e-6
C_U, C_ZP, C_Q, C_K, C_V, C_ZA, C_QI, C_KI, C_WI = np.cumsum(
    [0, POOLW, POOLW, HEADS * HD, KVH * HD, KVH * HD, HEADS * HD, IH * ID, ID]).tolist()
DIN = C_WI + IH
KT = D // 128
HALF = KT // 2
NMAIN = C_QI // 128
NQI = IH * ID // 128
NOUT = D // 128
CHUNKS = [(0, 350), (350, 350), (700, T - 700)]
BANK = 512
NEG_MASK = -1.0e38
NEG_TAKEN = -3.0e38
NEG_BIAS = -1.0e30
FIRST_TOPK = TOPK // 128
TOPK_TILES = list(range(FIRST_TOPK, NTILE))
ROUNDS = TOPK // 8




def rows_of(i):
    return 128 if i < NTILE - 1 else TAIL


def cols_of(i):
    return 128 if i < NTILE - 1 else T - 128 * i


def keys_of(i):
    return min(128 * (i + 1), L)


def banks(width):
    return [(c, min(BANK, width - c)) for c in range(0, width, BANK)]


K_ID, K_TQ, K_ESEL, K_ONEB, K_SLOPE, K_CINV, K_STATE, K_S = np.cumsum(
    [0, 128, NTILE, 64, 8, 1, 4 * 16, 4 * 8]).tolist()
K_ALL = K_S + L


def constants():
    c = np.zeros((128, K_ALL), np.float32)
    p = np.arange(128)
    c[:, K_ID:K_ID + 128] = np.eye(128)
    c[:, K_S:K_S + L] = np.arange(L)[None]
    for i in range(NTILE):
        c[:, K_TQ + i] = -(128 * i + p)
    c[32:40, K_TQ + NTILE - 1] = -PAST
    for b in range(NSAMP):
        c[32 + b, K_ESEL + 8 * b:K_ESEL + 8 * b + 8] = 1
        c[16 * b:16 * b + 16, K_ONEB + b] = 1
    c[:, K_SLOPE] = 2.0 ** -(p % 8 + 1)
    for g in range(4):
        w = 2 << g
        c[:, K_CINV + 16 * g:K_CINV + 16 * g + 16] = 1 / np.minimum(np.arange(16) + 1, w)
        for b in range(NSAMP):
            c[15 * b + 16 - w:15 * b + 15, K_STATE + 8 * g + b] = 1
    return c


def build(nc, io):
    xp, xs_, ck, cv, cik = (io[n] for n in ("x_prompt", "x_sample", "cache_k", "cache_v", "cache_idx_k"))
    state, ptab, meta = io["state_pool"], io["page_table"], io["meta_tokens"]
    norm_g, w_in, w_pool, pscale = io["norm_g"], io["w_in"], io["w_pool"], io["pool_scale"]
    w_out, fin_g, consts = io["w_out"], io["final_norm_g"], io["consts"]

    proj = nc.dram_tensor("proj_scratch", (DIN, T), F32, kind="Internal").ap()
    mixt = nc.dram_tensor("mix_scratch", (D, T), F32, kind="Internal").ap()
    hbuf_d = nc.dram_tensor("h_scratch", (NTILE * 128, D), F32, kind="Internal").ap()

    def x_parts(i):
        if i == 0:
            return [(0, META, meta[:, :]), (META, 128 - META, xp[0, 0:128 - META, :])]
        lo = 128 * i - META
        if i < NTILE - 1:
            return [(0, 128, xp[0, lo:lo + 128, :])]
        return [(0, TAIL, xp[0, lo:SEQ, :]), (TAIL, NSAMP, xs_[:, 0, :])]

    X_PARTS = [len(x_parts(i)) for i in range(NTILE)]

    with ExitStack() as top:
        def sem(name):
            return top.enter_context(nc.semaphore(name))

        def sb(name, shape, dt=F32, ctx=top):
            return ctx.enter_context(nc.sbuf_tensor(name, shape, dt))

        ps = top.enter_context(nc.psum_tensor("ps", [128, 8, BANK], F32))
        psf = ps[:, :, :].rearrange("p b c -> p (b c)")
        cst = sb("cst", [128, K_S])
        ident = cst[:, K_ID:K_ID + 128]
        pages = sb("pages", [1, NSAMP * NPAGES], I32)
        wraw = sb("wraw", [128, 4, HALF, 128])
        whi = sb("whi", [128, 2, HALF, 128], F32R)
        wlo = sb("wlo", [128, 2, HALF, 128], F32R)
        c1 = ExitStack()
        with c1:
            akh = sb("akh", [128, KVH, L], F32R, c1)
            akl = sb("akl", [128, KVH, L], F32R, c1)
            kvtok = sb("kvtok", [128, NTILE, 2 * KVH * HD], F32, c1)
            pts = sb("pts", [128, 2, BANK], F32, c1)
            qin = sb("qin", [128, 2, HEADS, 128], F32, c1)
            qh = sb("qh", [128, 2, HEADS, 128], F32R, c1)
            ql = sb("ql", [128, 2, HEADS, 128], F32R, c1)
            with ExitStack() as c2:
                kvin = sb("kvin", [128, 2 * KVH, T], F32, c2)
            slot = sb("slot", [128, 4, NPAGES, KVH * HD], F32, c1)
            with ExitStack() as c2:
                prob = sb("prob", [128, 2, 4, L], F32, c2)
            with ExitStack() as c2:
                skt = sb("skt", [128, 2, PAST], F32, c2)
                qz = sb("qz", [128, NSAMP * KVH, 64], F32, c2)
                sbias = sb("sbias", [64, PAST + 1], F32, c2)
                sprob = sb("sprob", [64, PAST + 1], F32, c2)
                spt = sb("spt", [128, NPAGES + 1, 64], F32, c2)
                vnew = sb("vnew", [1, NSAMP * KVH * HD], F32, c2)
        with ExitStack() as c1:
            ohi = sb("ohi", [128, KT, T], F32R, c1)
            olo = sb("olo", [128, KT, T], F32R, c1)
        with ExitStack() as c1:
            fh = sb("fh", [128, NTILE, D], F32, c1)
            fg = sb("fg", [128, D], F32, c1)
        ahi = sb("ahi", [128, KT, T], F32R)
        alo = sb("alo", [128, KT, T], F32R)
        with ExitStack() as c1:
            xt = sb("xt", [128, 3, D], F32, c1)
            gb = sb("gb", [128, D], F32, c1)
            nst = sb("nst", [128, 6, NTILE], F32, c1)
        stage = sb("stage", [128, 2, T])
        with ExitStack() as c1:
            orow = sb("orow", [128, 4, T], F32, c1)
            xblk = sb("xblk", [128, 2, NTILE, 128], F32, c1)
            hblk = sb("hblk", [128, 2, NTILE, 128], F32, c1)
            sq = sb("sq", [128, 2, NTILE], F32, c1)
            sqj = sb("sqj", [128, NTILE, 128], F32, c1)
            fst = sb("fst", [128, 6, NTILE], F32, c1)
        score = sb("score", [128, sum(keys_of(i) for i in TOPK_TILES)])
        m8 = sb("m8", [128, len(TOPK_TILES), 8])
        with ExitStack() as c1:
            kiw = sb("kiw", [128, NTILE, ID + IH], F32, c1)
            wsc = sb("wsc", [128, NTILE, IH], F32, c1)
            khi = sb("khi", [128, L], F32R, c1)
            klo = sb("klo", [128, L], F32R, c1)
            wcol = sb("wcol", [128, 1], F32, c1)
            with ExitStack() as c2:
                qst = sb("qst", [128, 2, IH // 2, 128], F32R, c2)
                qraw = sb("qraw", [128, 2, IH // 2, 128], F32, c2)
            with ExitStack() as c2:
                qbd = sb("qbd", [128, 4, 128], F32, c2)
                rsc = sb("rsc", [128, PAST + 1], F32, c2)
                iload = sb("iload", [128, NPAGES, 2, ID], F32, c2)
                ikt = sb("ikt", [128, PAST + 1], F32, c2)
        with ExitStack() as c1:
            psc = sb("psc", [128, POOLW // 128], F32, c1)
            psg = sb("psg", [128, 2], F32, c1)
            sst = sb("sst", [128, POOLW // 128, NSAMP], F32, c1)
            pw = sb("pw", [128, 2, GROUP], F32, c1)
            pu = sb("pu", [128, 2, T], F32, c1)
            pt = sb("pt", [128, 2, T], F32, c1)
            with ExitStack() as c2:
                pz = sb("pz", [128, 2, T], F32, c2)
            ulast = sb("ulast", [128, POOLW // 128, PAD + NSAMP], F32, c1)
            ulrow = sb("ulrow", [PAD + NSAMP, POOLW], F32, c1)
            strow = sb("strow", [NSAMP * PAD, POOLW], F32, c1)
        with ExitStack() as c1:
            spos = sb("spos", [128, L], F32, c1)
            dist01 = sb("dist01", [128, 3 * 128], F32, c1)
            zin = sb("zin", [128, 2, HEADS, 128], F32, c1)
            osb = sb("osb", [128, 2, 4, 128], F32, c1)
            knew = sb("knew", [128, KVH, NSAMP], F32, c1)
            ast = sb("ast", [128, 3, 2, 4], F32, c1)
            sst64 = sb("sst64", [64, 3], F32, c1)
            osamp = sb("osamp", [128, HEADS, NSAMP], F32, c1)
        SOFF = {i: sum(keys_of(j) for j in TOPK_TILES if j < i) for i in TOPK_TILES}
        relu = stage

        def score_of(i):
            return score[:, SOFF[i]:SOFF[i] + keys_of(i)]

        S = {}
        for name in ("cst_in", "g_in", "x_in0", "x_in1", "x_in2", "x_sq", "x_rms", "x_sqrt", "x_rstd", "x_scaled",
                     "x_turned", "a_hi", "a_lo", "w_in0", "w_in1", "w_in2", "w_in3", "w_hi", "w_lo", "w_used",
                     "evac", "stored0", "stored1", "small", "pages_in", "state_in", "ul_in", "ul_turned", "ul_kept", "ul_out", "st_summed", "st_kept", "psg_kept",
                     "p_in", "p_mixed", "p_mm", "p_scaled", "p_gated", "p_stored", "pool_step",
                     "spos_in", "kv_in", "aq_in0", "aq_in1", "kvtok_kept", "kv_turned", "gated", "o_stored0", "o_stored1",
                     "pv_mm", "vnew_in", "sv_used", "slot_in0", "slot_in1", "slot_in2", "slot_in3",
                     "sgated", "os_stored", "o_in0", "o_in1", "o_in2", "o_in3", "o_hi", "o_lo",
                     "xb_in0", "xb_in1", "h_added", "h_part", "h_turned", "h_squared", "sq_added", "h_stored0", "h_stored1",
                     "fg_in", *(f"fh_in{i}" for i in range(NTILE)), "f_rms", "f_sqrt", "f_done", "y_out",
                     "ak_hi", "ak_lo", "knew_kept", "aqk", "aq_hi", "aq_lo", "p_turned", "pt_copied", "amax", "aexp",
                     "abias", "normed", "dist_made", "dist_masked", "sk_turned", "sk_copied", "sqk", "smax", "sexp",
                     "sp_turned", "spt_copied", "qz_made", "sdist", "sbias_made", "snormed",
                     "kiw_turned", "kiw_out", "kiw_kept", "kiraw_in", "ki_hi", "ki_lo", "q_in0", "q_in1", "q_hi", "q_lo", "q_used",
                     "logits", "relu_done", "scored", "score_init",
                     "ik_in", "ik_turned", "ik_copied", "ik_used", "qb_ready", "slogits", "srelu", "ssum", "ssum_kept",
                     "wcol_in", "ikn_in", "maxed", "taken", "outs"):
            S[name] = sem(name)
        block = top.enter_context(nc.Block())

        B_MAIN = 1 + NQI
        B_OUT = B_MAIN + NMAIN
        WIDTH0 = ID + IH

        def parity(n):
            return 1 - n % 2

        def uses(n):
            return (n + 1) // 2 if n % 2 else n // 2 + 1

        def load_block(q, n, src, width=128, i=None, guard=True):
            p = parity(n)
            add = 0 if i is None else 4 * i
            for s in range(2):
                if guard:
                    q.wait_ge(S["w_lo"], 2 * n + s - 3 + add)
                q.dma_start(wraw[:, 2 * p + s, :, 0:width],
                            src[s * HALF * 128:(s + 1) * HALF * 128, :].rearrange("(k p) n -> p k n", p=128)
                            ).then_inc(S[f"w_in{2 * p + s}"], 16)

        def split_hi(act, n, s, width=128, i=None, first=False):
            p = parity(n)
            add1, add4 = (0, 0) if i is None else (i, 4 * i)
            act.wait_ge(S[f"w_in{2 * p + s}"], 16 * uses(n) + 16 * add1)
            if not first:
                act.wait_ge(S["w_used"], 2 * n + s - 1 + add4)
            nc.scalar.activation(whi[:, s, :, 0:width], wraw[:, 2 * p + s, :, 0:width],
                                 ACT.Copy).then_inc(S["w_hi"], 1)

        def split_lo(dve, n, s, width=128, i=None):
            p = parity(n)
            add = 0 if i is None else 4 * i
            dve.wait_ge(S["w_hi"], 2 * n + s + 1 + add)
            nc.vector.tensor_tensor(wlo[:, s, :, 0:width], wraw[:, 2 * p + s, :, 0:width],
                                    whi[:, s, :, 0:width].bitcast(F32), ALU.subtract).then_inc(S["w_lo"], 1)

        def project(pe, n, width=128, i=None, first=False, src=None, first_out=False, between=None):
            p = parity(n)
            add2, add4 = (0, 0) if i is None else (2 * i, 4 * i)
            if not first:
                pe.wait_ge(S["evac"], n - 1 + add2)
            mhi, mlo = src or (ahi, alo)
            for s in range(2):
                pe.wait_ge(S["w_lo"], 2 * n + s + 1 + add4)
                if s and between:
                    between()
                for k in range(HALF):
                    a = s * HALF + k
                    if first_out:
                        pe.wait_ge(S["o_lo"], a + 1)
                    for w, parts in ((whi, (mhi, mlo)), (wlo, (mhi,))):
                        for m in parts:
                            for c, (t0, tn) in enumerate(CHUNKS):
                                last = nc.tensor.matmul(ps[0:width, 3 * p + c, 0:tn], w[:, s, k, 0:width],
                                                        m[:, a, t0:t0 + tn],
                                                        start=(a == 0 and w is whi and m is mhi),
                                                        stop=(a == KT - 1 and w is wlo))
                last.then_inc(S["w_used"], 1)

        def quarter(i, r):
            nb = i + 1
            return range(r * nb // 4, (r + 1) * nb // 4)

        def evacuate(act, n, width=128, i=None, func=None, first=False, stored=True):
            p = parity(n)
            add1, add4 = (0, 0) if i is None else (i, 4 * i)
            act.wait_ge(S["w_used"], 2 * n + 2 + add4)
            if not first and stored:
                act.wait_ge(S[f"stored{p}"], 16 * (uses(n) - 1) + 16 * add1)
            f = func or ACT.Copy
            nc.scalar.activation(stage[0:width, p, 0:700].rearrange("p (c t) -> p c t", c=2),
                                 ps[0:width, 3 * p:3 * p + 2, 0:350], f)
            nc.scalar.activation(stage[0:width, p, 700:T], ps[0:width, 3 * p + 2, 0:T - 700],
                                 f).then_inc(S["evac"], 1)

        def store_block(act, n, dst, width=128, i=None):
            p = parity(n)
            add2 = 0 if i is None else 2 * i
            act.wait_ge(S["evac"], n + 1 + add2)
            act.dma_start(dst, stage[0:width, p, :]).then_inc(S[f"stored{p}"], 16)

        AUNITS = [(i, g) for i in range(NTILE) for g in range(KVH)]

        def blocks_to(u):
            return sum(i + 1 for i, _ in AUNITS[:u])

        def dist_of(i):
            if i in SOFF:
                return score_of(i)
            return dist01[:, 128 * (i * (i + 1) // 2):128 * (i * (i + 1) // 2) + keys_of(i)]

        def page_ids(q, b):
            _, ids = nc.values_load_multi_w_load_instructions(
                pages[0:1, b * NPAGES:(b + 1) * NPAGES], engines=[q.engine], min_val=0, max_val=NPHYS - 1)
            return ids

        @block.sync
        def _(sp):
            sp.dma_start(cst[:, :], consts[:, 0:K_S]).then_inc(S["cst_in"], 16)
            sp.dma_start(pages[:, :], ptab.rearrange("(o b) k -> o (b k)", o=1)).then_inc(S["pages_in"], 16)
            for i in range(NTILE):
                if i >= 3:
                    sp.wait_ge(S["x_turned"], 4 * (i - 2))
                for r0, n, src in x_parts(i):
                    sp.dma_start(xt[r0:r0 + n, i % 3, :], src).then_inc(S[f"x_in{i % 3}"], 16)
                if i == 0:
                    sp.dma_start(gb[:, :], norm_g[0, :].partition_broadcast(128)).then_inc(S["g_in"], 16)
                if i == 2:
                    load_block(sp, 0, w_in[0, :, C_KI:DIN], WIDTH0, guard=False)
            load_block(sp, 1, w_in[0, :, C_QI:C_QI + 128], guard=False)
            sp.wait_ge(S["w_lo"], 1)
            load_block(sp, 2, w_in[0, :, C_QI + 128:C_QI + 256])
            sp.wait_ge(S["kiw_kept"], 1)
            new_ik_p, new_ik_s = io["new_idx_k_prompt"], io["new_idx_k_sample"]
            full = 128 * (NTILE - 1)
            sp.dma_start(new_ik_p[0, 0, 0:full, :].rearrange("(t p) d -> p t d", p=128),
                         kiw[:, 0:NTILE - 1, 0:ID]).then_inc(S["outs"], 16)
            sp.dma_start(new_ik_p[0, 0, full:L, :], kiw[0:TAIL, NTILE - 1, 0:ID]).then_inc(S["outs"], 16)
            sp.dma_start(new_ik_s[0, :, 0, :], kiw[TAIL:TAIL + NSAMP, NTILE - 1, 0:ID]).then_inc(S["outs"], 16)
            with sp.Fori(0, NQI // 2 - 1) as i:
                load_block(sp, 3, w_in[0, :, bass.ds(i * 256 + C_QI + 256, 128)], i=i)
                load_block(sp, 4, w_in[0, :, bass.ds(i * 256 + C_QI + 384, 128)], i=i)
            load_block(sp, B_MAIN, w_in[0, :, 0:128])
            load_block(sp, B_MAIN + 1, w_in[0, :, 128:256])
            for r in range(2):
                if r == 0:
                    sp.wait_ge(S["stored1"], 16 * uses(NQI))
                    sp.wait_ge(S["stored0"], 16 * uses(NQI - 1))
                sp.dma_start(stage[64 * r:64 * r + 64, 0, 0:L], proj[C_KI:C_WI, 0:L]).then_inc(S["kiraw_in"], 16)
            for n, (i, h) in enumerate((i, h) for i in TOPK_TILES for h in range(2)):
                if n >= 2:
                    sp.wait_ge(S["q_lo"], n - 1)
                cols = cols_of(i)
                for r in range(2):
                    sp.dma_start(qraw[64 * r:64 * r + 64, n % 2, :, 0:cols],
                                 proj[C_QI + 512 * h:C_QI + 512 * h + 512, 128 * i:128 * i + cols]
                                 .rearrange("(h d) t -> d h t", d=64)).then_inc(S[f"q_in{n % 2}"], 16)
            with nc.allow_non_contiguous_dma(reason="128 single weights"):
                for b in range(NSAMP):
                    sp.dma_start(wcol[16 * b:16 * b + 16, :], proj[C_WI:DIN, L + b:L + b + 1]).then_inc(S["wcol_in"], 16)
            sp.wait_ge(S["pages_in"], 16)
            for j in range(NSAMP // 2):
                if j == 0:
                    sp.wait_ge(S["qb_ready"], 8)
                else:
                    sp.wait_ge(S["ik_turned"], j)
                for b in range(2):
                    for k, page in enumerate(page_ids(sp, 2 * j + b)):
                        sp.dma_start(iload[:, k, b, :], cik[0, bass.ds(page, 1), :, :].rearrange("o s d -> (o s) d")
                                     ).then_inc(S["ik_in"], 16)
                with nc.allow_non_contiguous_dma(reason="one new key"):
                    for b in range(2):
                        if j > 0 and b == 0:
                            sp.wait_ge(S["slogits"], j)
                        sp.dma_start(ikt[64 * b:64 * b + 64, PAST:PAST + 1],
                                     proj[C_KI:C_WI, L + 2 * j + b:L + 2 * j + b + 1]).then_inc(S["ikn_in"], 16)
            sp.wait_ge(S["srelu"], 1)
            sp.wait_ge(S["ssum"], 1)
            with nc.allow_non_contiguous_dma(reason="one scale a channel"):
                sp.dma_start(psc[:, :], pscale[0, :].rearrange("(c p) -> p c", p=128)).then_inc(S["state_in"], 16)
            sp.dma_start(strow[:, :], state[0].rearrange("b r c -> (b r) c")).then_inc(S["state_in"], 16)
            for b in range(NSAMP):
                sp.dma_start(io["new_pool_sample"][0, b, 0:PAD - 1, :], state[0, b, 1:PAD, :]).then_inc(S["outs"], 16)
            with sp.Fori(0, NMAIN // 2 - 1) as i:
                load_block(sp, B_MAIN + 2, w_in[0, :, bass.ds(i * 256 + 256, 128)], i=i)
                load_block(sp, B_MAIN + 3, w_in[0, :, bass.ds(i * 256 + 384, 128)], i=i)
            load_block(sp, B_OUT, w_out[0, :, 0:128])
            load_block(sp, B_OUT + 1, w_out[0, :, 128:256])
            sp.wait_ge(S["p_stored"], 16 * 4)
            sp.dma_start(spos[:, :], consts[:, K_S:K_ALL]).then_inc(S["spos_in"], 16)
            sp.wait_ge(S["w_used"], 2 * B_OUT)
            for n in (B_OUT - 2, B_OUT - 1):
                sp.wait_ge(S[f"stored{parity(n)}"], 16 * uses(n))
            sp.dma_start(kvin[:, :, :], proj[C_K:C_ZA, :].rearrange("(b p) t -> p b t", p=128)).then_inc(S["kv_in"], 16)

            def load_q(i):
                c = cols_of(i)
                tok = slice(128 * i, 128 * i + c)
                sp.dma_start(qin[:, i % 2, :, 0:c], proj[C_Q:C_K, tok].rearrange("(h p) t -> p h t", p=128)
                             ).then_inc(S[f"aq_in{i % 2}"], 16)
                sp.dma_start(zin[:, i % 2, :, 0:c], proj[C_ZA:C_QI, tok].rearrange("(h p) t -> p h t", p=128)
                             ).then_inc(S[f"aq_in{i % 2}"], 16)

            load_q(0)
            load_q(1)
            sp.wait_ge(S["kvtok_kept"], NTILE)
            for kv, name in ((0, "k"), (1, "v")):
                cols = slice(kv * KVH * HD, (kv + 1) * KVH * HD)
                sp.dma_start(io[f"new_{name}_prompt"][0, 0, 0:full].rearrange("(t p) g d -> p t (g d)", p=128),
                             kvtok[:, 0:NTILE - 1, cols]).then_inc(S["outs"], 16)
                sp.dma_start(io[f"new_{name}_prompt"][0, 0, full:L].rearrange("t g d -> t (g d)"),
                             kvtok[0:TAIL, NTILE - 1, cols]).then_inc(S["outs"], 16)
                sp.dma_start(io[f"new_{name}_sample"][0, :, 0].rearrange("b g d -> b (g d)"),
                             kvtok[TAIL:TAIL + NSAMP, NTILE - 1, cols]).then_inc(S["outs"], 16)
            for u, (i, g) in enumerate(AUNITS):
                sp.wait_ge(S["gated"], u + 1)
                r = rows_of(i)
                sp.dma_start(mixt[POOLW + 512 * g:POOLW + 512 * g + 512, 128 * i:128 * i + r]
                             .rearrange("(h p) t -> p h t", p=128),
                             osb[:, u % 2, :, 0:r]).then_inc(S[f"o_stored{u % 2}"], 16)
                if g == KVH - 1 and i + 2 < NTILE:
                    load_q(i + 2)
            sp.wait_ge(S["pv_mm"], blocks_to(len(AUNITS)))
            sp.dma_start(vnew[0:1, :].rearrange("o (b c) -> o b c", b=NSAMP),
                         kvtok[TAIL:TAIL + NSAMP, NTILE - 1, KVH * HD:2 * KVH * HD]).then_inc(S["vnew_in"], 16)
            for m in range(2 * NSAMP):
                src = (ck, cv)[m // NSAMP]
                if 4 <= m < NSAMP + 4:
                    sp.wait_ge(S["sk_turned"], KVH * (m - 3))
                elif m >= 4:
                    sp.wait_ge(S["sv_used"], m - NSAMP - 3)
                for k, page in enumerate(page_ids(sp, m % NSAMP)):
                    sp.dma_start(slot[:, m % 4, k, :], src[0, bass.ds(page, 1), :, :, :].rearrange("o s g d -> (o s) (g d)")
                                 ).then_inc(S[f"slot_in{m % 4}"], 16)
            with nc.allow_non_contiguous_dma(reason="32-byte rows"):
                sp.wait_ge(S["sgated"], 1)
                sp.dma_start(mixt[POOLW:D, L:T].rearrange("(h p) t -> p h t", p=128), osamp[:, :, :]
                             ).then_inc(S["os_stored"], 16)
            sp.wait_ge(S["os_stored"], 16)
            for p in range(2):
                sp.wait_ge(S[f"o_stored{p}"], 16 * len(AUNITS[p::2]))
            sp.wait_ge(S["sv_used"], NSAMP)
            for k in range(KT):
                if k >= 4:
                    sp.wait_ge(S["o_lo"], k - 3)
                sp.dma_start(orow[:, k % 4, :], mixt[128 * k:128 * k + 128, :]).then_inc(S[f"o_in{k % 4}"], 16)

            def load_x(n, c0, i=None):
                p = parity(n)
                add2 = 0 if i is None else 2 * i
                if n >= B_OUT + 2:
                    sp.wait_ge(S["h_added"], n - B_OUT - 1 + add2)
                x = xblk[:, p, :, :]
                s_ = S[f"xb_in{p}"]
                c = c0
                lo = 128 - META
                sp.dma_start(x[0:META, 0, :], meta[:, c]).then_inc(s_, 16)
                sp.dma_start(x[META:128, 0, :], xp[0, 0:lo, c]).then_inc(s_, 16)
                sp.dma_start(x[:, 1:NTILE - 1, :],
                             xp[0, lo:lo + 128 * (NTILE - 2), c].rearrange("(t p) d -> p t d", p=128)).then_inc(s_, 16)
                sp.dma_start(x[0:TAIL, NTILE - 1, :], xp[0, SEQ - TAIL:SEQ, c]).then_inc(s_, 16)
                sp.dma_start(x[TAIL:TAIL + NSAMP, NTILE - 1, :], xs_[:, 0, c]).then_inc(s_, 16)

            load_x(B_OUT, slice(0, 128))
            load_x(B_OUT + 1, slice(128, 256))
            with sp.Fori(0, NOUT // 2 - 1) as i:
                for r in range(2):
                    c = bass.ds(i * 256 + 256 + 128 * r, 128)
                    load_block(sp, B_OUT + 2 + r, w_out[0, :, c], i=i)
                    load_x(B_OUT + 2 + r, c, i=i)
            sp.wait_ge(S["w_used"], 2 * (B_OUT + NOUT))
            sp.dma_start(fg[:, :], fin_g.partition_broadcast(128)).then_inc(S["fg_in"], 16)
            for p in range(2):
                sp.wait_ge(S[f"h_stored{p}"], 32 * NOUT // 2)
            for i in range(NTILE):
                n = cols_of(i)
                sp.dma_start(fh[0:n, i, :], hbuf_d[128 * i:128 * i + n, :]).then_inc(S[f"fh_in{i}"], 16)

        @block.scalar
        def _(act):
            def turned_hi(i):
                for q in range(4):
                    act.wait_ge(S["x_turned"], 4 * i + q + 1)
                    c = cols_of(i)
                    nc.scalar.activation(ahi[:, 4 * q:4 * q + 4, 128 * i:128 * i + c],
                                         ps[:, q, :].rearrange("p (k t) -> p k t", k=4)[:, :, 0:c],
                                         ACT.Copy).then_inc(S["a_hi"], 1)

            for i in range(NTILE):
                n = cols_of(i)
                act.wait_ge(S[f"x_in{i % 3}"], 16 * sum(X_PARTS[i % 3:i + 1:3]))
                if i:
                    act.wait_ge(S["x_sqrt"], i)
                nc.scalar.activation(psf[0:n, 2048:4096], xt[0:n, i % 3, :], ACT.Square,
                                     accum_out=nst[0:n, 0, i:i + 1]).then_inc(S["x_sq"], 1)
                act.wait_ge(S["x_rms"], i + 1)
                nc.scalar.activation(nst[0:n, 3, i:i + 1], nst[0:n, 2, i:i + 1], ACT.Sqrt).then_inc(S["x_sqrt"], 1)
                if i:
                    turned_hi(i - 1)
            turned_hi(NTILE - 1)

            split_hi(act, 0, 0, WIDTH0, first=True)
            split_hi(act, 0, 1, WIDTH0, first=True)
            split_hi(act, 1, 0)
            evacuate(act, 0, WIDTH0, first=True)
            store_block(act, 0, proj[C_KI:DIN, :], WIDTH0)
            split_hi(act, 1, 1)

            def query_block(n, dst, i=None, first=False):
                split_hi(act, n + 1, 0, i=i)
                evacuate(act, n, i=i, first=first)
                store_block(act, n, dst, i=i)
                split_hi(act, n + 1, 1, i=i)

            query_block(1, proj[C_QI:C_QI + 128, :], first=True)
            query_block(2, proj[C_QI + 128:C_QI + 256, :])
            with act.Fori(0, NQI // 2 - 1) as i:
                for n in (3, 4):
                    query_block(n, proj[bass.ds(i * 256 + C_QI + 128 * (n - 1), 128), :], i=i)
            act.wait_ge(S["kiraw_in"], 32)
            nc.scalar.activation(khi[:, :], stage[:, 0, 0:L], ACT.Copy).then_inc(S["ki_hi"], 1)

            def query_hi(n, i):
                act.wait_ge(S[f"q_in{n % 2}"], 32 * (n // 2 + 1))
                if n >= 2:
                    act.wait_ge(S["logits"], 8 * (n - 1))
                c = cols_of(i)
                nc.scalar.activation(qst[:, n % 2, :, 0:c], qraw[:, n % 2, :, 0:c], ACT.Copy).then_inc(S["q_hi"], 1)

            units = [(i, h) for i in TOPK_TILES for h in range(2)]
            query_hi(0, units[0][0])
            act.wait_ge(S["ki_lo"], 1)
            u = 0
            for n, (i, h) in enumerate(units):
                if n + 1 < len(units):
                    query_hi(n + 1, units[n + 1][0])
                rows, w = rows_of(i), keys_of(i)
                for k in range(IH // 2):
                    act.wait_ge(S["logits"], u + 1)
                    if u >= 2:
                        act.wait_ge(S["scored"], u - 1)
                    nc.scalar.activation(relu[0:rows, u % 2, 0:w], psf[0:rows, 1536 * (u % 2):1536 * (u % 2) + w],
                                         ACT.Relu).then_inc(S["relu_done"], 1)
                    u += 1
            for j in range(NSAMP // 2):
                act.wait_ge(S["ik_turned"], j + 1)
                if j:
                    act.wait_ge(S["slogits"], j)
                nc.scalar.activation(ikt[:, 0:PAST], psf[:, 3072:3072 + PAST], ACT.Copy).then_inc(S["ik_copied"], 1)
            act.wait_ge(S["scored"], u)
            B_GRP = B_MAIN + 2 * (POOLW // 128)
            for first, func in ((0, ACT.Copy), (POOLW // 256, ACT.Silu)):
                with act.Fori(first, first + POOLW // 256) as i:
                    for n in (B_MAIN, B_MAIN + 1):
                        split_hi(act, n + 1, 0, i=i)
                        evacuate(act, n, i=i, func=func)
                        store_block(act, n, proj[bass.ds(i * 256 + 128 * (n - B_MAIN), 128), :], i=i)
                        split_hi(act, n + 1, 1, i=i)
            act.wait_ge(S["stored0"], 16 * uses(B_MAIN + POOLW // 128 - 2))
            act.wait_ge(S["stored1"], 16 * uses(B_MAIN + POOLW // 128 - 1))
            act.dma_start(ulast[:, :, :], proj[C_U:C_ZP, L - PAD:T].rearrange("(c p) t -> p c t", p=128)
                          ).then_inc(S["ul_in"], 16)
            act.wait_ge(S["ul_turned"], 1)
            nc.scalar.activation(ulrow[:, :], psf[0:PAD + NSAMP, 3072:4096], ACT.Copy).then_inc(S["ul_kept"], 1)
            act.wait_ge(S["st_summed"], 1)
            nc.scalar.activation(sst[:, :, :], psf[:, 3072:3072 + 64].rearrange("p (c b) -> p c b", b=NSAMP),
                                 ACT.Copy).then_inc(S["st_kept"], 1)
            act.wait_ge(S["ul_kept"], 1)
            act.dma_start(io["new_pool_prompt"][0, 0, :, :], ulrow[0:PAD, :]).then_inc(S["ul_out"], 16)
            act.dma_start(io["new_pool_sample"][0, :, PAD - 1, :], ulrow[PAD:PAD + NSAMP, :]).then_inc(S["ul_out"], 16)

            def pool_group(g, i2, func, first=False):
                for q in range(4):
                    n = B_GRP + q
                    split_hi(act, n + 1, 0, i=i2)
                    evacuate(act, n, i=i2, func=func)
                    store_block(act, n, proj[bass.ds(g * 512 + 2 * POOLW + 128 * q, 128), :], i=i2)
                    split_hi(act, n + 1, 1, i=i2)
                    if q == 0:
                        if not first:
                            act.wait_ge(S["p_gated"], g)
                            act.wait_ge(S["p_stored"], g * 16)
                        act.wait_ge(S["ul_out"], 32)
                        nc.scalar.activation(psg[:, :], psc[:, bass.ds(g * 2, 2)], ACT.Copy).then_inc(S["psg_kept"], 1)
                        act.dma_start(pu[:, :, :], proj[bass.ds(g * GROUP, GROUP), :].rearrange("(c p) t -> p c t", p=128)
                                      ).then_inc(S["p_in"], 16)
                        act.dma_start(pz[:, :, :], proj[bass.ds(g * GROUP + C_ZP, GROUP), :]
                                      .rearrange("(c p) t -> p c t", p=128)).then_inc(S["p_in"], 16)
                        act.dma_start(pw[:, :, :], w_pool[0, bass.ds(g, 1), :, :].rearrange("o (c p) d -> p (o c) d", p=128)
                                      ).then_inc(S["p_in"], 16)
                act.wait_ge(S["psg_kept"], g + 1)
                for x in range(6):
                    m, c = divmod(x, 3)
                    t0, tn = CHUNKS[c]
                    act.wait_ge(S["p_mm"], g * 6 + x + 1)
                    nc.scalar.activation(pt[:, m, t0:t0 + tn], ps[:, 6 + x % 2, 0:tn], ACT.Identity,
                                         scale=psg[:, m:m + 1]).then_inc(S["p_scaled"], 1)

            groups = POOLW // GROUP
            pool_group(0, 0, ACT.Copy, first=True)
            with act.Fori(1, groups - 1) as g:
                pool_group(g, g * 2, ACT.Copy)
            for q in range(4):
                n = B_GRP + 4 * (groups - 1) + q
                split_hi(act, n + 1, 0)
                evacuate(act, n, func=ACT.Silu)
                r0 = (n - B_MAIN) * 128
                store_block(act, n, proj[r0:r0 + 128, :])
                split_hi(act, n + 1, 1)
                if q == 0:
                    g = groups - 1
                    act.wait_ge(S["p_gated"], g)
                    act.wait_ge(S["p_stored"], g * 16)
                    act.dma_start(pu[:, :, :], proj[g * GROUP:(g + 1) * GROUP, :].rearrange("(c p) t -> p c t", p=128)
                                  ).then_inc(S["p_in"], 16)
                    act.dma_start(pz[:, :, :], proj[C_ZP + g * GROUP:C_ZP + (g + 1) * GROUP, :]
                                  .rearrange("(c p) t -> p c t", p=128)).then_inc(S["p_in"], 16)
                    act.dma_start(pw[:, :, :], w_pool[0, g, :, :].rearrange("(c p) d -> p c d", p=128)
                                  ).then_inc(S["p_in"], 16)
            for x in range(6):
                m, c = divmod(x, 3)
                t0, tn = CHUNKS[c]
                act.wait_ge(S["p_mm"], g * 6 + x + 1)
                nc.scalar.activation(pt[:, m, t0:t0 + tn], ps[:, 6 + x % 2, 0:tn], ACT.Identity,
                                     scale=psc[:, g * 2 + m:g * 2 + m + 1]).then_inc(S["p_scaled"], 1)
            for n in range(B_GRP + 4 * groups, B_OUT):
                split_hi(act, n + 1, 0)
                evacuate(act, n, func=ACT.Silu)
                r0 = (n - B_MAIN) * 128
                store_block(act, n, proj[r0:r0 + 128, :])
                split_hi(act, n + 1, 1)

            act.wait_ge(S["kv_in"], 16)
            nc.scalar.activation(akh[:, :, :], kvin[:, 0:KVH, 0:L], ACT.Copy).then_inc(S["ak_hi"], 1)
            act.wait_ge(S["p_stored"], 16 * groups)
            nc.scalar.activation(knew[:, :, :], kvin[:, 0:KVH, L:T], ACT.Copy).then_inc(S["knew_kept"], 1)

            def query_parts(i):
                act.wait_ge(S[f"aq_in{i % 2}"], 32 * (i // 2 + 1))
                if i >= 2:
                    act.wait_ge(S["aqk"], 8 * (i - 1))
                c = cols_of(i)
                nc.scalar.activation(qh[:, i % 2, :, 0:c], qin[:, i % 2, :, 0:c], ACT.Copy,
                                     scale=HD ** -0.5).then_inc(S["aq_hi"], 1)

            query_parts(0)
            for i in range(NTILE):
                n = cols_of(i)
                act.wait_ge(S["kv_turned"], i + 1)
                nc.scalar.activation(kvtok[0:n, i, :], ps[0:n, i % 6, :], ACT.Copy).then_inc(S["kvtok_kept"], 1)
            act.wait_ge(S["ak_lo"], 1)
            act.wait_ge(S["kv_turned"], NTILE)
            t = 0
            for u in range(len(AUNITS) + 1):
                for r in range(4):
                    if u:
                        i, g = AUNITS[u - 1]
                        for j in quarter(i, r):
                            act.wait_ge(S["p_turned"], t + 1)
                            if t >= 2:
                                act.wait_ge(S["pv_mm"], t - 1)
                            kn = min(128, L - 128 * j)
                            w = 4 * rows_of(i)
                            nc.scalar.activation(pts[0:kn, t % 2, 0:w], ps[0:kn, 6, 0:w], ACT.Copy
                                                 ).then_inc(S["pt_copied"], 1)
                            t += 1
                    if u < len(AUNITS):
                        i, g = AUNITS[u]
                        n, w = rows_of(i), keys_of(i)
                        act.wait_ge(S["amax"], 4 * u + r + 1)
                        x = prob[0:n, u % 2, r, 0:w]
                        nc.scalar.activation(x, x, ACT.Exp, bias=ast[0:n, 0, u % 2, r:r + 1],
                                             accum_out=ast[0:n, 1, u % 2, r:r + 1]).then_inc(S["aexp"], 1)
                        if g == KVH - 1 and r == 1 and i + 1 < NTILE:
                            query_parts(i + 1)
            for m in range(NSAMP * KVH):
                b, g = divmod(m, KVH)
                act.wait_ge(S["sk_turned"], m + 1)
                if m >= 2:
                    act.wait_ge(S["sqk"], m - 1)
                nc.scalar.activation(skt[:, m % 2, :], psf[:, 2048 + 1024 * (m % 2):3072 + 1024 * (m % 2)],
                                     ACT.Copy).then_inc(S["sk_copied"], 1)
            act.wait_ge(S["smax"], 1)
            nc.scalar.activation(sprob[:, :], sprob[:, :], ACT.Exp, bias=sst64[:, 0:1],
                                 accum_out=sst64[:, 1:2]).then_inc(S["sexp"], 1)
            act.wait_ge(S["sp_turned"], 1)
            nc.scalar.activation(spt[:, 0:NPAGES, :], ps[:, 3, :].rearrange("p (j r) -> p j r", r=64), ACT.Copy)
            nc.scalar.activation(spt[0:1, NPAGES, :], ps[0:1, 4, 0:64], ACT.Copy).then_inc(S["spt_copied"], 1)
            for k in range(KT):
                act.wait_ge(S[f"o_in{k % 4}"], 16 * (k // 4 + 1))
                nc.scalar.activation(ohi[:, k, :], orow[:, k % 4, :], ACT.Copy).then_inc(S["o_hi"], 1)

            def squares(n, i=None):
                p = parity(n)
                add2 = 0 if i is None else 2 * i
                act.wait_ge(S["h_added"], n - B_OUT + 1 + add2)
                for t in range(NTILE):
                    c = cols_of(t)
                    last = nc.scalar.activation(sqj[0:c, t, :], hblk[0:c, p, t, :], ACT.Square,
                                                accum_out=sq[0:c, p, t:t + 1])
                last.then_inc(S["h_squared"], 1)

            def store_h(n, c, i=None):
                p = parity(n)
                full = NTILE - 1
                act.dma_start(hbuf_d[0:128 * full, c].rearrange("(t p) d -> p t d", p=128),
                              hblk[:, p, 0:full, :]).then_inc(S[f"h_stored{p}"], 16)
                act.dma_start(hbuf_d[128 * full:T, c], hblk[0:T - 128 * full, p, full, :]
                              ).then_inc(S[f"h_stored{p}"], 16)

            with act.Fori(0, NOUT // 2 - 1) as i:
                for n in (B_OUT, B_OUT + 1):
                    split_hi(act, n + 1, 0, i=i)
                    evacuate(act, n, i=i, stored=False)
                    split_hi(act, n + 1, 1, i=i)
                    squares(n, i)
                    store_h(n, bass.ds(i * 256 + 128 * (n - B_OUT), 128), i)
            n = B_OUT + NOUT - 2
            split_hi(act, n + 1, 0)
            evacuate(act, n, stored=False)
            split_hi(act, n + 1, 1)
            squares(n)
            store_h(n, slice(D - 256, D - 128))
            evacuate(act, n + 1, stored=False)
            squares(n + 1)
            store_h(n + 1, slice(D - 128, D))
            act.wait_ge(S["f_rms"], 1)
            nc.scalar.activation(fst[:, 3, :], fst[:, 2, :], ACT.Sqrt).then_inc(S["f_sqrt"], 1)
            for i in range(NTILE):
                act.wait_ge(S["f_done"], i + 1)
                for r0, n, _ in x_parts(i):
                    if i == 0 and r0 == 0:
                        continue
                    if i == NTILE - 1 and r0:
                        dst = io["y_sample"][:, 0, :]
                    else:
                        lo = 128 * i - META + r0
                        dst = io["y_prompt"][0, lo:lo + n, :]
                    act.dma_start(dst, fh[r0:r0 + n, i, :]).then_inc(S["y_out"], 16)
            act.wait_ge(S["y_out"], 16 * (NTILE + 1))
            act.wait_ge(S["outs"], 16 * (3 + NSAMP + 6))

        @block.vector
        def _(dve):
            tick = [0]

            def chain(ins):
                tick[0] += 1
                ins.then_inc(S["small"], 1)
                dve.wait_ge(S["small"], tick[0])

            dve.wait_ge(S["cst_in"], 16)

            def turned_lo(i):
                for q in range(4):
                    dve.wait_ge(S["a_hi"], 4 * i + q + 1)
                    c = cols_of(i)
                    out = slice(128 * i, 128 * i + c)
                    nc.vector.tensor_tensor(alo[:, 4 * q:4 * q + 4, out],
                                            ps[:, q, :].rearrange("p (k t) -> p k t", k=4)[:, :, 0:c],
                                            ahi[:, 4 * q:4 * q + 4, out].bitcast(F32),
                                            ALU.subtract).then_inc(S["a_lo"], 1)

            for i in range(NTILE):
                n = cols_of(i)
                col = [nst[0:n, r, i:i + 1] for r in range(6)]
                dve.wait_ge(S["x_sq"], i + 1)
                chain(nc.vector.tensor_scalar(col[1], col[0], 1.0 / D, EPS, ALU.mult, ALU.add))
                nc.vector.reciprocal(col[2], col[1]).then_inc(S["x_rms"], 1)
                dve.wait_ge(S["x_sqrt"], i + 1)
                chain(nc.vector.tensor_tensor(col[4], col[3], col[3], ALU.mult))
                chain(nc.vector.tensor_tensor(col[4], col[4], col[1], ALU.mult))
                chain(nc.vector.tensor_scalar(col[4], col[4], -0.5, 1.5, ALU.mult, ALU.add))
                chain(nc.vector.tensor_tensor(col[5], col[4], col[3], ALU.mult))
                if i == 0:
                    dve.wait_ge(S["g_in"], 16)
                nc.vector.scalar_tensor_tensor(out=xt[0:n, i % 3, :], in0=xt[0:n, i % 3, :], scalar=col[5],
                                               in1=gb[0:n, :], op0=ALU.mult, op1=ALU.mult).then_inc(S["x_scaled"], 1)
                if i:
                    turned_lo(i - 1)
            turned_lo(NTILE - 1)

            for n in (0, 1):
                for s in range(2):
                    split_lo(dve, n, s, WIDTH0 if n == 0 else 128)
            dve.wait_ge(S["kiw_turned"], 1)
            nc.vector.tensor_copy(kiw[:, 0:6, :], psf[:, 3072:3072 + 480].rearrange("p (t c) -> p t c", c=80))
            chain(nc.vector.tensor_copy(kiw[:, 6:9, :], psf[:, 3584:3584 + 240].rearrange("p (t c) -> p t c", c=80)))
            nc.vector.tensor_scalar(wsc[:, :, :], kiw[:, :, ID:ID + IH], ID ** -0.5 * IH ** -0.5, None,
                                    ALU.mult).then_inc(S["kiw_kept"], 1)
            with dve.Fori(0, NQI // 2) as i:
                for n in (2, 3):
                    for s in range(2):
                        split_lo(dve, n, s, i=i)

            nc.vector.memset(score[:, :], 0.0).then_inc(S["score_init"], 1)
            dve.wait_ge(S["ki_hi"], 1)
            nc.vector.tensor_tensor(klo[:, :], stage[:, 0, 0:L], khi[:, :].bitcast(F32),
                                    ALU.subtract).then_inc(S["ki_lo"], 1)

            def query_lo(n, i):
                dve.wait_ge(S["q_hi"], n + 1)
                c = cols_of(i)
                nc.vector.tensor_tensor(qst[64:128, n % 2, :, 0:c], qraw[64:128, n % 2, :, 0:c],
                                        qst[64:128, n % 2, :, 0:c].bitcast(F32), ALU.subtract).then_inc(S["q_lo"], 1)

            units = [(i, h) for i in TOPK_TILES for h in range(2)]
            query_lo(0, units[0][0])
            dve.wait_ge(S["score_init"], 1)
            u = 0
            for n, (i, h) in enumerate(units):
                if n + 1 < len(units):
                    query_lo(n + 1, units[n + 1][0])
                rows = rows_of(i)
                for k in range(IH // 2):
                    dve.wait_ge(S["relu_done"], u + 1)
                    if u:
                        dve.wait_ge(S["scored"], u)
                    out = score_of(i)[0:rows, :]
                    nc.vector.scalar_tensor_tensor(out=out, in0=relu[0:rows, u % 2, 0:keys_of(i)],
                                                   scalar=wsc[0:rows, i, 8 * h + k:8 * h + k + 1], in1=out,
                                                   op0=ALU.mult, op1=ALU.add).then_inc(S["scored"], 1)
                    u += 1
            dve.wait_ge(S["logits"], 8 * len(units))
            chain(nc.vector.memset(qbd[:, :, :], 0.0))
            for b in range(NSAMP):
                r = 64 * (b % 2)
                for h in range(2):
                    last = nc.vector.tensor_copy(qbd[r:r + 64, b // 2, 16 * b + 8 * h:16 * b + 8 * h + 8],
                                                 qraw[r:r + 64, h, :, TAIL + b])
                last.then_inc(S["qb_ready"], 1)
            dve.wait_ge(S["slogits"], NSAMP // 2)
            dve.wait_ge(S["wcol_in"], 16 * NSAMP)
            nc.vector.tensor_scalar(rsc[:, :], psf[:, 0:PAST + 1], 0.0, wcol[:, :], ALU.max,
                                    ALU.mult).then_inc(S["srelu"], 1)
            dve.wait_ge(S["ssum"], 1)
            last8 = score_of(NTILE - 1)
            nc.vector.tensor_scalar(last8[32:40, 0:PAST + 1], psf[32:40, 1536:1536 + PAST + 1],
                                    ID ** -0.5 * IH ** -0.5, None, ALU.mult).then_inc(S["ssum_kept"], 1)
            dve.wait_ge(S["ssum_kept"], 1)
            chain(nc.vector.memset(last8[32:40, PAST + 1:L], NEG_MASK))
            dve.wait_ge(S["score_init"], 2)

            with dve.Fori(0, ROUNDS // 2) as i:
                for q, n in enumerate((B_MAIN + 1, B_MAIN + 2)):
                    for m, t in enumerate(TOPK_TILES):
                        r = 128 if t < NTILE - 1 else 40
                        x = nc.vector.max(m8[0:r, m, :], score_of(t)[0:r, :])
                    x.then_inc(S["maxed"], 1)
                    dve.wait_ge(S["maxed"], 2 * i + q + 1)
                    split_lo(dve, n, 0, i=i)
                    for m, t in enumerate(TOPK_TILES):
                        r = 128 if t < NTILE - 1 else 40
                        x = nc.vector.match_replace(score_of(t)[0:r, :], m8[0:r, m, :], score_of(t)[0:r, :], NEG_TAKEN)
                    x.then_inc(S["taken"], 1)
                    dve.wait_ge(S["taken"], 2 * i + q + 1)
                    split_lo(dve, n, 1, i=i)
            for n in range(B_MAIN + 1 + ROUNDS, B_OUT + 1):
                for s in range(2):
                    split_lo(dve, n, s)
            dve.wait_ge(S["spos_in"], 16)
            for t in TOPK_TILES:
                n = 128 if t < NTILE - 1 else 40
                x = score_of(t)[0:n, :]
                chain(nc.vector.tensor_scalar(x, x, (NEG_TAKEN + NEG_MASK) / 2, NEG_BIAS, ALU.is_gt, ALU.mult))
                chain(nc.vector.scalar_tensor_tensor(out=x, in0=x, scalar=cst[0:n, K_TQ + t:K_TQ + t + 1],
                                                     in1=spos[0:n, 0:keys_of(t)], op0=ALU.add, op1=ALU.add))
            for t in range(FIRST_TOPK):
                nc.vector.tensor_scalar(dist_of(t), spos[:, 0:keys_of(t)], cst[:, K_TQ + t:K_TQ + t + 1], None,
                                        ALU.add).then_inc(S["dist_made"], 1)
            dve.wait_ge(S["ak_hi"], 1)
            nc.vector.tensor_tensor(akl[:, :, :], kvin[:, 0:KVH, 0:L], akh[:, :, :].bitcast(F32),
                                    ALU.subtract).then_inc(S["ak_lo"], 1)

            def query_rest(i):
                dve.wait_ge(S["aq_hi"], i + 1)
                c = cols_of(i)
                nc.vector.scalar_tensor_tensor(out=ql[:, i % 2, :, 0:c], in0=qin[:, i % 2, :, 0:c], scalar=HD ** -0.5,
                                               in1=qh[:, i % 2, :, 0:c].bitcast(F32), op0=ALU.mult,
                                               op1=ALU.subtract).then_inc(S["aq_lo"], 1)

            query_rest(0)
            dve.wait_ge(S["dist_masked"], FIRST_TOPK)
            dve.wait_ge(S["kv_turned"], NTILE)

            def normalize(u, r):
                i, g = AUNITS[u]
                n, w = rows_of(i), keys_of(i)
                dve.wait_ge(S["aexp"], 4 * u + r + 1)
                chain(nc.vector.reciprocal(ast[0:n, 2, u % 2, r:r + 1], ast[0:n, 1, u % 2, r:r + 1]))
                x = prob[0:n, u % 2, r, 0:w]
                nc.vector.tensor_scalar(x, x, ast[0:n, 2, u % 2, r:r + 1], None, ALU.mult).then_inc(S["normed"], 1)

            def gate(u):
                i, g = AUNITS[u]
                n = rows_of(i)
                dve.wait_ge(S["pv_mm"], blocks_to(u + 1))
                if u >= 2:
                    dve.wait_ge(S[f"o_stored{u % 2}"], 16 * (u // 2))
                nc.vector.tensor_tensor(osb[:, u % 2, :, 0:n], ps[:, 7, 0:4 * n].rearrange("p (h t) -> p h t", h=4),
                                        zin[:, i % 2, 4 * g:4 * g + 4, 0:n], ALU.mult).then_inc(S["gated"], 1)

            for u, (i, g) in enumerate(AUNITS):
                n, w = rows_of(i), keys_of(i)
                for r in range(4):
                    k = 4 * u + r
                    dve.wait_ge(S["aqk"], k + 1)
                    if u >= 2 and r == 0:
                        dve.wait_ge(S["p_turned"], blocks_to(u - 1))
                    x = prob[0:n, u % 2, r, 0:w]
                    nc.vector.scalar_tensor_tensor(out=x, in0=dist_of(i)[0:n, :], scalar=2.0 ** -(4 * g + r + 1),
                                                   in1=psf[0:n, 1536 * (k % 2):1536 * (k % 2) + w],
                                                   op0=ALU.mult, op1=ALU.add).then_inc(S["abias"], 1)
                    dve.wait_ge(S["abias"], k + 1)
                    chain(nc.vector.tensor_reduce(ast[0:n, 0, u % 2, r:r + 1], x, AX.X, ALU.max))
                    nc.vector.tensor_scalar(ast[0:n, 0, u % 2, r:r + 1], ast[0:n, 0, u % 2, r:r + 1], -1.0, None,
                                            ALU.mult).then_inc(S["amax"], 1)
                    if r:
                        normalize(u, r - 1)
                    if g == KVH - 1 and r == 2 and i + 1 < NTILE:
                        query_rest(i + 1)
                normalize(u, 3)
                if u:
                    gate(u - 1)
            dve.wait_ge(S["p_turned"], blocks_to(len(AUNITS)))
            chain(nc.vector.memset(qz[:, :, :], 0.0))
            last_q = (NTILE - 1) % 2
            for m in range(NSAMP * KVH):
                b, g = divmod(m, KVH)
                x = nc.vector.tensor_scalar(qz[:, m, 8 * b + 4 * g:8 * b + 4 * g + 4],
                                            qin[:, last_q, 4 * g:4 * g + 4, TAIL + b], HD ** -0.5, None, ALU.mult)
            x.then_inc(S["qz_made"], 1)
            dve.wait_ge(S["sdist"], 1)
            nc.vector.tensor_scalar(sbias[:, :], psf[0:64, 0:PAST + 1], cst[0:64, K_SLOPE:K_SLOPE + 1], None,
                                    ALU.mult).then_inc(S["sbias_made"], 1)
            gate(len(AUNITS) - 1)
            dve.wait_ge(S["sqk"], NSAMP * KVH)
            dve.wait_ge(S["sbias_made"], 1)
            chain(nc.vector.tensor_tensor(sprob[:, :], psf[0:64, 0:PAST + 1], sbias[:, :], ALU.add))
            chain(nc.vector.tensor_reduce(sst64[:, 0:1], sprob[:, :], AX.X, ALU.max))
            nc.vector.tensor_scalar(sst64[:, 0:1], sst64[:, 0:1], -1.0, None, ALU.mult).then_inc(S["smax"], 1)
            dve.wait_ge(S["sexp"], 1)
            chain(nc.vector.reciprocal(sst64[:, 2:3], sst64[:, 1:2]))
            nc.vector.tensor_scalar(sprob[:, :], sprob[:, :], sst64[:, 2:3], None, ALU.mult).then_inc(S["snormed"], 1)
            dve.wait_ge(S["sv_used"], NSAMP)
            nc.vector.tensor_tensor(osamp[:, :, :].rearrange("p h b -> p b h"),
                                    ps[:, 5, 0:64].rearrange("p (b h) -> p b h", b=NSAMP),
                                    zin[:, last_q, :, TAIL:TAIL + NSAMP].rearrange("p h b -> p b h"),
                                    ALU.mult).then_inc(S["sgated"], 1)
            for k in range(KT):
                dve.wait_ge(S["o_hi"], k + 1)
                nc.vector.tensor_tensor(olo[:, k, :], orow[:, k % 4, :], ohi[:, k, :].bitcast(F32),
                                        ALU.subtract).then_inc(S["o_lo"], 1)
            chain(nc.vector.memset(fst[:, 0, :], 0.0))

            def add_residual(n, i=None):
                p = parity(n)
                add1, add2 = (0, 0) if i is None else (i, 2 * i)
                dve.wait_ge(S["h_turned"], 2 * (n - B_OUT) + 1 + 2 * add2)
                dve.wait_ge(S[f"xb_in{p}"], 80 * ((n - B_OUT) // 2 + 1) + 80 * add1)
                if n >= B_OUT + 2:
                    dve.wait_ge(S[f"h_stored{p}"], 32 * ((n - B_OUT) // 2) + 32 * add1)
                nc.vector.tensor_tensor(hblk[:, p, 0:8, :], psf[:, 3072:4096].rearrange("p (t c) -> p t c", c=128),
                                        xblk[:, p, 0:8, :], ALU.add).then_inc(S["h_part"], 1)
                dve.wait_ge(S["h_turned"], 2 * (n - B_OUT) + 2 + 2 * add2)
                c = cols_of(NTILE - 1)
                nc.vector.tensor_tensor(hblk[0:c, p, NTILE - 1, :], ps[0:c, 6, 0:128], xblk[0:c, p, NTILE - 1, :],
                                        ALU.add).then_inc(S["h_added"], 1)

            def add_squares(n, i=None):
                p = parity(n)
                add2 = 0 if i is None else 2 * i
                dve.wait_ge(S["h_squared"], n - B_OUT + 1 + add2)
                nc.vector.tensor_tensor(fst[:, 0, 0:8], fst[:, 0, 0:8], sq[:, p, 0:8], ALU.add)
                c = cols_of(NTILE - 1)
                nc.vector.tensor_tensor(fst[0:c, 0, 8:9], fst[0:c, 0, 8:9], sq[0:c, p, 8:9], ALU.add
                                        ).then_inc(S["sq_added"], 1)
                dve.wait_ge(S["sq_added"], n - B_OUT + 1 + add2)

            def out_block(n, i=None):
                split_lo(dve, n + 1, 0, i=i)
                split_lo(dve, n + 1, 1, i=i)
                add_residual(n, i)
                add_squares(n, i)

            out_block(B_OUT)
            out_block(B_OUT + 1)
            with dve.Fori(0, NOUT // 2 - 2) as i:
                out_block(B_OUT + 2, i)
                out_block(B_OUT + 3, i)
            n = B_OUT + NOUT - 2
            split_lo(dve, n + 1, 0)
            split_lo(dve, n + 1, 1)
            add_residual(n)
            add_squares(n)
            add_residual(n + 1)
            add_squares(n + 1)
            col = [fst[:, r, :] for r in range(6)]
            chain(nc.vector.tensor_scalar(col[1], col[0], 1.0 / D, EPS, ALU.mult, ALU.add))
            nc.vector.reciprocal(col[2], col[1]).then_inc(S["f_rms"], 1)
            dve.wait_ge(S["f_sqrt"], 1)
            chain(nc.vector.tensor_tensor(col[4], col[3], col[3], ALU.mult))
            chain(nc.vector.tensor_tensor(col[4], col[4], col[1], ALU.mult))
            chain(nc.vector.tensor_scalar(col[4], col[4], -0.5, 1.5, ALU.mult, ALU.add))
            chain(nc.vector.tensor_tensor(col[5], col[4], col[3], ALU.mult))
            dve.wait_ge(S["fg_in"], 16)
            for i in range(NTILE):
                n = cols_of(i)
                dve.wait_ge(S[f"fh_in{i}"], 16)
                nc.vector.scalar_tensor_tensor(out=fh[0:n, i, :], in0=fh[0:n, i, :], scalar=fst[0:n, 5, i:i + 1],
                                               in1=fg[0:n, :], op0=ALU.mult, op1=ALU.mult).then_inc(S["f_done"], 1)

        @block.tensor
        def _(pe):
            pe.wait_ge(S["cst_in"], 16)
            for i in range(NTILE):
                pe.wait_ge(S["x_scaled"], i + 1)
                n = cols_of(i)
                for q in range(4):
                    if i:
                        pe.wait_ge(S["a_lo"], 4 * (i - 1) + q + 1)
                    for k in range(4):
                        last = nc.tensor.transpose(ps[:, q, 128 * k:128 * k + n],
                                                   xt[0:n, i % 3, 128 * (4 * q + k):128 * (4 * q + k) + 128],
                                                   ident[0:n, 0:n])
                    last.then_inc(S["x_turned"], 1)
            pe.wait_ge(S["a_lo"], 4 * NTILE)
            pe.wait_ge(S["x_sq"], NTILE)
            project(pe, 0, WIDTH0, first=True)
            project(pe, 1, first=True)
            pe.wait_ge(S["evac"], 1)
            for i in range(NTILE):
                n = cols_of(i)
                at = 3072 + 80 * i if i < 6 else 3584 + 80 * (i - 6)
                last = nc.tensor.transpose(psf[0:n, at:at + WIDTH0], stage[0:WIDTH0, 1, 128 * i:128 * i + n],
                                           ident[0:WIDTH0, 0:WIDTH0])
            last.then_inc(S["kiw_turned"], 1)
            project(pe, 2)
            with pe.Fori(0, NQI // 2 - 1) as i:
                project(pe, 3, i=i)
                project(pe, 4, i=i)
            pe.wait_ge(S["evac"], B_MAIN)
            pe.wait_ge(S["ki_lo"], 1)
            units = [(i, h) for i in TOPK_TILES for h in range(2)]
            u = 0
            for n, (i, h) in enumerate(units):
                pe.wait_ge(S["q_lo"], n + 1)
                rows = rows_of(i)
                for k in range(IH // 2):
                    if u >= 2:
                        pe.wait_ge(S["relu_done"], u - 1)
                    for m in (khi, klo):
                        for c, w in banks(keys_of(i)):
                            o = 1536 * (u % 2) + c
                            last = nc.tensor.matmul(psf[0:rows, o:o + w], qst[:, n % 2, k, 0:rows], m[:, c:c + w],
                                                    start=m is khi, stop=m is klo)
                    last.then_inc(S["logits"], 1)
                    u += 1
            for j in range(NSAMP // 2):
                pe.wait_ge(S["ik_in"], 16 * 2 * NPAGES * (j + 1))
                if j:
                    pe.wait_ge(S["ik_copied"], j)
                for k in range(NPAGES):
                    last = nc.tensor.transpose(psf[:, 3072 + 128 * k:3072 + 128 * k + 128],
                                               iload[:, k, :, :].rearrange("p b d -> p (b d)"), ident)
                last.then_inc(S["ik_turned"], 1)
                pe.wait_ge(S["ik_copied"], j + 1)
                pe.wait_ge(S["ikn_in"], 32 * (j + 1))
                if j == 0:
                    pe.wait_ge(S["qb_ready"], 8)
                    pe.wait_ge(S["relu_done"], u)
                for c, w in banks(PAST + 1):
                    last = nc.tensor.matmul(psf[:, c:c + w], qbd[:, j, :], ikt[:, c:c + w],
                                            start=j == 0, stop=j == NSAMP // 2 - 1)
                last.then_inc(S["slogits"], 1)
            pe.wait_ge(S["srelu"], 1)
            for c, w in banks(PAST + 1):
                last = nc.tensor.matmul(psf[32:40, 1536 + c:1536 + c + w], cst[:, K_ONEB:K_ONEB + 8], rsc[:, c:c + w],
                                        start=True, stop=True)
            last.then_inc(S["ssum"], 1)
            pe.wait_ge(S["ssum_kept"], 1)
            with pe.Fori(0, POOLW // 128) as i:
                project(pe, B_MAIN, i=i)
                project(pe, B_MAIN + 1, i=i)
            pe.wait_ge(S["ul_in"], 16)
            for c in range(POOLW // 128):
                last = nc.tensor.transpose(psf[0:PAD + NSAMP, 3072 + 128 * c:3072 + 128 * c + 128], ulast[:, c, :], ident)
            last.then_inc(S["ul_turned"], 1)
            pe.wait_ge(S["state_in"], 32)
            pe.wait_ge(S["ul_kept"], 1)
            rows = NSAMP * PAD
            for c in range(POOLW // 128):
                g = c // 2
                last = nc.tensor.matmul(ps[:, 6, 8 * c:8 * c + 8], strow[:, 128 * c:128 * c + 128],
                                        cst[0:rows, K_STATE + 8 * g:K_STATE + 8 * g + 8], start=True, stop=True)
            last.then_inc(S["st_summed"], 1)
            B_GRP = B_MAIN + 2 * (POOLW // 128)
            with pe.Fori(0, POOLW // GROUP) as g:
                for q in range(4):
                    project(pe, B_GRP + q, i=g * 2)
                pe.wait_ge(S["p_mixed"], g + 1)
                pe.wait_ge(S["p_in"], g * 48 + 48)
                for x in range(6):
                    m, c = divmod(x, 3)
                    t0, tn = CHUNKS[c]
                    if x < 2:
                        pe.wait_ge(S["st_kept"], 1)
                    else:
                        pe.wait_ge(S["p_scaled"], g * 6 + x - 1)
                    for k in range(2):
                        last = nc.tensor.matmul(ps[:, 6 + x % 2, 0:tn], pw[:, k, 128 * m:128 * m + 128],
                                                pu[:, k, t0:t0 + tn], start=k == 0, stop=k == 1)
                    last.then_inc(S["p_mm"], 1)
            with pe.Fori(0, (B_OUT - B_GRP - 16) // 2) as i:
                project(pe, B_GRP + 16, i=i)
                project(pe, B_GRP + 17, i=i)
            pe.wait_ge(S["evac"], B_OUT)
            pe.wait_ge(S["kv_in"], 16)
            for i in range(NTILE):
                n = cols_of(i)
                if i >= 6:
                    pe.wait_ge(S["kvtok_kept"], i - 5)
                for b in range(2 * KVH):
                    last = nc.tensor.transpose(ps[0:n, i % 6, 128 * b:128 * b + 128], kvin[:, b, 128 * i:128 * i + n], ident)
                last.then_inc(S["kv_turned"], 1)
            pe.wait_ge(S["kvtok_kept"], NTILE)
            pe.wait_ge(S["ak_lo"], 1)
            pe.wait_ge(S["p_scaled"], 24)
            t = 0
            for u in range(len(AUNITS) + 1):
                for r in range(4):
                    if u < len(AUNITS):
                        i, g = AUNITS[u]
                        n, w = rows_of(i), keys_of(i)
                        k = 4 * u + r
                        if r == 0:
                            pe.wait_ge(S["aq_lo"], i + 1)
                        if k >= 2:
                            pe.wait_ge(S["abias"], k - 1)
                        h = 4 * g + r
                        for q, m in ((qh, akh), (qh, akl), (ql, akh)):
                            for c, cw in banks(w):
                                o = 1536 * (k % 2) + c
                                last = nc.tensor.matmul(psf[0:n, o:o + cw], q[:, i % 2, h, 0:n], m[:, g, c:c + cw],
                                                        start=m is akh and q is qh, stop=q is ql)
                        last.then_inc(S["aqk"], 1)
                    if u:
                        i, g = AUNITS[u - 1]
                        n = rows_of(i)
                        if r == 0:
                            pe.wait_ge(S["normed"], 4 * u)
                        for j in quarter(i, r):
                            kn = min(128, L - 128 * j)
                            if t:
                                pe.wait_ge(S["pt_copied"], t)
                            for h in range(4):
                                last = nc.tensor.transpose(ps[0:kn, 6, n * h:n * h + n],
                                                           prob[0:n, (u - 1) % 2, h, 128 * j:128 * j + kn],
                                                           ident[0:n, 0:n])
                            last.then_inc(S["p_turned"], 1)
                            pe.wait_ge(S["pt_copied"], t + 1)
                            if j == 0 and u > 1:
                                pe.wait_ge(S["gated"], u - 1)
                            last = nc.tensor.matmul(ps[:, 7, 0:4 * n], kvtok[0:kn, j, 256 + 128 * g:256 + 128 * g + 128],
                                                    pts[0:kn, t % 2, 0:4 * n], start=j == 0, stop=j == i)
                            last.then_inc(S["pv_mm"], 1)
                            t += 1
            pe.wait_ge(S["abias"], 4 * len(AUNITS))
            for c, w in banks(PAST + 1):
                last = nc.tensor.matmul(psf[0:64, c:c + w], cst[32:40, K_ESEL:K_ESEL + 64],
                                        score_of(NTILE - 1)[32:40, c:c + w], start=True, stop=True)
            last.then_inc(S["sdist"], 1)
            pe.wait_ge(S["gated"], len(AUNITS))
            for m in range(NSAMP * KVH + 1):
                if m < NSAMP * KVH:
                    b, g = divmod(m, KVH)
                    pe.wait_ge(S[f"slot_in{b % 4}"], 16 * NPAGES * (b // 4 + 1))
                    if m >= 2:
                        pe.wait_ge(S["sk_copied"], m - 1)
                    for k in range(NPAGES):
                        o = 2048 + 1024 * (m % 2) + 128 * k
                        last = nc.tensor.transpose(psf[:, o:o + 128], slot[:, b % 4, k, 128 * g:128 * g + 128], ident)
                    last.then_inc(S["sk_turned"], 1)
                if m == 0:
                    pe.wait_ge(S["qz_made"], 1)
                    pe.wait_ge(S["sbias_made"], 1)
                    pe.wait_ge(S["knew_kept"], 1)
                if m:
                    b, g = divmod(m - 1, KVH)
                    pe.wait_ge(S["sk_copied"], m)
                    q = qz[:, m - 1, :]
                    for c, w in banks(PAST):
                        nc.tensor.matmul(psf[0:64, c:c + w], q, skt[:, (m - 1) % 2, c:c + w], start=m == 1,
                                         stop=m == NSAMP * KVH)
                    nc.tensor.matmul(psf[0:64, PAST:PAST + 1], q, knew[:, g, b:b + 1], start=m == 1,
                                     stop=m == NSAMP * KVH).then_inc(S["sqk"], 1)
            pe.wait_ge(S["snormed"], 1)
            for k in range(NPAGES):
                nc.tensor.transpose(ps[:, 3, 64 * k:64 * k + 64], sprob[:, 128 * k:128 * k + 128], ident[0:64, 0:64])
            nc.tensor.transpose(ps[0:1, 4, 0:64], sprob[:, PAST:PAST + 1], ident[0:64, 0:64]).then_inc(S["sp_turned"], 1)
            pe.wait_ge(S["spt_copied"], 1)
            pe.wait_ge(S["vnew_in"], 16)
            for b in range(NSAMP):
                pe.wait_ge(S[f"slot_in{b % 4}"], 16 * NPAGES * (2 + b // 4 + 1))
                for g in range(KVH):
                    o = 8 * b + 4 * g
                    for k in range(NPAGES):
                        nc.tensor.matmul(ps[:, 5, o:o + 4], slot[:, b % 4, k, 128 * g:128 * g + 128],
                                         spt[:, k, o:o + 4], start=k == 0, stop=False)
                    v = vnew[0:1, 256 * b + 128 * g:256 * b + 128 * g + 128]
                    last = nc.tensor.matmul(ps[:, 5, o:o + 4], v, spt[0:1, NPAGES, o:o + 4], start=False, stop=True)
                last.then_inc(S["sv_used"], 1)

            def turn_h(n, part, i=None):
                p = parity(n)
                add2 = 0 if i is None else 2 * i
                if part == 0:
                    pe.wait_ge(S["evac"], n + 1 + add2)
                    if n > B_OUT:
                        pe.wait_ge(S["h_added"], n - B_OUT + add2)
                    else:
                        pe.wait_ge(S["sgated"], 1)
                    for t in range(NTILE - 1):
                        last = nc.tensor.transpose(psf[:, 3072 + 128 * t:3200 + 128 * t],
                                                   stage[:, p, 128 * t:128 * t + 128], ident)
                else:
                    pe.wait_ge(S["h_part"], n - B_OUT + 1 + add2)
                    c = cols_of(NTILE - 1)
                    last = nc.tensor.transpose(ps[0:c, 6, 0:128], stage[:, p, T - c:T], ident)
                last.then_inc(S["h_turned"], 1)

            def project_out(n, i=None, before=True):
                project(pe, n, i=i, src=(ohi, olo), first_out=n == B_OUT and i is None,
                        between=(lambda: turn_h(n - 1, 0, i)) if before else None)
                if before:
                    turn_h(n - 1, 1, i)

            project_out(B_OUT, before=False)
            project_out(B_OUT + 1)
            with pe.Fori(0, NOUT // 2 - 1) as i:
                project_out(B_OUT + 2, i)
                project_out(B_OUT + 3, i)
            turn_h(B_OUT + NOUT - 1, 0)
            turn_h(B_OUT + NOUT - 1, 1)

        @block.gpsimd
        def _(pool):
            pool.wait_ge(S["scored"], len(TOPK_TILES) * IH)
            for i in TOPK_TILES:
                x = score_of(i)[0:rows_of(i), :]
                last = nc.gpsimd.affine_select(out=x, in_=x, compare_op=ALU.is_ge, fill=NEG_MASK, base=128 * i,
                                               pattern=[[-1, keys_of(i)]], channel_multiplier=1)
            last.then_inc(S["score_init"], 1)
            tick = [0]

            def chain(ins):
                tick[0] += 1
                ins.then_inc(S["pool_step"], 1)
                pool.wait_ge(S["pool_step"], tick[0])

            for g in range(POOLW // GROUP):
                w = 2 << g
                pool.wait_ge(S["p_in"], 48 * (g + 1))
                pool.wait_ge(S["st_kept"], 1)
                for c in range(2):
                    u = pu[:, c, :]
                    a, b = pt[:, 0, :], pt[:, 1, :]
                    src, dst, step = u, a, 1
                    while step < w:
                        nc.gpsimd.tensor_copy(dst[:, 0:step], src[:, 0:step])
                        chain(nc.gpsimd.tensor_tensor(dst[:, step:L], src[:, step:L], src[:, 0:L - step], ALU.add))
                        src, dst, step = dst, (b if dst is a else a), 2 * step
                    nc.gpsimd.tensor_tensor(src[:, 0:16], src[:, 0:16], cst[:, K_CINV + 16 * g:K_CINV + 16 * g + 16], ALU.mult)
                    nc.gpsimd.tensor_scalar(src[:, 16:L], src[:, 16:L], 1.0 / w, None, ALU.mult)
                    chain(nc.gpsimd.tensor_tensor(dst[:, 0:NSAMP], sst[:, 2 * g + c, :], u[:, L:T], ALU.add))
                    chain(nc.gpsimd.tensor_scalar(dst[:, 0:NSAMP], dst[:, 0:NSAMP], 1.0 / w, None, ALU.mult))
                    nc.gpsimd.tensor_tensor(u[:, 0:L], src[:, 0:L], u[:, 0:L], ALU.subtract)
                    chain(nc.gpsimd.tensor_tensor(u[:, L:T], dst[:, 0:NSAMP], u[:, L:T], ALU.subtract))
                nc.gpsimd.engine_nop().then_inc(S["p_mixed"], 1)
                pool.wait_ge(S["p_scaled"], 6 * (g + 1))
                nc.gpsimd.tensor_tensor(pz[:, :, :], pz[:, :, :], pt[:, :, :], ALU.mult).then_inc(S["p_gated"], 1)
                pool.wait_ge(S["p_gated"], g + 1)
                pool.dma_start(mixt[GROUP * g:GROUP * (g + 1), :].rearrange("(c p) t -> p c t", p=128), pz[:, :, :]
                               ).then_inc(S["p_stored"], 16)
            for t in range(FIRST_TOPK):
                pool.wait_ge(S["dist_made"], FIRST_TOPK)
                nc.gpsimd.affine_select(out=dist_of(t), in_=dist_of(t), compare_op=ALU.is_ge, fill=NEG_BIAS,
                                        base=128 * t, pattern=[[-1, keys_of(t)]], channel_multiplier=1
                                        ).then_inc(S["dist_masked"], 1)


_INS = ["x_prompt", "x_sample", "cache_k", "cache_v", "cache_idx_k", "state_pool", "page_table",
        "meta_tokens", "norm_g", "w_in", "w_pool", "pool_scale", "w_out", "final_norm_g"]
_OUTS = [("y_prompt", (1, SEQ, D)), ("y_sample", (NSAMP, 1, D)),
         ("new_k_prompt", (1, 1, L, KVH, HD)), ("new_v_prompt", (1, 1, L, KVH, HD)),
         ("new_idx_k_prompt", (1, 1, L, ID)), ("new_pool_prompt", (1, 1, PAD, POOLW)),
         ("new_k_sample", (1, NSAMP, 1, KVH, HD)), ("new_v_sample", (1, NSAMP, 1, KVH, HD)),
         ("new_idx_k_sample", (1, NSAMP, 1, ID)), ("new_pool_sample", (1, NSAMP, PAD, POOLW))]


def kernel(**inputs):
    import concourse.bacc as _bacc
    from concourse.bass_utils import run_bass_kernel_spmd as _run

    nc = _bacc.Bacc("TRN2", target_bir_lowering=False, num_devices=1, dynamic_dma_scratch_size=1024)
    arrays = {n: np.ascontiguousarray(inputs[n]) for n in _INS}
    arrays["consts"] = constants()
    io = {n: nc.dram_tensor(n, a.shape, mybir.dt.from_np(a.dtype), kind="ExternalInput").ap()
          for n, a in arrays.items()}
    for n, shape in _OUTS:
        io[n] = nc.dram_tensor(n, shape, F32, kind="ExternalOutput").ap()
    build(nc, io)
    r = _run(nc, [arrays], core_ids=[0])
    return tuple(r.results[0][n] for n, _ in _OUTS)
```

```python
from contextlib import ExitStack

import concourse.bass as bass
import numpy as np
from concourse import mybir

F32 = mybir.dt.float32
F32R = mybir.dt.float32r
I32 = mybir.dt.int32
ALU = mybir.AluOpType
ACT = mybir.ActivationFunctionType
AX = mybir.AxisListType

D = 2048
META, SEQ, NSAMP = 16, 1024, 8
L = META + SEQ
T = L + NSAMP
NTILE = -(-T // 128)
TAIL = L - 128 * (NTILE - 1)
POOLW, GROUP, PAD = 1024, 256, 15
HEADS, KVH, HD = 8, 2, 128
IH, ID = 16, 64
PAST, PAGE, NPAGES = 1024, 128, 8
NPHYS = 80
TOPK = 256
EPS = 1e-6
C_U, C_ZP, C_Q, C_K, C_V, C_ZA, C_QI, C_KI, C_WI = np.cumsum(
    [0, POOLW, POOLW, HEADS * HD, KVH * HD, KVH * HD, HEADS * HD, IH * ID, ID]).tolist()
DIN = C_WI + IH
KT = D // 128
HALF = KT // 2
NMAIN = C_QI // 128
NQI = IH * ID // 128
NOUT = D // 128
CHUNKS = [(0, 350), (350, 350), (700, T - 700)]
BANK = 512
NEG_MASK = -1.0e38
NEG_TAKEN = -3.0e38
NEG_BIAS = -1.0e30
FIRST_TOPK = TOPK // 128
TOPK_TILES = list(range(FIRST_TOPK, NTILE))
ROUNDS = TOPK // 8




def rows_of(i):
    return 128 if i < NTILE - 1 else TAIL


def cols_of(i):
    return 128 if i < NTILE - 1 else T - 128 * i


def keys_of(i):
    return min(128 * (i + 1), L)


def banks(width):
    return [(c, min(BANK, width - c)) for c in range(0, width, BANK)]


K_ID, K_TQ, K_ESEL, K_ONEB, K_SLOPE, K_CINV, K_STATE, K_S = np.cumsum(
    [0, 128, NTILE, 64, 8, 1, 4 * 16, 4 * 8]).tolist()
K_ALL = K_S + L


def constants():
    c = np.zeros((128, K_ALL), np.float32)
    p = np.arange(128)
    c[:, K_ID:K_ID + 128] = np.eye(128)
    c[:, K_S:K_S + L] = np.arange(L)[None]
    for i in range(NTILE):
        c[:, K_TQ + i] = -(128 * i + p)
    c[32:40, K_TQ + NTILE - 1] = -PAST
    for b in range(NSAMP):
        c[32 + b, K_ESEL + 8 * b:K_ESEL + 8 * b + 8] = 1
        c[16 * b:16 * b + 16, K_ONEB + b] = 1
    c[:, K_SLOPE] = 2.0 ** -(p % 8 + 1)
    for g in range(4):
        w = 2 << g
        c[:, K_CINV + 16 * g:K_CINV + 16 * g + 16] = 1 / np.minimum(np.arange(16) + 1, w)
        for b in range(NSAMP):
            c[15 * b + 16 - w:15 * b + 15, K_STATE + 8 * g + b] = 1
    return c


def build(nc, io):
    xp, xs_, ck, cv, cik = (io[n] for n in ("x_prompt", "x_sample", "cache_k", "cache_v", "cache_idx_k"))
    state, ptab, meta = io["state_pool"], io["page_table"], io["meta_tokens"]
    norm_g, w_in, w_pool, pscale = io["norm_g"], io["w_in"], io["w_pool"], io["pool_scale"]
    w_out, fin_g, consts = io["w_out"], io["final_norm_g"], io["consts"]

    proj = nc.dram_tensor("proj_scratch", (DIN, T), F32, kind="Internal").ap()
    mixt = nc.dram_tensor("mix_scratch", (D, T), F32, kind="Internal").ap()
    hbuf_d = nc.dram_tensor("h_scratch", (NTILE * 128, D), F32, kind="Internal").ap()

    def x_parts(i):
        if i == 0:
            return [(0, META, meta[:, :]), (META, 128 - META, xp[0, 0:128 - META, :])]
        lo = 128 * i - META
        if i < NTILE - 1:
            return [(0, 128, xp[0, lo:lo + 128, :])]
        return [(0, TAIL, xp[0, lo:SEQ, :]), (TAIL, NSAMP, xs_[:, 0, :])]

    X_PARTS = [len(x_parts(i)) for i in range(NTILE)]

    with ExitStack() as top:
        def sem(name):
            return top.enter_context(nc.semaphore(name))

        def sb(name, shape, dt=F32, ctx=top):
            return ctx.enter_context(nc.sbuf_tensor(name, shape, dt))

        ps = top.enter_context(nc.psum_tensor("ps", [128, 8, BANK], F32))
        psf = ps[:, :, :].rearrange("p b c -> p (b c)")
        cst = sb("cst", [128, K_S])
        ident = cst[:, K_ID:K_ID + 128]
        pages = sb("pages", [1, NSAMP * NPAGES], I32)
        with ExitStack() as c1:
            wslot = sb("wslot", [128, 4, NPAGES, KVH * HD], F32, c1)
        wraw = sb("wraw", [128, 4, HALF, 128])
        whi = sb("whi", [128, 2, HALF, 128], F32R)
        wlo = sb("wlo", [128, 2, HALF, 128], F32R)
        with ExitStack() as c1:
            akh = sb("akh", [128, KVH, L], F32R, c1)
            akl = sb("akl", [128, KVH, L], F32R, c1)
            kvtok = sb("kvtok", [128, NTILE, 2 * KVH * HD], F32, c1)
            pts = sb("pts", [128, 2, BANK], F32, c1)
            with ExitStack() as c2:
                vslot = sb("vslot", [128, 3, NPAGES, KVH * HD], F32, c2)
            qin = sb("qin", [128, 2, HEADS, 128], F32, c1)
            qh = sb("qh", [128, 2, HEADS, 128], F32R, c1)
            ql = sb("ql", [128, 2, HEADS, 128], F32R, c1)
            slot = sb("slot", [128, 4, NPAGES, KVH * HD], F32, c1)
            with ExitStack() as c2:
                prob = sb("prob", [128, 2, 4, L], F32, c2)
            with ExitStack() as c2:
                vslot3 = sb("vslot3", [128, NPAGES, KVH * HD], F32, c2)
                skt = sb("skt", [128, 2, PAST], F32, c2)
                qz = sb("qz", [128, NSAMP * KVH, 64], F32, c2)
                sbias = sb("sbias", [64, PAST + 1], F32, c2)
                sprob = sb("sprob", [64, PAST + 1], F32, c2)
                spt = sb("spt", [128, NPAGES + 1, 64], F32, c2)
        with ExitStack() as c1:
            oparts = sb("oparts", [128, KT, 2, T], F32R, c1)
            ohi, olo = oparts[:, :, 0, :], oparts[:, :, 1, :]
        with ExitStack() as c1:
            fh = sb("fh", [128, NTILE, D], F32, c1)
            fg = sb("fg", [128, D], F32, c1)
        ahi = sb("ahi", [128, KT, T], F32R)
        alo = sb("alo", [128, KT, T], F32R)
        with ExitStack() as c1:
            xt = sb("xt", [128, 3, D], F32, c1)
            gb = sb("gb", [128, D], F32, c1)
            nst = sb("nst", [128, 6, NTILE], F32, c1)
        stage = sb("stage", [128, 2, T])
        with ExitStack() as c1:
            orow = sb("orow", [128, 4, T], F32, c1)
            xblk = sb("xblk", [128, 2, NTILE, 128], F32, c1)
            hblk = sb("hblk", [128, 2, NTILE, 128], F32, c1)
            sq = sb("sq", [128, 2, NTILE], F32, c1)
            sqj = sb("sqj", [128, NTILE, 128], F32, c1)
            fst = sb("fst", [128, 6, NTILE], F32, c1)
        score = sb("score", [128, sum(keys_of(i) for i in TOPK_TILES)])
        m8 = sb("m8", [128, len(TOPK_TILES), 8])
        with ExitStack() as c1:
            kiw = sb("kiw", [128, NTILE, ID + IH], F32, c1)
            wsc = sb("wsc", [128, NTILE, IH], F32, c1)
            wcol = sb("wcol", [128, 1], F32, c1)
            qlast = sb("qlast", [128, 2, IH // 2, NSAMP], F32, c1)
            with ExitStack() as c2:
                rsc = sb("rsc", [128, PAST + 1], F32, c2)
                ikt = sb("ikt", [128, PAST + 1], F32, c2)
            khi = sb("khi", [128, L], F32R, c1)
            klo = sb("klo", [128, L], F32R, c1)
            with ExitStack() as c2:
                qst = sb("qst", [128, 2, IH // 2, 128], F32R, c2)
                qraw = sb("qraw", [128, IH // 2, 128], F32, c2)
                relub = sb("relub", [128, L], F32, c2)
            with ExitStack() as c2:
                qbd = sb("qbd", [128, 4, 128], F32, c2)
                iload = sb("iload", [128, 2, NPAGES, 2, ID], F32, c2)
        with ExitStack() as c1:
            psc = sb("psc", [128, POOLW // 128], F32, c1)
            psg = sb("psg", [128, 2], F32, c1)
            sst = sb("sst", [128, POOLW // 128, NSAMP], F32, c1)
            pw = sb("pw", [128, 2, GROUP], F32, c1)
            pu = sb("pu", [128, 2, T], F32, c1)
            pt = sb("pt", [128, 2, T], F32, c1)
            with ExitStack() as c2:
                pz = sb("pz", [128, 2, T], F32, c2)
            ulast = sb("ulast", [128, POOLW // 128, PAD + NSAMP], F32, c1)
            ulrow = sb("ulrow", [PAD + NSAMP, POOLW], F32, c1)
            strow = sb("strow", [NSAMP * PAD, POOLW], F32, c1)
        with ExitStack() as c1:
            spos = sb("spos", [128, L], F32, c1)
            dist01 = sb("dist01", [128, 3 * 128], F32, c1)
            zin = sb("zin", [128, 2, HEADS, 128], F32, c1)
            osb = sb("osb", [128, 2, 4, 128], F32, c1)
            knew = sb("knew", [128, KVH, NSAMP], F32, c1)
            qsamp = sb("qsamp", [128, HEADS, NSAMP], F32, c1)
            zsamp = sb("zsamp", [128, HEADS, NSAMP], F32, c1)
            ast = sb("ast", [128, 3, 2, 4], F32, c1)
            sst64 = sb("sst64", [64, 3], F32, c1)
            osamp = sb("osamp", [128, HEADS, NSAMP], F32, c1)
            vtail = sb("vtail", [128, KVH, T - 128 * (NTILE - 1)], F32, c1)
            with ExitStack() as c2:
                kin = sb("kin", [128, KVH, T], F32, c2)
            with ExitStack() as c2:
                vnew = sb("vnew", [1, NSAMP * KVH * HD], F32, c2)
        SOFF = {i: sum(keys_of(j) for j in TOPK_TILES if j < i) for i in TOPK_TILES}
        vin = wraw[:, 0:2, :, :].rearrange("p g k n -> p g (k n)")
        relua = wraw[:, 2:4, :, :].rearrange("p g k n -> p (g k n)")

        def score_of(i):
            return score[:, SOFF[i]:SOFF[i] + keys_of(i)]

        S = {}
        for name in ("cst_in", "g_in", "x_in0", "x_in1", "x_in2", "x_sq", "x_rms", "x_sqrt", "x_rstd", "x_scaled",
                     "x_turned", "a_hi", "a_lo", "w_in0", "w_in1", "w_in2", "w_in3", "w_hi", "w_lo", "w_used",
                     "evac", "stored0", "stored1", "small", "pages_in", "state_in", "ul_in", "ul_turned", "ul_kept", "ul_out", "st_summed", "st_kept", "psg_kept",
                     "p_in", "p_mixed", "p_mm", "p_scaled", "p_gated", "p_stored", "pool_step",
                     "spos_in", "kin_in", "vin_in", "aq_in0", "aq_in1", "az_in0", "az_in1",
                     "kvtok_kept0", "kvtok_kept1", "samp_kept", "kv_out", "kv_turned", "gated", "o_stored0", "o_stored1",
                     "pv_mm", "vnew_in", "sv_used", "ck_in0", "ck_in1", "cv_in0", "cv_in1", "cv0_in4",
                     "cv0_in5", "cv0_in6", "cv0_in7", "cv1_in4", "cv1_in5", "cv1_in6", "cv1_in7",
                     "sgated", "os_stored", "o_in0", "o_in1", "o_in2", "o_in3", "o_hi", "o_lo",
                     "xb_in0", "xb_in1", "h_added", "h_part", "h_turned", "h_squared", "sq_added", "h_stored0", "h_stored1",
                     "fg_in", *(f"fh_in{i}" for i in range(NTILE)), "f_rms", "f_sqrt", "f_done", "y_out",
                     "ak_hi", "ak_lo", "knew_kept", "aqk", "aq_hi", "aq_lo", "p_turned", "pt_copied", "amax", "aexp",
                     "abias", "normed", "dist_made", "dist_masked", "sk_turned", "sk_copied", "sqk", "smax", "sexp",
                     "sp_turned", "spt_copied", "qz_made", "sdist", "sbias_made", "snormed",
                     "kiw_turned", "kiw_out", "kiw_kept", "kiraw_in", "ki_hi", "ki_lo", "q_in", "q_hi", "q_lo", "q_used",
                     "logits", "relu_done", "scored", "score_init",
                     "ik0_in0", "ik0_in1", "ik1_in0", "ik1_in1", "ik_turned", "ik_copied", "ik_used", "qb_ready", "slogits", "srelu", "ssum", "ssum_kept",
                     "wcol_in", "ikn_in", "maxed", "taken", "outs"):
            S[name] = sem(name)
        block = top.enter_context(nc.Block())

        B_MAIN = 1 + NQI
        B_OUT = B_MAIN + NMAIN
        WIDTH0 = ID + IH

        def parity(n):
            return 1 - n % 2

        def uses(n):
            return (n + 1) // 2 if n % 2 else n // 2 + 1

        NX, NX1 = 5, 3

        def among(n):
            return B_MAIN <= n < B_MAIN + NX

        def pair(n):
            return 0 if among(n) else parity(n)

        def before(n):
            return max(m for m in range(n) if pair(m) == pair(n))

        def loads(n):
            return sum(pair(m) == pair(n) for m in range(n + 1))

        def load_half(q, n, s, src, width=128, add1=0, guard=True):
            p = pair(n)
            if guard:
                q.wait_ge(S["w_lo"], 2 * before(n) + s + 1 + 4 * add1)
            q.dma_start(wraw[:, 2 * p + s, :, 0:width],
                        src[s * HALF * 128:(s + 1) * HALF * 128, :].rearrange("(k p) n -> p k n", p=128)
                        ).then_inc(S[f"w_in{2 * p + s}"], 16)

        def load_block(q, n, src, width=128, i=None, guard=True):
            for s in range(2):
                load_half(q, n, s, src, width, 0 if i is None else i, guard)

        def split_hi(act, n, s, width=128, i=None, first=False):
            p = pair(n)
            add1, add4 = (0, 0) if i is None else (i, 4 * i)
            act.wait_ge(S[f"w_in{2 * p + s}"], 16 * loads(n) + 16 * add1)
            if not first:
                act.wait_ge(S["w_used"], 2 * n + s - 1 + add4)
            nc.scalar.activation(whi[:, s, :, 0:width], wraw[:, 2 * p + s, :, 0:width],
                                 ACT.Copy).then_inc(S["w_hi"], 1)

        def split_lo(dve, n, s, width=128, i=None):
            p = pair(n)
            add = 0 if i is None else 4 * i
            dve.wait_ge(S["w_hi"], 2 * n + s + 1 + add)
            nc.vector.tensor_tensor(wlo[:, s, :, 0:width], wraw[:, 2 * p + s, :, 0:width],
                                    whi[:, s, :, 0:width].bitcast(F32), ALU.subtract).then_inc(S["w_lo"], 1)

        def project(pe, n, width=128, i=None, first=False, src=None, first_out=False, between=None):
            add2, add4 = (0, 0) if i is None else (2 * i, 4 * i)
            if not first:
                pe.wait_ge(S["evac"], before(n) + 1 + add2)
            for s in range(2):
                pe.wait_ge(S["w_lo"], 2 * n + s + 1 + add4)
                if s and between:
                    between()
                for a in range(s * HALF, s * HALF + HALF):
                    if first_out:
                        pe.wait_ge(S["o_lo"], a + 1)
                    last = step(n, a, width, src or (ahi, alo))
                last.then_inc(S["w_used"], 1)

        def step(n, a, width=128, src=(ahi, alo)):
            s, k = divmod(a, HALF)
            mhi, mlo = src
            for w, parts in ((whi, (mhi, mlo)), (wlo, (mhi,))):
                for m in parts:
                    for c, (t0, tn) in enumerate(CHUNKS):
                        last = nc.tensor.matmul(ps[0:width, 3 * pair(n) + c, 0:tn], w[:, s, k, 0:width],
                                                m[:, a, t0:t0 + tn],
                                                start=(a == 0 and w is whi and m is mhi),
                                                stop=(a == KT - 1 and w is wlo))
            return last

        IUNITS = [(i, h, k) for i in TOPK_TILES for h in range(2) for k in range(IH // 2)]
        QUNITS = [(i, h) for i in TOPK_TILES for h in range(2)]

        def steps_of(first, count):
            return [("step", n, a) for n in range(first, first + count) for a in range(KT)]

        def indexer_order():
            steps = steps_of(B_MAIN, NX1)
            order, early = steps[:HALF], steps[HALF:]
            done = 0
            for u in range(len(IUNITS)):
                order.append(("head", u))
                until = len(early) * (u + 1) // len(IUNITS)
                order += early[done:until]
                done = until
            return order

        def samples_order():
            steps = steps_of(B_MAIN + NX1, NX - NX1)
            order, done = [], 0
            for count, what in ((8, ("turn", 0)), (2, ("logit", 0)), (3, ("turn", 1)), (2, ("logit", 1)),
                                (3, ("turn", 2)), (2, ("logit", 2)), (3, ("turn", 3)), (2, ("logit", 3)),
                                (4, ("sum", 0))):
                order += steps[done:done + count] + [what]
                done += count
            return order + steps[done:]

        def weights_at(n, a):
            return {HALF - 1: 0, KT - 1: 1}.get(a)

        def step_among(pe, n, a):
            if a == 0:
                pe.wait_ge(S["evac"], before(n) + 1)
            if a % HALF == 0:
                pe.wait_ge(S["w_lo"], 2 * n + a // HALF + 1)
            last = step(n, a)
            if a % HALF == HALF - 1:
                last.then_inc(S["w_used"], 1)

        def step_act(act, n, a):
            s = weights_at(n, a)
            if s == 0:
                split_hi(act, n + 1, 0)
            if s == 1:
                evacuate(act, n)
                split_hi(act, n + 1, 1)
                store_block(act, n, proj[128 * (n - B_MAIN):128 * (n - B_MAIN) + 128, :])

        def step_dve(dve, n, a):
            if weights_at(n, a) is not None:
                split_lo(dve, n + 1, weights_at(n, a))

        def logit_column(u, w):
            return 1536 if u % 2 == 0 else 3072 - (w - 2 * BANK if w > 2 * BANK else 0)

        def relu_of(u):
            return relua if u % 2 == 0 else relub

        def load_index_keys(q, j, half):
            if j < 2:
                q.wait_ge(S["qb_ready"], 8)
            else:
                q.wait_ge(S["ik_turned"], j - 1)
            first = half * NPAGES // 2
            for b in range(2):
                for k, page in enumerate(page_ids(q, 2 * j + b, first, NPAGES // 2)):
                    q.dma_start(iload[:, j % 2, first + k, b, :], cik[0, bass.ds(page, 1), :, :].rearrange("o s d -> (o s) d")
                                ).then_inc(S[f"ik{half}_in{j % 2}"], 16)

        def key_slot(b):
            return wslot[:, b, :, :] if b < 4 else slot[:, b - 4, :, :]

        def value_slot(b):
            return vslot[:, b, :, :] if b < 3 else vslot3[:, :, :] if b == 3 else slot[:, b - 4, :, :]

        def load_pages(q, src, dst, b, half, arrived):
            first = half * NPAGES // 2
            for k, page in enumerate(page_ids(q, b, first, NPAGES // 2)):
                q.dma_start(dst[:, first + k, :], src[0, bass.ds(page, 1), :, :, :].rearrange("o s d e -> (o s) (d e)")
                            ).then_inc(S[arrived], 16)

        def load_keys(q, b, half):
            load_pages(q, ck, key_slot(b), b, half, f"ck_in{half}")

        def load_values(q, b, half):
            if b >= 4:
                q.wait_ge(S["sk_turned"], KVH * (b + 1))
            load_pages(q, cv, value_slot(b), b, half, f"cv_in{half}" if b < 4 else f"cv{half}_in{b}")

        def quarter(i, r):
            nb = i + 1
            return range(r * nb // 4, (r + 1) * nb // 4)

        def evacuate(act, n, width=128, i=None, func=None, first=False, stored=True):
            p = parity(n)
            add1, add4 = (0, 0) if i is None else (i, 4 * i)
            act.wait_ge(S["w_used"], 2 * n + 2 + add4)
            if not first and stored:
                act.wait_ge(S[f"stored{p}"], 16 * (uses(n) - 1) + 16 * add1)
            f = func or ACT.Copy
            b = 3 * pair(n)
            nc.scalar.activation(stage[0:width, p, 0:700].rearrange("p (c t) -> p c t", c=2),
                                 ps[0:width, b:b + 2, 0:350], f)
            nc.scalar.activation(stage[0:width, p, 700:T], ps[0:width, b + 2, 0:T - 700],
                                 f).then_inc(S["evac"], 1)

        def store_block(act, n, dst, width=128, i=None):
            p = parity(n)
            add2 = 0 if i is None else 2 * i
            act.wait_ge(S["evac"], n + 1 + add2)
            act.dma_start(dst, stage[0:width, p, :]).then_inc(S[f"stored{p}"], 16)

        ATILES = [NTILE - 1] + list(range(NTILE - 1))
        AUNITS = [(i, g) for i in ATILES for g in range(KVH)]
        NHEAD = 4 * len(AUNITS)
        LAG = 5

        def back_blocks(k):
            if k < LAG or k >= NHEAD + LAG:
                return []
            v, r = divmod(k - LAG, 4)
            return [(v, j) for j in quarter(AUNITS[v][0], r)]

        def qbuf(u):
            return (u // KVH) % 2

        def score_bank(k, w):
            return 0 if k % 2 == 0 else 1536 - (w - 2 * BANK if w > 2 * BANK else 0)

        def out_bank(u):
            return 7 if u % 2 == 0 else 2

        def blocks_to(u):
            return sum(i + 1 for i, _ in AUNITS[:u])

        def dist_of(i):
            if i in SOFF:
                return score_of(i)
            return dist01[:, 128 * (i * (i + 1) // 2):128 * (i * (i + 1) // 2) + keys_of(i)]

        def page_ids(q, b, first=0, count=NPAGES):
            at = b * NPAGES + first
            _, ids = nc.values_load_multi_w_load_instructions(
                pages[0:1, at:at + count], engines=[q.engine], min_val=0, max_val=NPHYS - 1)
            return ids

        @block.sync
        def _(sp):
            sp.dma_start(cst[:, :], consts[:, 0:K_S]).then_inc(S["cst_in"], 16)
            sp.dma_start(pages[:, :], ptab.rearrange("(o b) k -> o (b k)", o=1)).then_inc(S["pages_in"], 16)
            for i in range(NTILE):
                if i >= 3:
                    sp.wait_ge(S["x_turned"], 4 * (i - 2))
                for r0, n, src in x_parts(i):
                    sp.dma_start(xt[r0:r0 + n, i % 3, :], src).then_inc(S[f"x_in{i % 3}"], 16)
                if i == 0:
                    sp.dma_start(gb[:, :], norm_g[0, :].partition_broadcast(128)).then_inc(S["g_in"], 16)
                if i == 2:
                    load_block(sp, 0, w_in[0, :, C_KI:DIN], WIDTH0, guard=False)
            load_block(sp, 1, w_in[0, :, C_QI:C_QI + 128], guard=False)
            sp.wait_ge(S["w_lo"], 1)
            load_block(sp, 2, w_in[0, :, C_QI + 128:C_QI + 256])
            sp.wait_ge(S["kiw_kept"], 1)
            new_ik_p, new_ik_s = io["new_idx_k_prompt"], io["new_idx_k_sample"]
            full = 128 * (NTILE - 1)
            sp.dma_start(new_ik_p[0, 0, 0:full, :].rearrange("(t p) d -> p t d", p=128),
                         kiw[:, 0:NTILE - 1, 0:ID]).then_inc(S["outs"], 16)
            sp.dma_start(new_ik_p[0, 0, full:L, :], kiw[0:TAIL, NTILE - 1, 0:ID]).then_inc(S["outs"], 16)
            sp.dma_start(new_ik_s[0, :, 0, :], kiw[TAIL:TAIL + NSAMP, NTILE - 1, 0:ID]).then_inc(S["outs"], 16)
            with sp.Fori(0, NQI // 2 - 1) as i:
                load_block(sp, 3, w_in[0, :, bass.ds(i * 256 + C_QI + 256, 128)], i=i)
                load_block(sp, 4, w_in[0, :, bass.ds(i * 256 + C_QI + 384, 128)], i=i)
            load_block(sp, B_MAIN, w_in[0, :, 0:128])
            sp.wait_ge(S["stored1"], 16 * uses(NQI))
            sp.wait_ge(S["stored0"], 16 * uses(NQI - 1))
            for r in range(2):
                sp.dma_start(relub[64 * r:64 * r + 64, :], proj[C_KI:C_WI, 0:L]).then_inc(S["kiraw_in"], 16)

            def load_query(n):
                i, h = QUNITS[n]
                if n:
                    sp.wait_ge(S["q_lo"], n)
                cols = cols_of(i)
                for r in range(2):
                    sp.dma_start(qraw[64 * r:64 * r + 64, :, 0:cols],
                                 proj[C_QI + 512 * h:C_QI + 512 * h + 512, 128 * i:128 * i + cols]
                                 .rearrange("(h d) t -> d h t", d=64)).then_inc(S["q_in"], 16)

            def load_main_half(n, s):
                c = 128 * (n - B_MAIN)
                load_half(sp, n, s, w_in[0, :, c:c + 128])

            load_query(0)
            load_main_half(B_MAIN + 1, 0)
            load_main_half(B_MAIN + 1, 1)
            for what, *x in indexer_order():
                if what == "head" and x[0] % (IH // 2) == 0 and x[0] // (IH // 2) + 1 < len(QUNITS):
                    load_query(x[0] // (IH // 2) + 1)
                if what == "step" and weights_at(*x) is not None and x[0] + 2 < B_MAIN + NX:
                    load_main_half(x[0] + 2, weights_at(*x))
            with nc.allow_non_contiguous_dma(reason="128 single weights"):
                for b in range(NSAMP):
                    sp.dma_start(wcol[16 * b:16 * b + 16, :], proj[C_WI:DIN, L + b:L + b + 1]).then_inc(S["wcol_in"], 16)

            def load_new_keys(j):
                if j:
                    sp.wait_ge(S["slogits"], j)
                with nc.allow_non_contiguous_dma(reason="one new key"):
                    for b in range(2):
                        sp.dma_start(ikt[64 * b:64 * b + 64, PAST:PAST + 1],
                                     proj[C_KI:C_WI, L + 2 * j + b:L + 2 * j + b + 1]).then_inc(S["ikn_in"], 16)

            sp.wait_ge(S["pages_in"], 16)
            load_index_keys(sp, 0, 0)
            load_new_keys(0)
            load_index_keys(sp, 1, 0)
            for s in range(2):
                load_main_half(B_MAIN + NX, s)
            load_index_keys(sp, 2, 0)
            load_new_keys(1)
            load_index_keys(sp, 3, 0)
            load_new_keys(2)
            load_new_keys(3)
            for s in range(2):
                load_main_half(B_MAIN + NX + 1, s)
            sp.wait_ge(S["srelu"], 1)
            sp.wait_ge(S["ssum"], 1)
            with nc.allow_non_contiguous_dma(reason="one scale a channel"):
                sp.dma_start(psc[:, :], pscale[0, :].rearrange("(c p) -> p c", p=128)).then_inc(S["state_in"], 16)
            sp.dma_start(strow[:, :], state[0].rearrange("b r c -> (b r) c")).then_inc(S["state_in"], 16)
            for b in range(NSAMP):
                sp.dma_start(io["new_pool_sample"][0, b, 0:PAD - 1, :], state[0, b, 1:PAD, :]).then_inc(S["outs"], 16)
            for s in range(2):
                load_main_half(B_MAIN + NX + 2, s)
            first = B_MAIN + NX + 3
            with sp.Fori(0, (B_OUT - first) // 2) as i:
                for n in (first, first + 1):
                    load_block(sp, n, w_in[0, :, bass.ds(i * 256 + 128 * (n - B_MAIN), 128)], i=i)
            sp.wait_ge(S["p_stored"], 16 * 4)
            sp.dma_start(spos[:, :], consts[:, K_S:K_ALL]).then_inc(S["spos_in"], 16)
            sp.dma_start(kin[:, :, :], proj[C_K:C_V, :].rearrange("(b p) t -> p b t", p=128)).then_inc(S["kin_in"], 16)
            sp.wait_ge(S["w_lo"], 2 * (B_OUT - 1))
            last = 128 * (NTILE - 1)
            sp.dma_start(vin[:, :, :], proj[C_V:C_ZA, 0:last].rearrange("(b p) t -> p b t", p=128)).then_inc(S["vin_in"], 16)
            sp.dma_start(vtail[:, :, :], proj[C_V:C_ZA, last:T].rearrange("(b p) t -> p b t", p=128)
                         ).then_inc(S["vin_in"], 16)
            sp.wait_ge(S["w_used"], 2 * B_OUT)

            def load_q(s):
                i = ATILES[s]
                c = cols_of(i)
                if s >= 2:
                    sp.wait_ge(S["aq_lo"], s - 1)
                sp.dma_start(qin[:, s % 2, :, 0:c], proj[C_Q:C_K, 128 * i:128 * i + c].rearrange("(h p) t -> p h t", p=128)
                             ).then_inc(S[f"aq_in{s % 2}"], 16)

            def load_z(s):
                i = ATILES[s]
                c = cols_of(i)
                sp.dma_start(zin[:, s % 2, :, 0:c], proj[C_ZA:C_QI, 128 * i:128 * i + c].rearrange("(h p) t -> p h t", p=128)
                             ).then_inc(S[f"az_in{s % 2}"], 16)

            load_q(0)
            load_q(1)
            for n in (B_OUT - 2, B_OUT - 1):
                sp.wait_ge(S[f"stored{parity(n)}"], 16 * uses(n))
            load_z(0)
            load_z(1)
            sp.wait_ge(S["kvtok_kept0"], (NTILE + 1) // 2)
            sp.wait_ge(S["kvtok_kept1"], NTILE // 2)
            for kv, name in ((0, "k"), (1, "v")):
                cols = slice(kv * KVH * HD, (kv + 1) * KVH * HD)
                sp.dma_start(io[f"new_{name}_prompt"][0, 0, 0:full].rearrange("(t p) g d -> p t (g d)", p=128),
                             kvtok[:, 0:NTILE - 1, cols]).then_inc(S["kv_out"], 16)
                sp.dma_start(io[f"new_{name}_prompt"][0, 0, full:L].rearrange("t g d -> t (g d)"),
                             kvtok[0:TAIL, NTILE - 1, cols]).then_inc(S["kv_out"], 16)
                sp.dma_start(io[f"new_{name}_sample"][0, :, 0].rearrange("b g d -> b (g d)"),
                             kvtok[TAIL:TAIL + NSAMP, NTILE - 1, cols]).then_inc(S["kv_out"], 16)
            sp.wait_ge(S["ak_lo"], 1)
            sp.wait_ge(S["knew_kept"], 1)
            sp.dma_start(vnew[0:1, :].rearrange("o (b c) -> o b c", b=NSAMP),
                         kvtok[TAIL:TAIL + NSAMP, NTILE - 1, KVH * HD:2 * KVH * HD]).then_inc(S["vnew_in"], 16)
            load_q(2)
            for u, (i, g) in enumerate(AUNITS):
                sp.wait_ge(S["gated"], u + 1)
                r = rows_of(i)
                sp.dma_start(mixt[POOLW + 512 * g:POOLW + 512 * g + 512, 128 * i:128 * i + r]
                             .rearrange("(h p) t -> p h t", p=128),
                             osb[:, u % 2, :, 0:r]).then_inc(S[f"o_stored{u % 2}"], 16)
                if g == 0 and u // KVH + 3 < NTILE:
                    load_q(u // KVH + 3)
                if g == KVH - 1 and u // KVH + 2 < NTILE:
                    load_z(u // KVH + 2)
                if 2 <= u < 2 + NSAMP:
                    load_keys(sp, u - 2, 0)
                if u == len(AUNITS) - 2:
                    sp.wait_ge(S["p_turned"], blocks_to(len(AUNITS)))
                    for b in range(4):
                        load_values(sp, b, 0)
            for k in range(4):
                sp.dma_start(orow[:, k, :], mixt[128 * k:128 * k + 128, :]).then_inc(S[f"o_in{k}"], 16)
            load_values(sp, 4, 0)
            load_values(sp, 5, 0)
            load_block(sp, B_OUT, w_out[0, :, 0:128])
            load_block(sp, B_OUT + 1, w_out[0, :, 128:256])
            load_values(sp, 6, 0)
            load_values(sp, 7, 0)
            for k in range(4, KT):
                if k == POOLW // 128:
                    with nc.allow_non_contiguous_dma(reason="32-byte rows"):
                        sp.wait_ge(S["sgated"], 1)
                        sp.dma_start(mixt[POOLW:D, L:T].rearrange("(h p) t -> p h t", p=128), osamp[:, :, :]
                                     ).then_inc(S["os_stored"], 16)
                    sp.wait_ge(S["os_stored"], 16)
                    for p in range(2):
                        sp.wait_ge(S[f"o_stored{p}"], 16 * len(AUNITS[p::2]))
                sp.wait_ge(S["o_lo"], k - 3)
                sp.dma_start(orow[:, k % 4, :], mixt[128 * k:128 * k + 128, :]).then_inc(S[f"o_in{k % 4}"], 16)

            def load_x(n, c0, i=None):
                p = parity(n)
                add2 = 0 if i is None else 2 * i
                if n >= B_OUT + 2:
                    sp.wait_ge(S["h_added"], n - B_OUT - 1 + add2)
                x = xblk[:, p, :, :]
                s_ = S[f"xb_in{p}"]
                c = c0
                lo = 128 - META
                sp.dma_start(x[0:META, 0, :], meta[:, c]).then_inc(s_, 16)
                sp.dma_start(x[META:128, 0, :], xp[0, 0:lo, c]).then_inc(s_, 16)
                sp.dma_start(x[:, 1:NTILE - 1, :],
                             xp[0, lo:lo + 128 * (NTILE - 2), c].rearrange("(t p) d -> p t d", p=128)).then_inc(s_, 16)
                sp.dma_start(x[0:TAIL, NTILE - 1, :], xp[0, SEQ - TAIL:SEQ, c]).then_inc(s_, 16)
                sp.dma_start(x[TAIL:TAIL + NSAMP, NTILE - 1, :], xs_[:, 0, c]).then_inc(s_, 16)

            load_x(B_OUT, slice(0, 128))
            load_x(B_OUT + 1, slice(128, 256))
            with sp.Fori(0, NOUT // 2 - 1) as i:
                for r in range(2):
                    c = bass.ds(i * 256 + 256 + 128 * r, 128)
                    load_block(sp, B_OUT + 2 + r, w_out[0, :, c], i=i)
                    load_x(B_OUT + 2 + r, c, i=i)
            sp.wait_ge(S["w_used"], 2 * (B_OUT + NOUT))
            sp.dma_start(fg[:, :], fin_g.partition_broadcast(128)).then_inc(S["fg_in"], 16)
            for p in range(2):
                sp.wait_ge(S[f"h_stored{p}"], 32 * NOUT // 2)
            for i in range(NTILE):
                n = cols_of(i)
                sp.dma_start(fh[0:n, i, :], hbuf_d[128 * i:128 * i + n, :]).then_inc(S[f"fh_in{i}"], 16)

        @block.scalar
        def _(act):
            def turned_hi(i):
                for q in range(4):
                    act.wait_ge(S["x_turned"], 4 * i + q + 1)
                    c = cols_of(i)
                    nc.scalar.activation(ahi[:, 4 * q:4 * q + 4, 128 * i:128 * i + c],
                                         ps[:, q, :].rearrange("p (k t) -> p k t", k=4)[:, :, 0:c],
                                         ACT.Copy).then_inc(S["a_hi"], 1)

            for i in range(NTILE):
                n = cols_of(i)
                act.wait_ge(S[f"x_in{i % 3}"], 16 * sum(X_PARTS[i % 3:i + 1:3]))
                if i:
                    act.wait_ge(S["x_sqrt"], i)
                nc.scalar.activation(psf[0:n, 2048:4096], xt[0:n, i % 3, :], ACT.Square,
                                     accum_out=nst[0:n, 0, i:i + 1]).then_inc(S["x_sq"], 1)
                act.wait_ge(S["x_rms"], i + 1)
                nc.scalar.activation(nst[0:n, 3, i:i + 1], nst[0:n, 2, i:i + 1], ACT.Sqrt).then_inc(S["x_sqrt"], 1)
                if i:
                    turned_hi(i - 1)
            turned_hi(NTILE - 1)

            split_hi(act, 0, 0, WIDTH0, first=True)
            split_hi(act, 0, 1, WIDTH0, first=True)
            split_hi(act, 1, 0)
            evacuate(act, 0, WIDTH0, first=True)
            store_block(act, 0, proj[C_KI:DIN, :], WIDTH0)
            split_hi(act, 1, 1)

            def query_block(n, dst, i=None, first=False):
                split_hi(act, n + 1, 0, i=i)
                evacuate(act, n, i=i, first=first)
                store_block(act, n, dst, i=i)
                split_hi(act, n + 1, 1, i=i)

            query_block(1, proj[C_QI:C_QI + 128, :], first=True)
            query_block(2, proj[C_QI + 128:C_QI + 256, :])
            with act.Fori(0, NQI // 2 - 1) as i:
                for n in (3, 4):
                    query_block(n, proj[bass.ds(i * 256 + C_QI + 128 * (n - 1), 128), :], i=i)
            act.wait_ge(S["kiraw_in"], 32)
            nc.scalar.activation(khi[:, :], relub[:, :], ACT.Copy).then_inc(S["ki_hi"], 1)

            def query_hi(n):
                i = QUNITS[n][0]
                act.wait_ge(S["q_in"], 32 * (n + 1))
                if n >= 2:
                    act.wait_ge(S["logits"], 8 * (n - 1))
                c = cols_of(i)
                nc.scalar.activation(qst[:, n % 2, :, 0:c], qraw[:, :, 0:c], ACT.Copy).then_inc(S["q_hi"], 1)

            query_hi(0)
            act.wait_ge(S["ki_lo"], 1)
            for what, *x in indexer_order():
                if what == "step":
                    step_act(act, *x)
                    continue
                u = x[0]
                i = IUNITS[u][0]
                n, k = divmod(u, IH // 2)
                if k == 0 and n + 1 < len(QUNITS):
                    query_hi(n + 1)
                rows, w = rows_of(i), keys_of(i)
                act.wait_ge(S["logits"], u + 1)
                if u >= 2:
                    act.wait_ge(S["scored"], u - 1)
                o = logit_column(u, w)
                nc.scalar.activation(relu_of(u)[0:rows, 0:w], psf[0:rows, o:o + w], ACT.Relu).then_inc(S["relu_done"], 1)
            for what, *x in samples_order():
                if what == "step":
                    step_act(act, *x)
                if what == "turn":
                    j = x[0]
                    act.wait_ge(S["ik_turned"], j + 1)
                    if j:
                        act.wait_ge(S["slogits"], j)
                    nc.scalar.activation(ikt[:, 0:PAST], psf[:, 3072:3072 + PAST], ACT.Copy).then_inc(S["ik_copied"], 1)
            B_GRP = B_MAIN + 2 * (POOLW // 128)
            B_ZP = B_MAIN + POOLW // 128
            for n in range(B_MAIN + NX, B_ZP):
                split_hi(act, n + 1, 0)
                evacuate(act, n)
                store_block(act, n, proj[128 * (n - B_MAIN):128 * (n - B_MAIN) + 128, :])
                split_hi(act, n + 1, 1)
            with act.Fori(0, (B_GRP - B_ZP) // 2) as i:
                for n in (B_ZP, B_ZP + 1):
                    split_hi(act, n + 1, 0, i=i)
                    evacuate(act, n, i=i, func=ACT.Silu)
                    store_block(act, n, proj[bass.ds(i * 256 + 128 * (n - B_MAIN), 128), :], i=i)
                    split_hi(act, n + 1, 1, i=i)
            act.wait_ge(S["stored0"], 16 * uses(B_MAIN + POOLW // 128 - 2))
            act.wait_ge(S["stored1"], 16 * uses(B_MAIN + POOLW // 128 - 1))
            act.dma_start(ulast[:, :, :], proj[C_U:C_ZP, L - PAD:T].rearrange("(c p) t -> p c t", p=128)
                          ).then_inc(S["ul_in"], 16)
            act.wait_ge(S["ul_turned"], 1)
            nc.scalar.activation(ulrow[:, :], psf[0:PAD + NSAMP, 3072:4096], ACT.Copy).then_inc(S["ul_kept"], 1)
            act.wait_ge(S["st_summed"], 1)
            nc.scalar.activation(sst[:, :, :], psf[:, 3072:3072 + 64].rearrange("p (c b) -> p c b", b=NSAMP),
                                 ACT.Copy).then_inc(S["st_kept"], 1)
            act.wait_ge(S["ul_kept"], 1)
            act.dma_start(io["new_pool_prompt"][0, 0, :, :], ulrow[0:PAD, :]).then_inc(S["ul_out"], 16)
            act.dma_start(io["new_pool_sample"][0, :, PAD - 1, :], ulrow[PAD:PAD + NSAMP, :]).then_inc(S["ul_out"], 16)

            def pool_group(g, i2, func, first=False):
                for q in range(4):
                    n = B_GRP + q
                    split_hi(act, n + 1, 0, i=i2)
                    evacuate(act, n, i=i2, func=func)
                    store_block(act, n, proj[bass.ds(g * 512 + 2 * POOLW + 128 * q, 128), :], i=i2)
                    split_hi(act, n + 1, 1, i=i2)
                    if q == 0:
                        if not first:
                            act.wait_ge(S["p_gated"], g)
                            act.wait_ge(S["p_stored"], g * 16)
                        act.wait_ge(S["ul_out"], 32)
                        nc.scalar.activation(psg[:, :], psc[:, bass.ds(g * 2, 2)], ACT.Copy).then_inc(S["psg_kept"], 1)
                        act.dma_start(pu[:, :, :], proj[bass.ds(g * GROUP, GROUP), :].rearrange("(c p) t -> p c t", p=128)
                                      ).then_inc(S["p_in"], 16)
                        act.dma_start(pz[:, :, :], proj[bass.ds(g * GROUP + C_ZP, GROUP), :]
                                      .rearrange("(c p) t -> p c t", p=128)).then_inc(S["p_in"], 16)
                        act.dma_start(pw[:, :, :], w_pool[0, bass.ds(g, 1), :, :].rearrange("o (c p) d -> p (o c) d", p=128)
                                      ).then_inc(S["p_in"], 16)
                act.wait_ge(S["psg_kept"], g + 1)
                for x in range(6):
                    m, c = divmod(x, 3)
                    t0, tn = CHUNKS[c]
                    act.wait_ge(S["p_mm"], g * 6 + x + 1)
                    nc.scalar.activation(pt[:, m, t0:t0 + tn], ps[:, 6 + x % 2, 0:tn], ACT.Identity,
                                         scale=psg[:, m:m + 1]).then_inc(S["p_scaled"], 1)

            groups = POOLW // GROUP
            pool_group(0, 0, ACT.Copy, first=True)
            with act.Fori(1, groups - 1) as g:
                pool_group(g, g * 2, ACT.Copy)
            for q in range(4):
                n = B_GRP + 4 * (groups - 1) + q
                split_hi(act, n + 1, 0)
                evacuate(act, n, func=ACT.Silu)
                r0 = (n - B_MAIN) * 128
                store_block(act, n, proj[r0:r0 + 128, :])
                split_hi(act, n + 1, 1)
                if q == 0:
                    g = groups - 1
                    act.wait_ge(S["p_gated"], g)
                    act.wait_ge(S["p_stored"], g * 16)
                    act.dma_start(pu[:, :, :], proj[g * GROUP:(g + 1) * GROUP, :].rearrange("(c p) t -> p c t", p=128)
                                  ).then_inc(S["p_in"], 16)
                    act.dma_start(pz[:, :, :], proj[C_ZP + g * GROUP:C_ZP + (g + 1) * GROUP, :]
                                  .rearrange("(c p) t -> p c t", p=128)).then_inc(S["p_in"], 16)
                    act.dma_start(pw[:, :, :], w_pool[0, g, :, :].rearrange("(c p) d -> p c d", p=128)
                                  ).then_inc(S["p_in"], 16)
            for x in range(6):
                m, c = divmod(x, 3)
                t0, tn = CHUNKS[c]
                act.wait_ge(S["p_mm"], g * 6 + x + 1)
                nc.scalar.activation(pt[:, m, t0:t0 + tn], ps[:, 6 + x % 2, 0:tn], ACT.Identity,
                                     scale=psc[:, g * 2 + m:g * 2 + m + 1]).then_inc(S["p_scaled"], 1)
            for n in range(B_GRP + 4 * groups, B_OUT):
                if n + 1 < B_OUT:
                    split_hi(act, n + 1, 0)
                evacuate(act, n, func=ACT.Silu)
                r0 = (n - B_MAIN) * 128
                store_block(act, n, proj[r0:r0 + 128, :])
                if n + 1 < B_OUT:
                    split_hi(act, n + 1, 1)

            act.wait_ge(S["kin_in"], 16)
            act.wait_ge(S["w_used"], 2 * B_OUT)
            nc.scalar.activation(akh[:, :, :], kin[:, :, 0:L], ACT.Copy).then_inc(S["ak_hi"], 1)

            def query_parts(s):
                act.wait_ge(S[f"aq_in{s % 2}"], 16 * (s // 2 + 1))
                if s >= 2:
                    act.wait_ge(S["aqk"], 8 * (s - 1))
                c = cols_of(ATILES[s])
                nc.scalar.activation(qh[:, s % 2, :, 0:c], qin[:, s % 2, :, 0:c], ACT.Copy,
                                     scale=HD ** -0.5).then_inc(S["aq_hi"], 1)

            query_parts(0)
            nc.scalar.activation(knew[:, :, :], kin[:, :, L:T], ACT.Copy).then_inc(S["knew_kept"], 1)
            for i in range(0, NTILE, 2):
                n = cols_of(i)
                act.wait_ge(S["kv_turned"], i + 1)
                nc.scalar.activation(kvtok[0:n, i, :], ps[0:n, i % 6, :], ACT.Copy).then_inc(S["kvtok_kept0"], 1)
            t = 0
            for k in range(NHEAD + LAG):
                for v, j in back_blocks(k):
                    i = AUNITS[v][0]
                    act.wait_ge(S["p_turned"], t + 1)
                    if t >= 2:
                        act.wait_ge(S["pv_mm"], t - 1)
                    kn = min(128, L - 128 * j)
                    w = 4 * rows_of(i)
                    nc.scalar.activation(pts[0:kn, t % 2, 0:w], ps[0:kn, 5 + t % 2, 0:w], ACT.Copy
                                         ).then_inc(S["pt_copied"], 1)
                    t += 1
                if k < NHEAD:
                    u, r = divmod(k, 4)
                    i, g = AUNITS[u]
                    n, w = rows_of(i), keys_of(i)
                    act.wait_ge(S["amax"], k + 1)
                    x = prob[0:n, u % 2, r, 0:w]
                    nc.scalar.activation(x, x, ACT.Exp, bias=ast[0:n, 0, u % 2, r:r + 1],
                                         accum_out=ast[0:n, 1, u % 2, r:r + 1]).then_inc(S["aexp"], 1)
                    if g == KVH - 1 and r == 1 and u // KVH + 1 < NTILE:
                        query_parts(u // KVH + 1)

            def operand_hi(k):
                act.wait_ge(S[f"o_in{k % 4}"], 16 * (k // 4 + 1))
                nc.scalar.activation(ohi[:, k, :], orow[:, k % 4, :], ACT.Copy).then_inc(S["o_hi"], 1)

            for m in range(NSAMP * KVH):
                b, g = divmod(m, KVH)
                act.wait_ge(S["sk_turned"], m + 1)
                if m == 0:
                    act.wait_ge(S["p_turned"], blocks_to(len(AUNITS)))
                if m >= 2:
                    act.wait_ge(S["sqk"], m - 1)
                nc.scalar.activation(skt[:, m % 2, :], psf[:, 2048 + 1024 * (m % 2):3072 + 1024 * (m % 2)],
                                     ACT.Copy).then_inc(S["sk_copied"], 1)
                if m == 8:
                    act.wait_ge(S["kv_out"], 16 * 6)
                    act.wait_ge(S["vnew_in"], 16)
                if m in (8, 10, 12, 14):
                    operand_hi((m - 8) // 2)
            act.wait_ge(S["smax"], 1)
            nc.scalar.activation(sprob[:, :], sprob[:, :], ACT.Exp, bias=sst64[:, 0:1],
                                 accum_out=sst64[:, 1:2]).then_inc(S["sexp"], 1)
            for s in range(2):
                split_hi(act, B_OUT, s)
            act.wait_ge(S["sp_turned"], 1)
            nc.scalar.activation(spt[:, 0:NPAGES, :], ps[:, 3, :].rearrange("p (j r) -> p j r", r=64), ACT.Copy)
            nc.scalar.activation(spt[0:1, NPAGES, :], ps[0:1, 4, 0:64], ACT.Copy).then_inc(S["spt_copied"], 1)
            act.wait_ge(S["sv_used"], NSAMP)
            for k in range(4, KT):
                operand_hi(k)

            def squares(n, i=None):
                p = parity(n)
                add2 = 0 if i is None else 2 * i
                act.wait_ge(S["h_added"], n - B_OUT + 1 + add2)
                if n > B_OUT:
                    act.wait_ge(S["h_squared"], n - B_OUT + add2)
                for t in range(NTILE):
                    c = cols_of(t)
                    last = nc.scalar.activation(sqj[0:c, t, :], hblk[0:c, p, t, :], ACT.Square,
                                                accum_out=sq[0:c, p, t:t + 1])
                last.then_inc(S["h_squared"], 1)

            def store_h(n, c, i=None):
                p = parity(n)
                full = NTILE - 1
                act.dma_start(hbuf_d[0:128 * full, c].rearrange("(t p) d -> p t d", p=128),
                              hblk[:, p, 0:full, :]).then_inc(S[f"h_stored{p}"], 16)
                act.dma_start(hbuf_d[128 * full:T, c], hblk[0:T - 128 * full, p, full, :]
                              ).then_inc(S[f"h_stored{p}"], 16)

            def out_block(n, i=None, c=None):
                split_hi(act, n + 1, 0, i=i)
                evacuate(act, n, i=i, stored=False)
                split_hi(act, n + 1, 1, i=i)
                if c is not None:
                    squares(n - 1, i)
                    store_h(n - 1, c, i)

            out_block(B_OUT)
            out_block(B_OUT + 1, c=slice(0, 128))
            with act.Fori(0, NOUT // 2 - 2) as i:
                out_block(B_OUT + 2, i, bass.ds(i * 256 + 128, 128))
                out_block(B_OUT + 3, i, bass.ds(i * 256 + 256, 128))
            out_block(B_OUT + NOUT - 2, c=slice(D - 384, D - 256))
            n = B_OUT + NOUT - 1
            evacuate(act, n, stored=False)
            squares(n - 1)
            store_h(n - 1, slice(D - 256, D - 128))
            squares(n)
            store_h(n, slice(D - 128, D))
            act.wait_ge(S["f_rms"], 1)
            nc.scalar.activation(fst[:, 3, :], fst[:, 2, :], ACT.Sqrt).then_inc(S["f_sqrt"], 1)
            for i in range(NTILE):
                act.wait_ge(S["f_done"], i + 1)
                for r0, n, _ in x_parts(i):
                    if i == 0 and r0 == 0:
                        continue
                    if i == NTILE - 1 and r0:
                        dst = io["y_sample"][:, 0, :]
                    else:
                        lo = 128 * i - META + r0
                        dst = io["y_prompt"][0, lo:lo + n, :]
                    act.dma_start(dst, fh[r0:r0 + n, i, :]).then_inc(S["y_out"], 16)
            act.wait_ge(S["y_out"], 16 * (NTILE + 1))
            act.wait_ge(S["outs"], 16 * (3 + NSAMP))

        @block.vector
        def _(dve):
            tick = [0]

            def chain(ins):
                tick[0] += 1
                ins.then_inc(S["small"], 1)
                dve.wait_ge(S["small"], tick[0])

            dve.wait_ge(S["cst_in"], 16)

            def turned_lo(i):
                for q in range(4):
                    dve.wait_ge(S["a_hi"], 4 * i + q + 1)
                    c = cols_of(i)
                    out = slice(128 * i, 128 * i + c)
                    nc.vector.tensor_tensor(alo[:, 4 * q:4 * q + 4, out],
                                            ps[:, q, :].rearrange("p (k t) -> p k t", k=4)[:, :, 0:c],
                                            ahi[:, 4 * q:4 * q + 4, out].bitcast(F32),
                                            ALU.subtract).then_inc(S["a_lo"], 1)

            for i in range(NTILE):
                n = cols_of(i)
                col = [nst[0:n, r, i:i + 1] for r in range(6)]
                dve.wait_ge(S["x_sq"], i + 1)
                chain(nc.vector.tensor_scalar(col[1], col[0], 1.0 / D, EPS, ALU.mult, ALU.add))
                nc.vector.reciprocal(col[2], col[1]).then_inc(S["x_rms"], 1)
                dve.wait_ge(S["x_sqrt"], i + 1)
                chain(nc.vector.tensor_tensor(col[4], col[3], col[3], ALU.mult))
                chain(nc.vector.tensor_tensor(col[4], col[4], col[1], ALU.mult))
                chain(nc.vector.tensor_scalar(col[4], col[4], -0.5, 1.5, ALU.mult, ALU.add))
                chain(nc.vector.tensor_tensor(col[5], col[4], col[3], ALU.mult))
                if i == 0:
                    dve.wait_ge(S["g_in"], 16)
                nc.vector.scalar_tensor_tensor(out=xt[0:n, i % 3, :], in0=xt[0:n, i % 3, :], scalar=col[5],
                                               in1=gb[0:n, :], op0=ALU.mult, op1=ALU.mult).then_inc(S["x_scaled"], 1)
                if i:
                    turned_lo(i - 1)
            turned_lo(NTILE - 1)

            for n in (0, 1):
                for s in range(2):
                    split_lo(dve, n, s, WIDTH0 if n == 0 else 128)
            dve.wait_ge(S["kiw_turned"], 1)
            nc.vector.tensor_copy(kiw[:, 0:6, :], psf[:, 3072:3072 + 480].rearrange("p (t c) -> p t c", c=80))
            chain(nc.vector.tensor_copy(kiw[:, 6:9, :], psf[:, 3584:3584 + 240].rearrange("p (t c) -> p t c", c=80)))
            nc.vector.tensor_scalar(wsc[:, :, :], kiw[:, :, ID:ID + IH], ID ** -0.5 * IH ** -0.5, None,
                                    ALU.mult).then_inc(S["kiw_kept"], 1)
            with dve.Fori(0, NQI // 2) as i:
                for n in (2, 3):
                    for s in range(2):
                        split_lo(dve, n, s, i=i)

            nc.vector.memset(score[:, :], 0.0).then_inc(S["score_init"], 1)
            dve.wait_ge(S["ki_hi"], 1)
            nc.vector.tensor_tensor(klo[:, :], relub[:, :], khi[:, :].bitcast(F32),
                                    ALU.subtract).then_inc(S["ki_lo"], 1)

            def query_lo(n):
                i, h = QUNITS[n]
                dve.wait_ge(S["q_hi"], n + 1)
                c = cols_of(i)
                if i == NTILE - 1:
                    nc.vector.tensor_copy(qlast[:, h, :, :], qraw[:, :, TAIL:TAIL + NSAMP])
                nc.vector.tensor_tensor(qst[64:128, n % 2, :, 0:c], qraw[64:128, :, 0:c],
                                        qst[64:128, n % 2, :, 0:c].bitcast(F32), ALU.subtract).then_inc(S["q_lo"], 1)

            query_lo(0)
            dve.wait_ge(S["score_init"], 1)
            for what, *x in indexer_order():
                if what == "step":
                    step_dve(dve, *x)
                    continue
                u = x[0]
                i, h, k = IUNITS[u]
                n = u // (IH // 2)
                if k == 0 and n + 1 < len(QUNITS):
                    query_lo(n + 1)
                rows = rows_of(i)
                dve.wait_ge(S["relu_done"], u + 1)
                if u:
                    dve.wait_ge(S["scored"], u)
                out = score_of(i)[0:rows, :]
                nc.vector.scalar_tensor_tensor(out=out, in0=relu_of(u)[0:rows, 0:keys_of(i)],
                                               scalar=wsc[0:rows, i, 8 * h + k:8 * h + k + 1], in1=out,
                                               op0=ALU.mult, op1=ALU.add).then_inc(S["scored"], 1)
            dve.wait_ge(S["logits"], len(IUNITS))
            chain(nc.vector.memset(qbd[:, :, :], 0.0))
            for b in range(NSAMP):
                r = 64 * (b % 2)
                for h in range(2):
                    last = nc.vector.tensor_copy(qbd[r:r + 64, b // 2, 16 * b + 8 * h:16 * b + 8 * h + 8],
                                                 qlast[r:r + 64, h, :, b])
                last.then_inc(S["qb_ready"], 1)
            for what, *x in samples_order():
                if what == "sum":
                    break
                if what == "step":
                    step_dve(dve, *x)
            dve.wait_ge(S["slogits"], NSAMP // 2)
            dve.wait_ge(S["wcol_in"], 16 * NSAMP)
            nc.vector.tensor_scalar(rsc[:, :], psf[:, 1536:1536 + PAST + 1], 0.0, wcol[:, :], ALU.max,
                                    ALU.mult).then_inc(S["srelu"], 1)
            dve.wait_ge(S["ssum"], 1)
            last8 = score_of(NTILE - 1)
            nc.vector.tensor_scalar(last8[32:40, 0:PAST + 1], psf[32:40, 1536:1536 + PAST + 1],
                                    ID ** -0.5 * IH ** -0.5, None, ALU.mult).then_inc(S["ssum_kept"], 1)
            dve.wait_ge(S["ssum_kept"], 1)
            chain(nc.vector.memset(last8[32:40, PAST + 1:L], NEG_MASK))
            after = False
            for what, *x in samples_order():
                after = after or what == "sum"
                if after and what == "step":
                    step_dve(dve, *x)
            dve.wait_ge(S["score_init"], 2)

            def largest(count):
                for m, t in enumerate(TOPK_TILES):
                    r = 128 if t < NTILE - 1 else 40
                    x = nc.vector.max(m8[0:r, m, :], score_of(t)[0:r, :])
                x.then_inc(S["maxed"], 1)
                dve.wait_ge(S["maxed"], count)

            def take(count):
                for m, t in enumerate(TOPK_TILES):
                    r = 128 if t < NTILE - 1 else 40
                    x = nc.vector.match_replace(score_of(t)[0:r, :], m8[0:r, m, :], score_of(t)[0:r, :], NEG_TAKEN)
                x.then_inc(S["taken"], 1)
                dve.wait_ge(S["taken"], count)

            first = B_MAIN + NX + 1
            rounds = B_OUT - first
            with dve.Fori(0, rounds // 2) as i:
                for q in range(2):
                    largest(2 * i + q + 1)
                    split_lo(dve, first + q, 0, i=i)
                    take(2 * i + q + 1)
                    split_lo(dve, first + q, 1, i=i)
            for r in range(rounds, ROUNDS):
                largest(r + 1)
                take(r + 1)
            dve.wait_ge(S["spos_in"], 16)
            for t in TOPK_TILES:
                n = 128 if t < NTILE - 1 else 40
                x = score_of(t)[0:n, :]
                chain(nc.vector.tensor_scalar(x, x, (NEG_TAKEN + NEG_MASK) / 2, NEG_BIAS, ALU.is_gt, ALU.mult))
                chain(nc.vector.scalar_tensor_tensor(out=x, in0=x, scalar=cst[0:n, K_TQ + t:K_TQ + t + 1],
                                                     in1=spos[0:n, 0:keys_of(t)], op0=ALU.add, op1=ALU.add))
            for t in range(FIRST_TOPK):
                nc.vector.tensor_scalar(dist_of(t), spos[:, 0:keys_of(t)], cst[:, K_TQ + t:K_TQ + t + 1], None,
                                        ALU.add).then_inc(S["dist_made"], 1)
            dve.wait_ge(S["ak_hi"], 1)
            nc.vector.tensor_tensor(akl[:, :, :], kin[:, :, 0:L], akh[:, :, :].bitcast(F32),
                                    ALU.subtract).then_inc(S["ak_lo"], 1)

            def query_rest(s):
                dve.wait_ge(S["aq_hi"], s + 1)
                c = cols_of(ATILES[s])
                nc.vector.scalar_tensor_tensor(out=ql[:, s % 2, :, 0:c], in0=qin[:, s % 2, :, 0:c], scalar=HD ** -0.5,
                                               in1=qh[:, s % 2, :, 0:c].bitcast(F32), op0=ALU.mult,
                                               op1=ALU.subtract).then_inc(S["aq_lo"], 1)

            dve.wait_ge(S["aq_in0"], 16)
            nc.vector.tensor_scalar(qsamp[:, :, :], qin[:, 0, :, TAIL:TAIL + NSAMP], HD ** -0.5, None, ALU.mult)
            query_rest(0)
            for i in range(1, NTILE, 2):
                n = cols_of(i)
                dve.wait_ge(S["kv_turned"], i + 1)
                nc.vector.tensor_copy(kvtok[0:n, i, :], ps[0:n, i % 6, :]).then_inc(S["kvtok_kept1"], 1)
            dve.wait_ge(S["dist_masked"], FIRST_TOPK)

            def normalize(u, r):
                i, g = AUNITS[u]
                n, w = rows_of(i), keys_of(i)
                dve.wait_ge(S["aexp"], 4 * u + r + 1)
                chain(nc.vector.reciprocal(ast[0:n, 2, u % 2, r:r + 1], ast[0:n, 1, u % 2, r:r + 1]))
                x = prob[0:n, u % 2, r, 0:w]
                nc.vector.tensor_scalar(x, x, ast[0:n, 2, u % 2, r:r + 1], None, ALU.mult).then_inc(S["normed"], 1)

            def gate(u):
                i, g = AUNITS[u]
                n = rows_of(i)
                if g == 0:
                    dve.wait_ge(S[f"az_in{qbuf(u)}"], 16 * (u // KVH // 2 + 1))
                if u == 0:
                    nc.vector.tensor_copy(zsamp[:, :, :], zin[:, 0, :, TAIL:TAIL + NSAMP])
                dve.wait_ge(S["pv_mm"], blocks_to(u + 1))
                if u >= 2:
                    dve.wait_ge(S[f"o_stored{u % 2}"], 16 * (u // 2))
                nc.vector.tensor_tensor(osb[:, u % 2, :, 0:n],
                                        ps[:, out_bank(u), 0:4 * n].rearrange("p (h t) -> p h t", h=4),
                                        zin[:, qbuf(u), 4 * g:4 * g + 4, 0:n], ALU.mult).then_inc(S["gated"], 1)

            for k in range(NHEAD):
                u, r = divmod(k, 4)
                i, g = AUNITS[u]
                n, w = rows_of(i), keys_of(i)
                dve.wait_ge(S["aqk"], k + 1)
                if u >= 2 and r == 0:
                    dve.wait_ge(S["p_turned"], blocks_to(u - 1))
                x = prob[0:n, u % 2, r, 0:w]
                o = score_bank(k, w)
                nc.vector.scalar_tensor_tensor(out=x, in0=dist_of(i)[0:n, :], scalar=2.0 ** -(4 * g + r + 1),
                                               in1=psf[0:n, o:o + w], op0=ALU.mult, op1=ALU.add
                                               ).then_inc(S["abias"], 1)
                dve.wait_ge(S["abias"], k + 1)
                chain(nc.vector.tensor_reduce(ast[0:n, 0, u % 2, r:r + 1], x, AX.X, ALU.max))
                nc.vector.tensor_scalar(ast[0:n, 0, u % 2, r:r + 1], ast[0:n, 0, u % 2, r:r + 1], -1.0, None,
                                        ALU.mult).then_inc(S["amax"], 1)
                if k:
                    normalize(*divmod(k - 1, 4))
                if g == KVH - 1 and r == 2 and u // KVH + 1 < NTILE:
                    query_rest(u // KVH + 1)
                if r == 2 and u >= 2:
                    gate(u - 2)
            normalize(len(AUNITS) - 1, 3)
            gate(len(AUNITS) - 2)
            dve.wait_ge(S["p_turned"], blocks_to(len(AUNITS)))
            chain(nc.vector.memset(qz[:, :, :], 0.0))
            for m in range(NSAMP * KVH):
                b, g = divmod(m, KVH)
                x = nc.vector.tensor_copy(qz[:, m, 8 * b + 4 * g:8 * b + 4 * g + 4], qsamp[:, 4 * g:4 * g + 4, b])
            x.then_inc(S["qz_made"], 1)
            gate(len(AUNITS) - 1)
            dve.wait_ge(S["sdist"], 1)
            nc.vector.tensor_scalar(sbias[:, :], psf[0:64, 0:PAST + 1], cst[0:64, K_SLOPE:K_SLOPE + 1], None,
                                    ALU.mult).then_inc(S["sbias_made"], 1)

            def operand_lo(k):
                dve.wait_ge(S["o_hi"], k + 1)
                nc.vector.tensor_tensor(olo[:, k, :], orow[:, k % 4, :], ohi[:, k, :].bitcast(F32),
                                        ALU.subtract).then_inc(S["o_lo"], 1)

            for k in range(4):
                operand_lo(k)
            dve.wait_ge(S["sqk"], NSAMP * KVH)
            dve.wait_ge(S["sbias_made"], 1)
            chain(nc.vector.tensor_tensor(sprob[:, :], psf[0:64, 0:PAST + 1], sbias[:, :], ALU.add))
            chain(nc.vector.tensor_reduce(sst64[:, 0:1], sprob[:, :], AX.X, ALU.max))
            nc.vector.tensor_scalar(sst64[:, 0:1], sst64[:, 0:1], -1.0, None, ALU.mult).then_inc(S["smax"], 1)
            dve.wait_ge(S["sexp"], 1)
            chain(nc.vector.reciprocal(sst64[:, 2:3], sst64[:, 1:2]))
            nc.vector.tensor_scalar(sprob[:, :], sprob[:, :], sst64[:, 2:3], None, ALU.mult).then_inc(S["snormed"], 1)
            for s in range(2):
                split_lo(dve, B_OUT, s)
            dve.wait_ge(S["sv_used"], NSAMP)
            nc.vector.tensor_tensor(osamp[:, :, :].rearrange("p h b -> p b h"),
                                    ps[:, 5, 0:64].rearrange("p (b h) -> p b h", b=NSAMP),
                                    zsamp[:, :, :].rearrange("p h b -> p b h"),
                                    ALU.mult).then_inc(S["sgated"], 1)
            for k in range(4, KT):
                operand_lo(k)
            chain(nc.vector.memset(fst[:, 0, :], 0.0))

            def add_residual(n, part, i=None):
                p = parity(n)
                add1, add2 = (0, 0) if i is None else (i, 2 * i)
                if part == 0:
                    dve.wait_ge(S["h_turned"], 2 * (n - B_OUT) + 1 + 2 * add2)
                    dve.wait_ge(S[f"xb_in{p}"], 80 * ((n - B_OUT) // 2 + 1) + 80 * add1)
                    if n >= B_OUT + 2:
                        dve.wait_ge(S[f"h_stored{p}"], 32 * ((n - B_OUT) // 2) + 32 * add1)
                    nc.vector.tensor_tensor(hblk[:, p, 0:8, :], psf[:, 3072:4096].rearrange("p (t c) -> p t c", c=128),
                                            xblk[:, p, 0:8, :], ALU.add).then_inc(S["h_part"], 1)
                else:
                    dve.wait_ge(S["h_turned"], 2 * (n - B_OUT) + 2 + 2 * add2)
                    c = cols_of(NTILE - 1)
                    nc.vector.tensor_tensor(hblk[0:c, p, NTILE - 1, :], ps[0:c, 6, 0:128], xblk[0:c, p, NTILE - 1, :],
                                            ALU.add).then_inc(S["h_added"], 1)

            def add_squares(n, i=None):
                p = parity(n)
                add2 = 0 if i is None else 2 * i
                dve.wait_ge(S["h_squared"], n - B_OUT + 1 + add2)
                nc.vector.tensor_tensor(fst[:, 0, 0:8], fst[:, 0, 0:8], sq[:, p, 0:8], ALU.add)
                c = cols_of(NTILE - 1)
                nc.vector.tensor_tensor(fst[0:c, 0, 8:9], fst[0:c, 0, 8:9], sq[0:c, p, 8:9], ALU.add
                                        ).then_inc(S["sq_added"], 1)
                dve.wait_ge(S["sq_added"], n - B_OUT + 1 + add2)

            def out_block(n, i=None):
                split_lo(dve, n + 1, 0, i=i)
                if n > B_OUT:
                    add_residual(n - 1, 0, i)
                split_lo(dve, n + 1, 1, i=i)
                if n > B_OUT:
                    add_residual(n - 1, 1, i)
                if n > B_OUT + 1:
                    add_squares(n - 2, i)

            for n in range(B_OUT, B_OUT + 4):
                out_block(n)
            with dve.Fori(0, (NOUT - 6) // 2) as i:
                out_block(B_OUT + 4, i)
                out_block(B_OUT + 5, i)
            n = B_OUT + NOUT - 2
            out_block(n)
            for n in (n, n + 1):
                add_residual(n, 0)
                add_residual(n, 1)
                add_squares(n - 1)
            add_squares(n)
            col = [fst[:, r, :] for r in range(6)]
            chain(nc.vector.tensor_scalar(col[1], col[0], 1.0 / D, EPS, ALU.mult, ALU.add))
            nc.vector.reciprocal(col[2], col[1]).then_inc(S["f_rms"], 1)
            dve.wait_ge(S["f_sqrt"], 1)
            chain(nc.vector.tensor_tensor(col[4], col[3], col[3], ALU.mult))
            chain(nc.vector.tensor_tensor(col[4], col[4], col[1], ALU.mult))
            chain(nc.vector.tensor_scalar(col[4], col[4], -0.5, 1.5, ALU.mult, ALU.add))
            chain(nc.vector.tensor_tensor(col[5], col[4], col[3], ALU.mult))
            dve.wait_ge(S["fg_in"], 16)
            for i in range(NTILE):
                n = cols_of(i)
                dve.wait_ge(S[f"fh_in{i}"], 16)
                nc.vector.scalar_tensor_tensor(out=fh[0:n, i, :], in0=fh[0:n, i, :], scalar=fst[0:n, 5, i:i + 1],
                                               in1=fg[0:n, :], op0=ALU.mult, op1=ALU.mult).then_inc(S["f_done"], 1)

        @block.tensor
        def _(pe):
            pe.wait_ge(S["cst_in"], 16)
            for i in range(NTILE):
                pe.wait_ge(S["x_scaled"], i + 1)
                n = cols_of(i)
                for q in range(4):
                    if i:
                        pe.wait_ge(S["a_lo"], 4 * (i - 1) + q + 1)
                    for k in range(4):
                        last = nc.tensor.transpose(ps[:, q, 128 * k:128 * k + n],
                                                   xt[0:n, i % 3, 128 * (4 * q + k):128 * (4 * q + k) + 128],
                                                   ident[0:n, 0:n])
                    last.then_inc(S["x_turned"], 1)
            pe.wait_ge(S["a_lo"], 4 * NTILE)
            pe.wait_ge(S["x_sq"], NTILE)
            project(pe, 0, WIDTH0, first=True)
            project(pe, 1, first=True)
            pe.wait_ge(S["evac"], 1)
            for i in range(NTILE):
                n = cols_of(i)
                at = 3072 + 80 * i if i < 6 else 3584 + 80 * (i - 6)
                last = nc.tensor.transpose(psf[0:n, at:at + WIDTH0], stage[0:WIDTH0, 1, 128 * i:128 * i + n],
                                           ident[0:WIDTH0, 0:WIDTH0])
            last.then_inc(S["kiw_turned"], 1)
            project(pe, 2)
            with pe.Fori(0, NQI // 2 - 1) as i:
                project(pe, 3, i=i)
                project(pe, 4, i=i)
            for what, *x in indexer_order():
                if what == "step":
                    step_among(pe, *x)
                    continue
                u = x[0]
                i = IUNITS[u][0]
                n, k = divmod(u, IH // 2)
                rows, w = rows_of(i), keys_of(i)
                if k == 0:
                    pe.wait_ge(S["q_lo"], n + 1)
                if u == 0:
                    pe.wait_ge(S["evac"], B_MAIN)
                    pe.wait_ge(S["ki_lo"], 1)
                if u >= 2:
                    pe.wait_ge(S["relu_done"], u - 1)
                o = logit_column(u, w)
                if o % BANK:
                    whole, rest = [(w % BANK + BANK * b, BANK) for b in range(w // BANK)], [(0, w % BANK)]
                else:
                    whole = [x for x in banks(w) if x[0] < 2 * BANK]
                    rest = [x for x in banks(w) if x[0] >= 2 * BANK]
                for part in (whole, rest):
                    if part is rest and rest:
                        pe.wait_ge(S["relu_done"], u)
                    for m in (khi, klo):
                        for c, cw in part:
                            last = nc.tensor.matmul(psf[0:rows, o + c:o + c + cw], qst[:, n % 2, k, 0:rows], m[:, c:c + cw],
                                                    start=m is khi, stop=m is klo)
                last.then_inc(S["logits"], 1)
            for what, *x in samples_order():
                if what == "step":
                    step_among(pe, *x)
                if what == "turn":
                    j = x[0]
                    for half in range(2):
                        pe.wait_ge(S[f"ik{half}_in{j % 2}"], 16 * NPAGES * (j // 2 + 1))
                    if j == 0:
                        pe.wait_ge(S["relu_done"], len(IUNITS))
                    else:
                        pe.wait_ge(S["ik_copied"], j)
                    for k in range(NPAGES):
                        last = nc.tensor.transpose(psf[:, 3072 + 128 * k:3072 + 128 * k + 128],
                                                   iload[:, j % 2, k, :, :].rearrange("p b d -> p (b d)"), ident)
                    last.then_inc(S["ik_turned"], 1)
                if what == "logit":
                    j = x[0]
                    pe.wait_ge(S["ik_copied"], j + 1)
                    pe.wait_ge(S["ikn_in"], 32 * (j + 1))
                    if j == 0:
                        pe.wait_ge(S["qb_ready"], 8)
                    for c, w in banks(PAST + 1):
                        last = nc.tensor.matmul(psf[:, 1536 + c:1536 + c + w], qbd[:, j, :], ikt[:, c:c + w],
                                                start=j == 0, stop=j == NSAMP // 2 - 1)
                    last.then_inc(S["slogits"], 1)
                if what == "sum":
                    pe.wait_ge(S["srelu"], 1)
                    for c, w in banks(PAST + 1):
                        last = nc.tensor.matmul(psf[32:40, 1536 + c:1536 + c + w], cst[:, K_ONEB:K_ONEB + 8], rsc[:, c:c + w],
                                                start=True, stop=True)
                    last.then_inc(S["ssum"], 1)
            pe.wait_ge(S["ssum_kept"], 1)
            B_ZP = B_MAIN + POOLW // 128
            for n in range(B_MAIN + NX, B_ZP):
                project(pe, n)
            with pe.Fori(0, POOLW // 256) as i:
                project(pe, B_ZP, i=i)
                project(pe, B_ZP + 1, i=i)
            pe.wait_ge(S["ul_in"], 16)
            for c in range(POOLW // 128):
                last = nc.tensor.transpose(psf[0:PAD + NSAMP, 3072 + 128 * c:3072 + 128 * c + 128], ulast[:, c, :], ident)
            last.then_inc(S["ul_turned"], 1)
            pe.wait_ge(S["state_in"], 32)
            pe.wait_ge(S["ul_kept"], 1)
            rows = NSAMP * PAD
            for c in range(POOLW // 128):
                g = c // 2
                last = nc.tensor.matmul(ps[:, 6, 8 * c:8 * c + 8], strow[:, 128 * c:128 * c + 128],
                                        cst[0:rows, K_STATE + 8 * g:K_STATE + 8 * g + 8], start=True, stop=True)
            last.then_inc(S["st_summed"], 1)
            B_GRP = B_MAIN + 2 * (POOLW // 128)
            with pe.Fori(0, POOLW // GROUP) as g:
                for q in range(4):
                    project(pe, B_GRP + q, i=g * 2)
                pe.wait_ge(S["p_mixed"], g + 1)
                pe.wait_ge(S["p_in"], g * 48 + 48)
                for x in range(6):
                    m, c = divmod(x, 3)
                    t0, tn = CHUNKS[c]
                    if x < 2:
                        pe.wait_ge(S["st_kept"], 1)
                    else:
                        pe.wait_ge(S["p_scaled"], g * 6 + x - 1)
                    for k in range(2):
                        last = nc.tensor.matmul(ps[:, 6 + x % 2, 0:tn], pw[:, k, 128 * m:128 * m + 128],
                                                pu[:, k, t0:t0 + tn], start=k == 0, stop=k == 1)
                    last.then_inc(S["p_mm"], 1)
            with pe.Fori(0, (B_OUT - B_GRP - 16) // 2) as i:
                project(pe, B_GRP + 16, i=i)
                project(pe, B_GRP + 17, i=i)
            pe.wait_ge(S["kin_in"], 16)
            pe.wait_ge(S["vin_in"], 32)
            for i in range(NTILE):
                n = cols_of(i)
                if i == 0:
                    pe.wait_ge(S["evac"], B_OUT - 1)
                if i == 3:
                    pe.wait_ge(S["evac"], B_OUT)
                if i >= 6:
                    pe.wait_ge(S[f"kvtok_kept{i % 2}"], (i - 6) // 2 + 1)
                for b in range(2 * KVH):
                    at = slice(128 * i, 128 * i + n)
                    src = kin[:, b, at] if b < KVH else vin[:, b - KVH, at] if i < NTILE - 1 else vtail[:, b - KVH, :]
                    last = nc.tensor.transpose(ps[0:n, i % 6, 128 * b:128 * b + 128], src, ident)
                last.then_inc(S["kv_turned"], 1)
            pe.wait_ge(S["kvtok_kept0"], (NTILE + 1) // 2)
            pe.wait_ge(S["kvtok_kept1"], NTILE // 2)
            pe.wait_ge(S["ak_lo"], 1)
            pe.wait_ge(S["p_scaled"], 24)

            def scores(k):
                u, r = divmod(k, 4)
                i, g = AUNITS[u]
                n, w = rows_of(i), keys_of(i)
                if g == 0 and r == 0:
                    pe.wait_ge(S["aq_lo"], u // KVH + 1)
                if k >= 2:
                    pe.wait_ge(S["abias"], k - 1)
                o = score_bank(k, w)
                pieces = banks(w) if o % BANK == 0 else [(BANK * b + w % BANK, BANK) for b in range(w // BANK)]
                rest = [x for x in pieces if x[1] < BANK] if w > 2 * BANK else []
                if o % BANK:
                    rest = [(0, w % BANK)]
                for part in ([x for x in pieces if x not in rest], rest):
                    if part is rest and rest and k:
                        pe.wait_ge(S["abias"], k)
                    for q, m in ((qh, akh), (qh, akl), (ql, akh)):
                        for c, cw in part:
                            last = nc.tensor.matmul(psf[0:n, o + c:o + c + cw], q[:, qbuf(u), 4 * g + r, 0:n],
                                                    m[:, g, c:c + cw], start=m is akh and q is qh, stop=q is ql)
                last.then_inc(S["aqk"], 1)

            def weighted(t, v, j):
                i, g = AUNITS[v]
                n = rows_of(i)
                kn = min(128, L - 128 * j)
                pe.wait_ge(S["pt_copied"], t + 1)
                if j == 0 and v > 1:
                    pe.wait_ge(S["gated"], v - 1)
                if j == 0 and v == 1:
                    pe.wait_ge(S["abias"], 4 * KVH)
                nc.tensor.matmul(ps[:, out_bank(v), 0:4 * n], kvtok[0:kn, j, 256 + 128 * g:256 + 128 * g + 128],
                                 pts[0:kn, t % 2, 0:4 * n], start=j == 0, stop=j == i).then_inc(S["pv_mm"], 1)

            t, waiting = 0, None
            for k in range(NHEAD + LAG):
                if k < NHEAD:
                    scores(k)
                if waiting:
                    weighted(*waiting)
                    waiting = None
                for v, j in back_blocks(k):
                    i, g = AUNITS[v]
                    n = rows_of(i)
                    kn = min(128, L - 128 * j)
                    if j == 0:
                        pe.wait_ge(S["normed"], 4 * v + 4)
                    if t >= 2:
                        pe.wait_ge(S["pt_copied"], t - 1)
                    for h in range(4):
                        last = nc.tensor.transpose(ps[0:kn, 5 + t % 2, n * h:n * h + n],
                                                   prob[0:n, v % 2, h, 128 * j:128 * j + kn], ident[0:n, 0:n])
                    last.then_inc(S["p_turned"], 1)
                    if waiting:
                        weighted(*waiting)
                    waiting = (t, v, j)
                    t += 1
            if waiting:
                weighted(*waiting)

            pe.wait_ge(S["abias"], NHEAD)
            pe.wait_ge(S["pt_copied"], blocks_to(len(AUNITS)))
            for half in range(2):
                pe.wait_ge(S[f"ck_in{half}"], 16 * NSAMP * NPAGES // 2)
            for m in range(NSAMP * KVH + 1):
                if m < NSAMP * KVH:
                    b, g = divmod(m, KVH)
                    if m == 1:
                        pe.wait_ge(S["gated"], len(AUNITS))
                        for c, w in banks(PAST + 1):
                            last = nc.tensor.matmul(psf[0:64, c:c + w], cst[32:40, K_ESEL:K_ESEL + 64],
                                                    score_of(NTILE - 1)[32:40, c:c + w], start=True, stop=True)
                        last.then_inc(S["sdist"], 1)
                    if m >= 2:
                        pe.wait_ge(S["sk_copied"], m - 1)
                    for k in range(NPAGES):
                        o = 2048 + 1024 * (m % 2) + 128 * k
                        last = nc.tensor.transpose(psf[:, o:o + 128], key_slot(b)[:, k, 128 * g:128 * g + 128], ident)
                    last.then_inc(S["sk_turned"], 1)
                if m == 1:
                    pe.wait_ge(S["qz_made"], 1)
                    pe.wait_ge(S["sbias_made"], 1)
                    pe.wait_ge(S["knew_kept"], 1)
                if m:
                    b, g = divmod(m - 1, KVH)
                    pe.wait_ge(S["sk_copied"], m)
                    q = qz[:, m - 1, :]
                    for c, w in banks(PAST):
                        nc.tensor.matmul(psf[0:64, c:c + w], q, skt[:, (m - 1) % 2, c:c + w], start=m == 1,
                                         stop=m == NSAMP * KVH)
                    nc.tensor.matmul(psf[0:64, PAST:PAST + 1], q, knew[:, g, b:b + 1], start=m == 1,
                                     stop=m == NSAMP * KVH).then_inc(S["sqk"], 1)
            pe.wait_ge(S["snormed"], 1)
            for k in range(NPAGES):
                nc.tensor.transpose(ps[:, 3, 64 * k:64 * k + 64], sprob[:, 128 * k:128 * k + 128], ident[0:64, 0:64])
            nc.tensor.transpose(ps[0:1, 4, 0:64], sprob[:, PAST:PAST + 1], ident[0:64, 0:64]).then_inc(S["sp_turned"], 1)
            pe.wait_ge(S["spt_copied"], 1)
            pe.wait_ge(S["vnew_in"], 16)
            for b in range(NSAMP):
                for half in range(2):
                    if b == 0:
                        pe.wait_ge(S[f"cv_in{half}"], 16 * 4 * NPAGES // 2)
                    if b >= 4:
                        pe.wait_ge(S[f"cv{half}_in{b}"], 16 * NPAGES // 2)
                for g in range(KVH):
                    o = 8 * b + 4 * g
                    for k in range(NPAGES):
                        nc.tensor.matmul(ps[:, 5, o:o + 4], value_slot(b)[:, k, 128 * g:128 * g + 128],
                                         spt[:, k, o:o + 4], start=k == 0, stop=False)
                    v = vnew[0:1, 256 * b + 128 * g:256 * b + 128 * g + 128]
                    last = nc.tensor.matmul(ps[:, 5, o:o + 4], v, spt[0:1, NPAGES, o:o + 4], start=False, stop=True)
                last.then_inc(S["sv_used"], 1)

            def turn_h(n, part, i=None):
                p = parity(n)
                add2 = 0 if i is None else 2 * i
                if part == 0:
                    pe.wait_ge(S["evac"], n + 1 + add2)
                    if n > B_OUT:
                        pe.wait_ge(S["h_added"], n - B_OUT + add2)
                    else:
                        pe.wait_ge(S["sgated"], 1)
                    for t in range(NTILE - 1):
                        last = nc.tensor.transpose(psf[:, 3072 + 128 * t:3200 + 128 * t],
                                                   stage[:, p, 128 * t:128 * t + 128], ident)
                else:
                    pe.wait_ge(S["h_part"], n - B_OUT + 1 + add2)
                    c = cols_of(NTILE - 1)
                    last = nc.tensor.transpose(ps[0:c, 6, 0:128], stage[:, p, T - c:T], ident)
                last.then_inc(S["h_turned"], 1)

            def project_out(n, i=None, before=True):
                project(pe, n, i=i, src=(ohi, olo), first_out=n == B_OUT and i is None,
                        between=(lambda: turn_h(n - 1, 0, i)) if before else None)
                if before:
                    turn_h(n - 1, 1, i)

            project_out(B_OUT, before=False)
            project_out(B_OUT + 1)
            with pe.Fori(0, NOUT // 2 - 1) as i:
                project_out(B_OUT + 2, i)
                project_out(B_OUT + 3, i)
            turn_h(B_OUT + NOUT - 1, 0)
            turn_h(B_OUT + NOUT - 1, 1)

        @block.gpsimd
        def _(pool):
            pool.wait_ge(S["pages_in"], 16)
            for j in range(2):
                load_index_keys(pool, j, 1)
            pool.wait_ge(S["scored"], len(TOPK_TILES) * IH)
            for i in TOPK_TILES:
                x = score_of(i)[0:rows_of(i), :]
                last = nc.gpsimd.affine_select(out=x, in_=x, compare_op=ALU.is_ge, fill=NEG_MASK, base=128 * i,
                                               pattern=[[-1, keys_of(i)]], channel_multiplier=1)
            last.then_inc(S["score_init"], 1)
            for j in range(2, NSAMP // 2):
                load_index_keys(pool, j, 1)
            tick = [0]

            def chain(ins):
                tick[0] += 1
                ins.then_inc(S["pool_step"], 1)
                pool.wait_ge(S["pool_step"], tick[0])

            for g in range(POOLW // GROUP):
                w = 2 << g
                pool.wait_ge(S["p_in"], 48 * (g + 1))
                pool.wait_ge(S["st_kept"], 1)
                for c in range(2):
                    u = pu[:, c, :]
                    a, b = pt[:, 0, :], pt[:, 1, :]
                    src, dst, step = u, a, 1
                    while step < w:
                        nc.gpsimd.tensor_copy(dst[:, 0:step], src[:, 0:step])
                        chain(nc.gpsimd.tensor_tensor(dst[:, step:L], src[:, step:L], src[:, 0:L - step], ALU.add))
                        src, dst, step = dst, (b if dst is a else a), 2 * step
                    nc.gpsimd.tensor_tensor(src[:, 0:16], src[:, 0:16], cst[:, K_CINV + 16 * g:K_CINV + 16 * g + 16], ALU.mult)
                    nc.gpsimd.tensor_scalar(src[:, 16:L], src[:, 16:L], 1.0 / w, None, ALU.mult)
                    chain(nc.gpsimd.tensor_tensor(dst[:, 0:NSAMP], sst[:, 2 * g + c, :], u[:, L:T], ALU.add))
                    chain(nc.gpsimd.tensor_scalar(dst[:, 0:NSAMP], dst[:, 0:NSAMP], 1.0 / w, None, ALU.mult))
                    nc.gpsimd.tensor_tensor(u[:, 0:L], src[:, 0:L], u[:, 0:L], ALU.subtract)
                    chain(nc.gpsimd.tensor_tensor(u[:, L:T], dst[:, 0:NSAMP], u[:, L:T], ALU.subtract))
                nc.gpsimd.engine_nop().then_inc(S["p_mixed"], 1)
                pool.wait_ge(S["p_scaled"], 6 * (g + 1))
                nc.gpsimd.tensor_tensor(pz[:, :, :], pz[:, :, :], pt[:, :, :], ALU.mult).then_inc(S["p_gated"], 1)
                pool.wait_ge(S["p_gated"], g + 1)
                pool.dma_start(mixt[GROUP * g:GROUP * (g + 1), :].rearrange("(c p) t -> p c t", p=128), pz[:, :, :]
                               ).then_inc(S["p_stored"], 16)
            for t in range(FIRST_TOPK):
                pool.wait_ge(S["dist_made"], FIRST_TOPK)
                nc.gpsimd.affine_select(out=dist_of(t), in_=dist_of(t), compare_op=ALU.is_ge, fill=NEG_BIAS,
                                        base=128 * t, pattern=[[-1, keys_of(t)]], channel_multiplier=1
                                        ).then_inc(S["dist_masked"], 1)
            pool.wait_ge(S["kv_turned"], NTILE)
            pool.wait_ge(S["pages_in"], 16)
            for b in range(NSAMP):
                load_keys(pool, b, 1)
            pool.wait_ge(S["p_turned"], blocks_to(len(AUNITS)))
            for b in range(NSAMP):
                load_values(pool, b, 1)


_INS = ["x_prompt", "x_sample", "cache_k", "cache_v", "cache_idx_k", "state_pool", "page_table",
        "meta_tokens", "norm_g", "w_in", "w_pool", "pool_scale", "w_out", "final_norm_g"]
_OUTS = [("y_prompt", (1, SEQ, D)), ("y_sample", (NSAMP, 1, D)),
         ("new_k_prompt", (1, 1, L, KVH, HD)), ("new_v_prompt", (1, 1, L, KVH, HD)),
         ("new_idx_k_prompt", (1, 1, L, ID)), ("new_pool_prompt", (1, 1, PAD, POOLW)),
         ("new_k_sample", (1, NSAMP, 1, KVH, HD)), ("new_v_sample", (1, NSAMP, 1, KVH, HD)),
         ("new_idx_k_sample", (1, NSAMP, 1, ID)), ("new_pool_sample", (1, NSAMP, PAD, POOLW))]


def kernel(**inputs):
    import concourse.bacc as _bacc
    from concourse.bass_utils import run_bass_kernel_spmd as _run

    nc = _bacc.Bacc("TRN2", target_bir_lowering=False, num_devices=1, dynamic_dma_scratch_size=1024)
    arrays = {n: np.ascontiguousarray(inputs[n]) for n in _INS}
    arrays["consts"] = constants()
    io = {n: nc.dram_tensor(n, a.shape, mybir.dt.from_np(a.dtype), kind="ExternalInput").ap()
          for n, a in arrays.items()}
    for n, shape in _OUTS:
        io[n] = nc.dram_tensor(n, shape, F32, kind="ExternalOutput").ap()
    build(nc, io)
    r = _run(nc, [arrays], core_ids=[0])
    return tuple(r.results[0][n] for n, _ in _OUTS)
```

```python
from contextlib import ExitStack

import concourse.bass as bass
import numpy as np
from concourse import mybir

F32 = mybir.dt.float32
F32R = mybir.dt.float32r
I32 = mybir.dt.int32
ALU = mybir.AluOpType
ACT = mybir.ActivationFunctionType
AX = mybir.AxisListType

D = 2048
META, SEQ, NSAMP = 16, 1024, 8
L = META + SEQ
T = L + NSAMP
NTILE = -(-T // 128)
TAIL = L - 128 * (NTILE - 1)
POOLW, GROUP, PAD = 1024, 256, 15
HEADS, KVH, HD = 8, 2, 128
IH, ID = 16, 64
PAST, PAGE, NPAGES = 1024, 128, 8
NPHYS = 80
TOPK = 256
EPS = 1e-6
C_U, C_ZP, C_Q, C_K, C_V, C_ZA, C_QI, C_KI, C_WI = np.cumsum(
    [0, POOLW, POOLW, HEADS * HD, KVH * HD, KVH * HD, HEADS * HD, IH * ID, ID]).tolist()
DIN = C_WI + IH
KT = D // 128
HALF = KT // 2
NMAIN = C_QI // 128
NQI = IH * ID // 128
NOUT = D // 128
CHUNKS = [(0, 350), (350, 350), (700, T - 700)]
BANK = 512
NEG_MASK = -1.0e38
NEG_TAKEN = -3.0e38
NEG_BIAS = -1.0e30
DSPLIT = 12 * 128
NPROB = 3
FIRST_TOPK = TOPK // 128
TOPK_TILES = list(range(FIRST_TOPK, NTILE))
ROUNDS = TOPK // 8




def rows_of(i):
    return 128 if i < NTILE - 1 else TAIL


def cols_of(i):
    return 128 if i < NTILE - 1 else T - 128 * i


def keys_of(i):
    return min(128 * (i + 1), L)


def banks(width):
    return [(c, min(BANK, width - c)) for c in range(0, width, BANK)]


K_ID, K_TQ, K_ESEL, K_ONEB, K_SLOPE, K_CINV, K_STATE, K_S = np.cumsum(
    [0, 128, NTILE, 64, 8, 1, 4 * 16, 4 * 8]).tolist()
K_ALL = K_S + L


def constants():
    c = np.zeros((128, K_ALL), np.float32)
    p = np.arange(128)
    c[:, K_ID:K_ID + 128] = np.eye(128)
    c[:, K_S:K_S + L] = np.arange(L)[None]
    for i in range(NTILE):
        c[:, K_TQ + i] = -(128 * i + p)
    c[32:40, K_TQ + NTILE - 1] = -PAST
    for b in range(NSAMP):
        c[32 + b, K_ESEL + 8 * b:K_ESEL + 8 * b + 8] = 1
        c[16 * b:16 * b + 16, K_ONEB + b] = 1
    c[:, K_SLOPE] = 2.0 ** -(p % 8 + 1)
    for g in range(4):
        w = 2 << g
        c[:, K_CINV + 16 * g:K_CINV + 16 * g + 16] = 1 / np.minimum(np.arange(16) + 1, w)
        for b in range(NSAMP):
            c[15 * b + 16 - w:15 * b + 15, K_STATE + 8 * g + b] = 1
    return c


def build(nc, io):
    xp, xs_, ck, cv, cik = (io[n] for n in ("x_prompt", "x_sample", "cache_k", "cache_v", "cache_idx_k"))
    state, ptab, meta = io["state_pool"], io["page_table"], io["meta_tokens"]
    norm_g, w_in, w_pool, pscale = io["norm_g"], io["w_in"], io["w_pool"], io["pool_scale"]
    w_out, fin_g, consts = io["w_out"], io["final_norm_g"], io["consts"]

    proj = nc.dram_tensor("proj_scratch", (DIN, T), F32, kind="Internal").ap()
    mixt = nc.dram_tensor("mix_scratch", (D, T), F32, kind="Internal").ap()
    hbuf_d = nc.dram_tensor("h_scratch", (NTILE * 128, D), F32, kind="Internal").ap()

    def x_parts(i):
        if i == 0:
            return [(0, META, meta[:, :]), (META, 128 - META, xp[0, 0:128 - META, :])]
        lo = 128 * i - META
        if i < NTILE - 1:
            return [(0, 128, xp[0, lo:lo + 128, :])]
        return [(0, TAIL, xp[0, lo:SEQ, :]), (TAIL, NSAMP, xs_[:, 0, :])]

    X_PARTS = [len(x_parts(i)) for i in range(NTILE)]

    with ExitStack() as top:
        def sem(name):
            return top.enter_context(nc.semaphore(name))

        def sb(name, shape, dt=F32, ctx=top):
            return ctx.enter_context(nc.sbuf_tensor(name, shape, dt))

        ps = top.enter_context(nc.psum_tensor("ps", [128, 8, BANK], F32))
        psf = ps[:, :, :].rearrange("p b c -> p (b c)")
        cst = sb("cst", [128, K_S])
        ident = cst[:, K_ID:K_ID + 128]
        pages = sb("pages", [1, NSAMP * NPAGES], I32)
        with ExitStack() as c1:
            wslot = sb("wslot", [128, 4, NPAGES, KVH * HD], F32, c1)
        with ExitStack() as c1:
            fh01 = sb("fh01", [128, 2, D], F32, c1)
        wraw = sb("wraw", [128, 4, HALF, 128])
        whi = sb("whi", [128, 2, HALF, 128], F32R)
        wlo = sb("wlo", [128, 2, HALF, 128], F32R)
        with ExitStack() as c1:
            akh = sb("akh", [128, KVH, L], F32R, c1)
            akl = sb("akl", [128, KVH, L], F32R, c1)
            kvtok = sb("kvtok", [128, NTILE, 2 * KVH * HD], F32, c1)
            pts = sb("pts", [128, 2, BANK], F32, c1)
            with ExitStack() as c2:
                vslot = sb("vslot", [128, 3, NPAGES, KVH * HD], F32, c2)
            qin = sb("qin", [128, 2, HEADS, 128], F32, c1)
            qh = sb("qh", [128, 2, HEADS, 128], F32R, c1)
            ql = sb("ql", [128, 2, HEADS, 128], F32R, c1)
            slot = sb("slot", [128, 2, NPAGES, KVH * HD], F32, c1)
            with ExitStack() as c2:
                prob = sb("prob", [128, NPROB, 4, L], F32, c2)
            with ExitStack() as c2:
                slot67 = sb("slot67", [128, 2, NPAGES, KVH * HD], F32, c2)
                vslot3 = sb("vslot3", [128, NPAGES, KVH * HD], F32, c2)
                skt = sb("skt", [128, 2, PAST], F32, c2)
                qz = sb("qz", [128, NSAMP * KVH, 64], F32, c2)
                sbias = sb("sbias", [64, PAST + 1], F32, c2)
                sprob = sb("sprob", [64, PAST + 1], F32, c2)
                spt = sb("spt", [128, NPAGES + 1, 64], F32, c2)
        with ExitStack() as c1:
            oparts = sb("oparts", [128, KT, 2, T], F32R, c1)
            ohi, olo = oparts[:, :, 0, :], oparts[:, :, 1, :]
        with ExitStack() as c1:
            fh58 = sb("fh58", [128, 4, D], F32, c1)
            fg = sb("fg", [128, D], F32, c1)
        ahi = sb("ahi", [128, KT, T], F32R)
        alo = sb("alo", [128, KT, T], F32R)
        with ExitStack() as c1:
            xt = sb("xt", [128, 3, D], F32, c1)
            gb = sb("gb", [128, D], F32, c1)
            xsq = sb("xsq", [128, D], F32, c1)
            nst = sb("nst", [128, 6, NTILE], F32, c1)
        stage = sb("stage", [128, 2, T])
        with ExitStack() as c1:
            with ExitStack() as c2:
                fh23 = sb("fh23", [128, 2, D], F32, c2)
            orow = sb("orow", [128, 4, T], F32, c1)
            xblk = sb("xblk", [128, 2, NTILE, 128], F32, c1)
            hblk = sb("hblk", [128, 2, NTILE, 128], F32, c1)
            sq = sb("sq", [128, 2, NTILE], F32, c1)
            sqj = sb("sqj", [128, NTILE, 128], F32, c1)
            fst = sb("fst", [128, 6, NTILE], F32, c1)
            fh4 = sb("fh4", [128, 1, D], F32, c1)
        score = sb("score", [128, sum(keys_of(i) for i in TOPK_TILES)])
        m8 = sb("m8", [128, len(TOPK_TILES), 8])
        with ExitStack() as c1:
            kiw = sb("kiw", [128, NTILE, ID + IH], F32, c1)
            wsc = sb("wsc", [128, NTILE, IH], F32, c1)
            wcol = sb("wcol", [128, 1], F32, c1)
            qlast = sb("qlast", [128, 2, IH // 2, NSAMP], F32, c1)
            with ExitStack() as c2:
                rsc = sb("rsc", [128, PAST + 1], F32, c2)
                ikt = sb("ikt", [128, PAST + 1], F32, c2)
            khi = sb("khi", [128, L], F32R, c1)
            klo = sb("klo", [128, L], F32R, c1)
            with ExitStack() as c2:
                qst = sb("qst", [128, 2, IH // 2, 128], F32R, c2)
                qraw = sb("qraw", [128, IH // 2, 128], F32, c2)
                relub = sb("relub", [128, L], F32, c2)
            with ExitStack() as c2:
                qbd = sb("qbd", [128, 4, 128], F32, c2)
                iload = sb("iload", [128, 2, NPAGES, 2, ID], F32, c2)
        with ExitStack() as c1:
            psc = sb("psc", [128, POOLW // 128], F32, c1)
            psg = sb("psg", [128, 2], F32, c1)
            sst = sb("sst", [128, POOLW // 128, NSAMP], F32, c1)
            pw = sb("pw", [128, 2, GROUP], F32, c1)
            pu = sb("pu", [128, 2, T], F32, c1)
            pt = sb("pt", [128, 2, T], F32, c1)
            with ExitStack() as c2:
                pz = sb("pz", [128, 2, T], F32, c2)
            ulast = sb("ulast", [128, POOLW // 128, PAD + NSAMP], F32, c1)
            ulrow = sb("ulrow", [PAD + NSAMP, POOLW], F32, c1)
            strow = sb("strow", [NSAMP * PAD, POOLW], F32, c1)
        with ExitStack() as c1:
            spos = sb("spos", [128, L], F32, c1)
            dist01 = sb("dist01", [128, 3 * 128], F32, c1)
            zin = sb("zin", [128, 2, HEADS, 128], F32, c1)
            osb = sb("osb", [128, 2, 4, 128], F32, c1)
            knew = sb("knew", [128, KVH, NSAMP], F32, c1)
            qsamp = sb("qsamp", [128, HEADS, NSAMP], F32, c1)
            zsamp = sb("zsamp", [128, HEADS, NSAMP], F32, c1)
            ast = sb("ast", [128, 3, NPROB, 4], F32, c1)
            sst64 = sb("sst64", [64, 3], F32, c1)
            osamp = sb("osamp", [128, HEADS, NSAMP], F32, c1)
            vtail = sb("vtail", [128, KVH, T - 128 * (NTILE - 1)], F32, c1)
            with ExitStack() as c2:
                kin = sb("kin", [128, KVH, T], F32, c2)
            with ExitStack() as c2:
                vnew = sb("vnew", [1, NSAMP * KVH * HD], F32, c2)
        SOFF = {i: sum(keys_of(j) for j in TOPK_TILES if j < i) for i in TOPK_TILES}
        vin = wraw[:, 0:2, :, :].rearrange("p g k n -> p g (k n)")
        relua = wraw[:, 2:4, :, :].rearrange("p g k n -> p (g k n)")

        def score_of(i):
            return score[:, SOFF[i]:SOFF[i] + keys_of(i)]

        S = {}
        for name in ("cst_in", "g_in", "x_in0", "x_in1", "x_in2", "x_sq", "x_rms", "x_sqrt", "x_scaled",
                     "x_scaled_rest", "x_turned", "a_hi", "a_lo", "w_in0", "w_in1", "w_in2", "w_in3", "w_hi", "w_lo",
                     "w_used", "evac", "stored0", "stored1", "small", "pages_in", "state_in", "ul_in", "ul_turned",
                     "ul_kept", "ul_out", "st_summed", "st_kept", "psg_kept", "p_in", "p_mixed", "p_mm", "p_scaled",
                     "p_gated", "p_stored", "pool_step", "spos_in", "kin_in", "vin_in", "aq_in0", "aq_in1", "az_in0",
                     "az_in1", "kvtok_kept0", "kvtok_kept1", "kv_out", "kv_turned", "gated", "o_stored0", "o_stored1",
                     "pv_mm", "vnew_in", "sv_used", "so_copied", "so_turned", "ck_in0", "ck_in1", "cv_in0", "cv_in1",
                     "cv0_in4", "cv0_in5", "cv0_in6", "cv0_in7", "cv1_in4", "cv1_in5", "cv1_in6", "cv1_in7", "sgated",
                     "os_stored", "o_in0", "o_in1", "o_in2", "o_in3", "o_hi", "o_lo", "xb_in0", "xb_in1", "h_added",
                     "h_part", "h_turned", "h_squared", "sq_added", "h_stored0", "h_stored1", "fg_in",
                     *(f"fh_in{i}" for i in range(NTILE)), "f_rms", "f_sqrt", "f_done", "y_out", "ak_hi", "ak_lo",
                     "knew_kept", "aqk", "aq_hi", "aq_lo", "p_turned", "pt_copied", "amax", "aexp", "abias", "normed0",
                     "normed1", "inverse", "dist_made", "dist_masked", "sk_turned", "sk_copied", "sqk", "smax", "sexp",
                     "sp_turned", "spt_copied", "qz_made", "sdist", "sbias_made", "snormed", "kiw_turned", "kiw_kept",
                     "kiraw_in", "ki_hi", "ki_lo", "q_in", "q_hi", "q_lo", "logits", "relu_done", "scored",
                     "score_init", "ik0_in0", "ik0_in1", "ik1_in0", "ik1_in1", "ik_turned", "ik_copied", "qb_ready",
                     "slogits", "srelu", "ssum", "ssum_kept", "wcol_in", "ikn_in", "maxed", "taken", "outs"):
            S[name] = sem(name)
        block = top.enter_context(nc.Block())

        B_MAIN = 1 + NQI
        B_OUT = B_MAIN + NMAIN
        WIDTH0 = ID + IH

        def parity(n):
            return 1 - n % 2

        def uses(n):
            return (n + 1) // 2 if n % 2 else n // 2 + 1

        NX, NX1 = 5, 3

        def among(n):
            return B_MAIN <= n < B_MAIN + NX

        def pair(n):
            return 0 if among(n) else parity(n)

        def before(n):
            return max(m for m in range(n) if pair(m) == pair(n))

        def loads(n):
            return sum(pair(m) == pair(n) for m in range(n + 1))

        def load_half(q, n, s, src, width=128, add1=0, guard=True):
            p = pair(n)
            if guard:
                q.wait_ge(S["w_lo"], 2 * before(n) + s + 1 + 4 * add1)
            q.dma_start(wraw[:, 2 * p + s, :, 0:width],
                        src[s * HALF * 128:(s + 1) * HALF * 128, :].rearrange("(k p) n -> p k n", p=128)
                        ).then_inc(S[f"w_in{2 * p + s}"], 16)

        def load_block(q, n, src, width=128, i=None, guard=True):
            for s in range(2):
                load_half(q, n, s, src, width, 0 if i is None else i, guard)

        def split_hi(act, n, s, width=128, i=None, first=False):
            p = pair(n)
            add1, add4 = (0, 0) if i is None else (i, 4 * i)
            act.wait_ge(S[f"w_in{2 * p + s}"], 16 * loads(n) + 16 * add1)
            if not first:
                act.wait_ge(S["w_used"], 2 * n + s - 1 + add4)
            nc.scalar.activation(whi[:, s, :, 0:width], wraw[:, 2 * p + s, :, 0:width],
                                 ACT.Copy).then_inc(S["w_hi"], 1)

        def split_lo(dve, n, s, width=128, i=None):
            p = pair(n)
            add = 0 if i is None else 4 * i
            dve.wait_ge(S["w_hi"], 2 * n + s + 1 + add)
            nc.vector.tensor_tensor(wlo[:, s, :, 0:width], wraw[:, 2 * p + s, :, 0:width],
                                    whi[:, s, :, 0:width].bitcast(F32), ALU.subtract).then_inc(S["w_lo"], 1)

        def project(pe, n, width=128, i=None, first=False, src=None, first_out=False, between=None):
            add2, add4 = (0, 0) if i is None else (2 * i, 4 * i)
            if not first:
                pe.wait_ge(S["evac"], before(n) + 1 + add2)
            for s in range(2):
                pe.wait_ge(S["w_lo"], 2 * n + s + 1 + add4)
                if s and between:
                    between()
                for a in range(s * HALF, s * HALF + HALF):
                    if first_out:
                        pe.wait_ge(S["o_lo"], a + 1)
                    last = step(n, a, width, src or (ahi, alo))
                last.then_inc(S["w_used"], 1)

        def step(n, a, width=128, src=(ahi, alo), chunks=range(len(CHUNKS))):
            s, k = divmod(a, HALF)
            mhi, mlo = src
            for w, parts in ((whi, (mhi, mlo)), (wlo, (mhi,))):
                for m in parts:
                    for c in chunks:
                        t0, tn = CHUNKS[c]
                        last = nc.tensor.matmul(ps[0:width, 3 * pair(n) + c, 0:tn], w[:, s, k, 0:width],
                                                m[:, a, t0:t0 + tn],
                                                start=(a == 0 and w is whi and m is mhi),
                                                stop=(a == KT - 1 and w is wlo))
            return last

        TBANKS = (0, 1, 2, 6)
        EARLY = {3: (0, 0, 6), 4: (0, 6, 11), 5: (0, 11, 16), 6: (1, 0, 6), 7: (1, 6, 11), 8: (1, 11, 16)}

        IUNITS = [(i, h, k) for i in TOPK_TILES for h in range(2) for k in range(IH // 2)]
        QUNITS = [(i, h) for i in TOPK_TILES for h in range(2)]

        def steps_of(first, count):
            return [("step", n, a) for n in range(first, first + count) for a in range(KT)]

        def indexer_order():
            steps = steps_of(B_MAIN, NX1)
            order, early = steps[:HALF], steps[HALF:]
            done, cost = 0, [keys_of(i) + 200 for i, _, _ in IUNITS]
            for u in range(len(IUNITS)):
                order.append(("head", u))
                until = len(early) * sum(cost[:u + 1]) // sum(cost)
                order += early[done:until]
                done = until
            return order

        def samples_order():
            steps = steps_of(B_MAIN + NX1, NX - NX1)
            order, done = [], 0
            for count, what in ((8, ("turn", 0)), (2, ("logit", 0)), (3, ("turn", 1)), (2, ("logit", 1)),
                                (3, ("turn", 2)), (2, ("logit", 2)), (3, ("turn", 3)), (2, ("logit", 3)),
                                (4, ("sum", 0))):
                order += steps[done:done + count] + [what]
                done += count
            return order + steps[done:]

        def weights_at(n, a):
            return {HALF - 1: 0, KT - 1: 1}.get(a)

        def step_among(pe, n, a):
            if a == 0:
                pe.wait_ge(S["evac"], before(n) + 1)
            if a % HALF == 0:
                pe.wait_ge(S["w_lo"], 2 * n + a // HALF + 1)
            last = step(n, a)
            if a % HALF == HALF - 1:
                last.then_inc(S["w_used"], 1)

        def step_act(act, n, a):
            s = weights_at(n, a)
            if s == 0:
                split_hi(act, n + 1, 0)
            if s == 1:
                evacuate(act, n)
                split_hi(act, n + 1, 1)
                store_block(act, n, proj[128 * (n - B_MAIN):128 * (n - B_MAIN) + 128, :])

        def step_dve(dve, n, a):
            if weights_at(n, a) is not None:
                split_lo(dve, n + 1, weights_at(n, a))

        def logit_column(u, w):
            return 1536 if u % 2 == 0 else 3072 - (w - 2 * BANK if w > 2 * BANK else 0)

        def relu_of(u):
            return relua if u % 2 == 0 else relub

        def load_index_keys(q, j, half):
            if j < 2:
                q.wait_ge(S["qb_ready"], 8)
            else:
                q.wait_ge(S["ik_turned"], j - 1)
            first = half * NPAGES // 2
            for b in range(2):
                for k, page in enumerate(page_ids(q, 2 * j + b, first, NPAGES // 2)):
                    q.dma_start(iload[:, j % 2, first + k, b, :], cik[0, bass.ds(page, 1), :, :].rearrange("o s d -> (o s) d")
                                ).then_inc(S[f"ik{half}_in{j % 2}"], 16)

        FTILES = (2, 3, 4, 0, 1, 5, 6, 7, 8)
        FPLACES = ((0, 2, fh01), (2, 2, fh23), (4, 1, fh4), (5, 4, fh58))
        KEPT = D - 256

        def final_rows(t):
            for first, count, place in FPLACES:
                if first <= t < first + count:
                    return place[:, t - first, :]

        def key_slot(b):
            return wslot[:, b, :, :] if b < 4 else late_slot(b)

        def late_slot(b):
            return slot[:, b - 4, :, :] if b < 6 else slot67[:, b - 6, :, :]

        def value_slot(b):
            return vslot[:, b, :, :] if b < 3 else vslot3[:, :, :] if b == 3 else late_slot(b)

        def load_pages(q, src, dst, b, half, arrived):
            first = half * NPAGES // 2
            for k, page in enumerate(page_ids(q, b, first, NPAGES // 2)):
                q.dma_start(dst[:, first + k, :], src[0, bass.ds(page, 1), :, :, :].rearrange("o s d e -> (o s) (d e)")
                            ).then_inc(S[arrived], 16)

        def load_keys(q, b, half):
            if b == 6:
                q.wait_ge(S["p_turned"], blocks_to(len(AUNITS)))
                q.wait_ge(S[f"ck_in{half}"], 8 * 6 * NPAGES)
            load_pages(q, ck, key_slot(b), b, half, f"ck_in{half}")

        def load_values(q, b, half):
            if b >= 4:
                q.wait_ge(S["sk_turned"], KVH * (b + 1))
            load_pages(q, cv, value_slot(b), b, half, f"cv_in{half}" if b < 4 else f"cv{half}_in{b}")

        def quarter(i, r):
            nb = i + 1
            return range(r * nb // 4, (r + 1) * nb // 4)

        def evacuate(act, n, width=128, i=None, func=None, first=False, stored=True):
            p = parity(n)
            add1, add4 = (0, 0) if i is None else (i, 4 * i)
            act.wait_ge(S["w_used"], 2 * n + 2 + add4)
            if not first and stored:
                act.wait_ge(S[f"stored{p}"], 16 * (uses(n) - 1) + 16 * add1)
            f = func or ACT.Copy
            b = 3 * pair(n)
            nc.scalar.activation(stage[0:width, p, 0:700].rearrange("p (c t) -> p c t", c=2),
                                 ps[0:width, b:b + 2, 0:350], f)
            nc.scalar.activation(stage[0:width, p, 700:T], ps[0:width, b + 2, 0:T - 700],
                                 f).then_inc(S["evac"], 1)

        def store_block(act, n, dst, width=128, i=None):
            p = parity(n)
            add2 = 0 if i is None else 2 * i
            act.wait_ge(S["evac"], n + 1 + add2)
            act.dma_start(dst, stage[0:width, p, :]).then_inc(S[f"stored{p}"], 16)

        ATILES = [8, 7, 6, 5, 4, 3, 2, 1, 0]
        AUNITS = [(i, g) for i in ATILES for g in range(KVH)]
        NHEAD = 4 * len(AUNITS)
        LAG = 7

        def back_blocks(k):
            if k < LAG or k >= NHEAD + LAG:
                return []
            v, r = divmod(k - LAG, 4)
            return [(v, j) for j in quarter(AUNITS[v][0], r)]

        def qbuf(u):
            return (u // KVH) % 2

        def score_bank(k, w):
            return 0 if k % 2 == 0 else 1536 - (w - 2 * BANK if w > 2 * BANK else 0)

        SAMPLE_BANKS = (0, 1, 2, 5)
        sout = skt[0:HEADS, :, :].rearrange("p a (j c) -> p (a j) c", c=BANK)

        def sample_out(b):
            return ps[0:HEADS, SAMPLE_BANKS[b // 2], 256 * (b % 2):256 * (b % 2) + 256]

        def out_bank(u):
            return 7 if u % 2 == 0 else 2

        def blocks_to(u):
            return sum(i + 1 for i, _ in AUNITS[:u])

        def dist_of(i):
            if i in SOFF:
                return score_of(i)
            return dist01[:, 128 * (i * (i + 1) // 2):128 * (i * (i + 1) // 2) + keys_of(i)]

        def page_ids(q, b, first=0, count=NPAGES):
            at = b * NPAGES + first
            _, ids = nc.values_load_multi_w_load_instructions(
                pages[0:1, at:at + count], engines=[q.engine], min_val=0, max_val=NPHYS - 1)
            return ids

        @block.sync
        def _(sp):
            sp.dma_start(cst[:, :], consts[:, 0:K_S]).then_inc(S["cst_in"], 16)
            sp.dma_start(pages[:, :], ptab.rearrange("(o b) k -> o (b k)", o=1)).then_inc(S["pages_in"], 16)
            for i in range(NTILE):
                if i >= 3:
                    sp.wait_ge(S["x_turned"], 4 * (i - 2))
                for r0, n, src in x_parts(i):
                    sp.dma_start(xt[r0:r0 + n, i % 3, :], src).then_inc(S[f"x_in{i % 3}"], 16)
                if i == 0:
                    sp.dma_start(gb[:, :], norm_g[0, :].partition_broadcast(128)).then_inc(S["g_in"], 16)
                if i == 2:
                    load_block(sp, 0, w_in[0, :, C_KI:DIN], WIDTH0, guard=False)
            load_block(sp, 1, w_in[0, :, C_QI:C_QI + 128], guard=False)
            sp.wait_ge(S["w_lo"], 1)
            load_block(sp, 2, w_in[0, :, C_QI + 128:C_QI + 256])
            sp.wait_ge(S["kiw_kept"], 1)
            new_ik_p, new_ik_s = io["new_idx_k_prompt"], io["new_idx_k_sample"]
            full = 128 * (NTILE - 1)
            sp.dma_start(new_ik_p[0, 0, 0:full, :].rearrange("(t p) d -> p t d", p=128),
                         kiw[:, 0:NTILE - 1, 0:ID]).then_inc(S["outs"], 16)
            sp.dma_start(new_ik_p[0, 0, full:L, :], kiw[0:TAIL, NTILE - 1, 0:ID]).then_inc(S["outs"], 16)
            sp.dma_start(new_ik_s[0, :, 0, :], kiw[TAIL:TAIL + NSAMP, NTILE - 1, 0:ID]).then_inc(S["outs"], 16)
            with sp.Fori(0, NQI // 2 - 1) as i:
                load_block(sp, 3, w_in[0, :, bass.ds(i * 256 + C_QI + 256, 128)], i=i)
                load_block(sp, 4, w_in[0, :, bass.ds(i * 256 + C_QI + 384, 128)], i=i)
            load_block(sp, B_MAIN, w_in[0, :, 0:128])
            sp.wait_ge(S["stored1"], 16 * uses(NQI))
            sp.wait_ge(S["stored0"], 16 * uses(NQI - 1))
            for r in range(2):
                sp.dma_start(relub[64 * r:64 * r + 64, :], proj[C_KI:C_WI, 0:L]).then_inc(S["kiraw_in"], 16)

            def load_query(n):
                i, h = QUNITS[n]
                if n:
                    sp.wait_ge(S["q_lo"], n)
                cols = cols_of(i)
                for r in range(2):
                    sp.dma_start(qraw[64 * r:64 * r + 64, :, 0:cols],
                                 proj[C_QI + 512 * h:C_QI + 512 * h + 512, 128 * i:128 * i + cols]
                                 .rearrange("(h d) t -> d h t", d=64)).then_inc(S["q_in"], 16)

            def load_main_half(n, s):
                c = 128 * (n - B_MAIN)
                load_half(sp, n, s, w_in[0, :, c:c + 128])

            load_query(0)
            load_main_half(B_MAIN + 1, 0)
            load_main_half(B_MAIN + 1, 1)
            for what, *x in indexer_order():
                if what == "head" and x[0] % (IH // 2) == 0 and x[0] // (IH // 2) + 1 < len(QUNITS):
                    load_query(x[0] // (IH // 2) + 1)
                if what == "step" and weights_at(*x) is not None and x[0] + 2 < B_MAIN + NX:
                    load_main_half(x[0] + 2, weights_at(*x))
            with nc.allow_non_contiguous_dma(reason="128 single weights"):
                for b in range(NSAMP):
                    sp.dma_start(wcol[16 * b:16 * b + 16, :], proj[C_WI:DIN, L + b:L + b + 1]).then_inc(S["wcol_in"], 16)

            def load_new_keys(j):
                if j:
                    sp.wait_ge(S["slogits"], j)
                with nc.allow_non_contiguous_dma(reason="one new key"):
                    for b in range(2):
                        sp.dma_start(ikt[64 * b:64 * b + 64, PAST:PAST + 1],
                                     proj[C_KI:C_WI, L + 2 * j + b:L + 2 * j + b + 1]).then_inc(S["ikn_in"], 16)

            sp.wait_ge(S["pages_in"], 16)
            load_index_keys(sp, 0, 0)
            load_new_keys(0)
            load_index_keys(sp, 1, 0)
            for s in range(2):
                load_main_half(B_MAIN + NX, s)
            load_index_keys(sp, 2, 0)
            load_new_keys(1)
            load_index_keys(sp, 3, 0)
            load_new_keys(2)
            load_new_keys(3)
            for s in range(2):
                load_main_half(B_MAIN + NX + 1, s)
            sp.wait_ge(S["srelu"], 1)
            sp.wait_ge(S["ssum"], 1)
            with nc.allow_non_contiguous_dma(reason="one scale a channel"):
                sp.dma_start(psc[:, :], pscale[0, :].rearrange("(c p) -> p c", p=128)).then_inc(S["state_in"], 16)
            sp.dma_start(strow[:, :], state[0].rearrange("b r c -> (b r) c")).then_inc(S["state_in"], 16)
            for b in range(NSAMP):
                sp.dma_start(io["new_pool_sample"][0, b, 0:PAD - 1, :], state[0, b, 1:PAD, :]).then_inc(S["outs"], 16)
            for s in range(2):
                load_main_half(B_MAIN + NX + 2, s)
            first = B_MAIN + NX + 3
            with sp.Fori(0, (B_OUT - first) // 2) as i:
                for n in (first, first + 1):
                    load_block(sp, n, w_in[0, :, bass.ds(i * 256 + 128 * (n - B_MAIN), 128)], i=i)
            sp.wait_ge(S["p_stored"], 16 * 4)
            sp.dma_start(spos[:, :], consts[:, K_S:K_ALL]).then_inc(S["spos_in"], 16)
            sp.dma_start(kin[:, :, :], proj[C_K:C_V, :].rearrange("(b p) t -> p b t", p=128)).then_inc(S["kin_in"], 16)
            sp.wait_ge(S["w_lo"], 2 * (B_OUT - 1))
            last = 128 * (NTILE - 1)
            sp.dma_start(vin[:, :, :], proj[C_V:C_ZA, 0:last].rearrange("(b p) t -> p b t", p=128)).then_inc(S["vin_in"], 16)
            sp.dma_start(vtail[:, :, :], proj[C_V:C_ZA, last:T].rearrange("(b p) t -> p b t", p=128)
                         ).then_inc(S["vin_in"], 16)
            sp.wait_ge(S["w_used"], 2 * B_OUT)

            def load_q(s):
                i = ATILES[s]
                c = cols_of(i)
                if s >= 2:
                    sp.wait_ge(S["aq_lo"], s - 1)
                sp.dma_start(qin[:, s % 2, :, 0:c], proj[C_Q:C_K, 128 * i:128 * i + c].rearrange("(h p) t -> p h t", p=128)
                             ).then_inc(S[f"aq_in{s % 2}"], 16)

            def load_z(s):
                i = ATILES[s]
                c = cols_of(i)
                sp.dma_start(zin[:, s % 2, :, 0:c], proj[C_ZA:C_QI, 128 * i:128 * i + c].rearrange("(h p) t -> p h t", p=128)
                             ).then_inc(S[f"az_in{s % 2}"], 16)

            load_q(0)
            load_q(1)
            for n in (B_OUT - 2, B_OUT - 1):
                sp.wait_ge(S[f"stored{parity(n)}"], 16 * uses(n))
            load_z(0)
            load_z(1)
            sp.wait_ge(S["kvtok_kept0"], (NTILE + 1) // 2)
            sp.wait_ge(S["kvtok_kept1"], NTILE // 2)
            for kv, name in ((0, "k"), (1, "v")):
                cols = slice(kv * KVH * HD, (kv + 1) * KVH * HD)
                sp.dma_start(io[f"new_{name}_prompt"][0, 0, 0:full].rearrange("(t p) g d -> p t (g d)", p=128),
                             kvtok[:, 0:NTILE - 1, cols]).then_inc(S["kv_out"], 16)
                sp.dma_start(io[f"new_{name}_prompt"][0, 0, full:L].rearrange("t g d -> t (g d)"),
                             kvtok[0:TAIL, NTILE - 1, cols]).then_inc(S["kv_out"], 16)
                sp.dma_start(io[f"new_{name}_sample"][0, :, 0].rearrange("b g d -> b (g d)"),
                             kvtok[TAIL:TAIL + NSAMP, NTILE - 1, cols]).then_inc(S["kv_out"], 16)
            sp.wait_ge(S["ak_lo"], 1)
            sp.wait_ge(S["knew_kept"], 1)
            sp.dma_start(vnew[0:1, :].rearrange("o (b c) -> o b c", b=NSAMP),
                         kvtok[TAIL:TAIL + NSAMP, NTILE - 1, KVH * HD:2 * KVH * HD]).then_inc(S["vnew_in"], 16)
            load_q(2)
            for u, (i, g) in enumerate(AUNITS):
                sp.wait_ge(S["gated"], u + 1)
                r = rows_of(i)
                sp.dma_start(mixt[POOLW + 512 * g:POOLW + 512 * g + 512, 128 * i:128 * i + r]
                             .rearrange("(h p) t -> p h t", p=128),
                             osb[:, u % 2, :, 0:r]).then_inc(S[f"o_stored{u % 2}"], 16)
                if g == 0 and u // KVH + 3 < NTILE:
                    load_q(u // KVH + 3)
                if g == KVH - 1 and u // KVH + 2 < NTILE:
                    load_z(u // KVH + 2)
                if 2 <= u < 8:
                    load_keys(sp, u - 2, 0)
                if u == len(AUNITS) - 2:
                    sp.wait_ge(S["p_turned"], blocks_to(len(AUNITS)))
                    for b in (6, 7):
                        load_keys(sp, b, 0)
                    for b in range(4):
                        load_values(sp, b, 0)
            for k in range(4):
                sp.dma_start(orow[:, k, :], mixt[128 * k:128 * k + 128, :]).then_inc(S[f"o_in{k}"], 16)
            load_values(sp, 4, 0)
            load_values(sp, 5, 0)
            load_block(sp, B_OUT, w_out[0, :, 0:128])
            load_block(sp, B_OUT + 1, w_out[0, :, 128:256])
            load_values(sp, 6, 0)
            load_values(sp, 7, 0)
            for k in range(4, KT):
                if k == POOLW // 128:
                    with nc.allow_non_contiguous_dma(reason="32-byte rows"):
                        sp.wait_ge(S["sgated"], 1)
                        sp.dma_start(mixt[POOLW:D, L:T].rearrange("(h p) t -> p h t", p=128), osamp[:, :, :]
                                     ).then_inc(S["os_stored"], 16)
                    sp.wait_ge(S["os_stored"], 16)
                    for p in range(2):
                        sp.wait_ge(S[f"o_stored{p}"], 16 * len(AUNITS[p::2]))
                sp.wait_ge(S["o_lo"], k - 3)
                sp.dma_start(orow[:, k % 4, :], mixt[128 * k:128 * k + 128, :]).then_inc(S[f"o_in{k % 4}"], 16)

            def load_x(n, c0, i=None):
                p = parity(n)
                add2 = 0 if i is None else 2 * i
                if n >= B_OUT + 2:
                    sp.wait_ge(S["h_added"], n - B_OUT - 1 + add2)
                x = xblk[:, p, :, :]
                s_ = S[f"xb_in{p}"]
                c = c0
                lo = 128 - META
                sp.dma_start(x[0:META, 0, :], meta[:, c]).then_inc(s_, 16)
                sp.dma_start(x[META:128, 0, :], xp[0, 0:lo, c]).then_inc(s_, 16)
                sp.dma_start(x[:, 1:NTILE - 1, :],
                             xp[0, lo:lo + 128 * (NTILE - 2), c].rearrange("(t p) d -> p t d", p=128)).then_inc(s_, 16)
                sp.dma_start(x[0:TAIL, NTILE - 1, :], xp[0, SEQ - TAIL:SEQ, c]).then_inc(s_, 16)
                sp.dma_start(x[TAIL:TAIL + NSAMP, NTILE - 1, :], xs_[:, 0, c]).then_inc(s_, 16)

            load_x(B_OUT, slice(0, 128))
            load_x(B_OUT + 1, slice(128, 256))
            with sp.Fori(0, NOUT // 2 - 1) as i:
                for r in range(2):
                    c = bass.ds(i * 256 + 256 + 128 * r, 128)
                    load_block(sp, B_OUT + 2 + r, w_out[0, :, c], i=i)
                    load_x(B_OUT + 2 + r, c, i=i)
            sp.wait_ge(S["o_lo"], KT)
            for p in range(2):
                sp.wait_ge(S[f"h_stored{p}"], 32 * (NOUT - 2) // 2)
            for t in FTILES:
                n = cols_of(t)
                if t == 0:
                    sp.wait_ge(S["w_lo"], 2 * (B_OUT + NOUT))
                if t == 5:
                    sp.wait_ge(S["w_used"], 2 * (B_OUT + NOUT) - 1)
                    sp.dma_start(fg[:, :], fin_g.partition_broadcast(128)).then_inc(S["fg_in"], 16)
                sp.dma_start(final_rows(t)[0:n, 0:KEPT], hbuf_d[128 * t:128 * t + n, 0:KEPT]).then_inc(S[f"fh_in{t}"], 16)

        @block.scalar
        def _(act):
            def turned_hi(i):
                for q in range(4):
                    act.wait_ge(S["x_turned"], 4 * i + q + 1)
                    c = cols_of(i)
                    nc.scalar.activation(ahi[:, 4 * q:4 * q + 4, 128 * i:128 * i + c],
                                         ps[:, TBANKS[q], :].rearrange("p (k t) -> p k t", k=4)[:, :, 0:c],
                                         ACT.Copy).then_inc(S["a_hi"], 1)

            for i in range(NTILE):
                n = cols_of(i)
                act.wait_ge(S[f"x_in{i % 3}"], 16 * sum(X_PARTS[i % 3:i + 1:3]))
                if i:
                    act.wait_ge(S["x_sqrt"], i)
                nc.scalar.activation(xsq[0:n, :], xt[0:n, i % 3, :], ACT.Square,
                                     accum_out=nst[0:n, 0, i:i + 1]).then_inc(S["x_sq"], 1)
                act.wait_ge(S["x_rms"], i + 1)
                nc.scalar.activation(nst[0:n, 3, i:i + 1], nst[0:n, 2, i:i + 1], ACT.Sqrt).then_inc(S["x_sqrt"], 1)
                if i:
                    turned_hi(i - 1)
                if i == 3:
                    split_hi(act, 0, 0, WIDTH0, first=True)
                    split_hi(act, 0, 1, WIDTH0, first=True)
            turned_hi(NTILE - 1)

            split_hi(act, 1, 0)
            evacuate(act, 0, WIDTH0, first=True)
            store_block(act, 0, proj[C_KI:DIN, :], WIDTH0)
            split_hi(act, 1, 1)

            def query_block(n, dst, i=None, first=False):
                split_hi(act, n + 1, 0, i=i)
                evacuate(act, n, i=i, first=first)
                store_block(act, n, dst, i=i)
                split_hi(act, n + 1, 1, i=i)

            query_block(1, proj[C_QI:C_QI + 128, :], first=True)
            query_block(2, proj[C_QI + 128:C_QI + 256, :])
            with act.Fori(0, NQI // 2 - 1) as i:
                for n in (3, 4):
                    query_block(n, proj[bass.ds(i * 256 + C_QI + 128 * (n - 1), 128), :], i=i)
            act.wait_ge(S["kiraw_in"], 32)
            nc.scalar.activation(khi[:, :], relub[:, :], ACT.Copy).then_inc(S["ki_hi"], 1)

            def query_hi(n):
                i = QUNITS[n][0]
                act.wait_ge(S["q_in"], 32 * (n + 1))
                if n >= 2:
                    act.wait_ge(S["logits"], 8 * (n - 1))
                c = cols_of(i)
                nc.scalar.activation(qst[:, n % 2, :, 0:c], qraw[:, :, 0:c], ACT.Copy).then_inc(S["q_hi"], 1)

            query_hi(0)
            act.wait_ge(S["ki_lo"], 1)
            for what, *x in indexer_order():
                if what == "step":
                    step_act(act, *x)
                    continue
                u = x[0]
                i = IUNITS[u][0]
                n, k = divmod(u, IH // 2)
                if k == 4 and n + 1 < len(QUNITS):
                    query_hi(n + 1)
                rows, w = rows_of(i), keys_of(i)
                act.wait_ge(S["logits"], u + 1)
                if u >= 2:
                    act.wait_ge(S["scored"], u - 1)
                o = logit_column(u, w)
                nc.scalar.activation(relu_of(u)[0:rows, 0:w], psf[0:rows, o:o + w], ACT.Relu).then_inc(S["relu_done"], 1)
            for what, *x in samples_order():
                if what == "step":
                    step_act(act, *x)
                if what == "turn":
                    j = x[0]
                    act.wait_ge(S["ik_turned"], j + 1)
                    if j:
                        act.wait_ge(S["slogits"], j)
                    nc.scalar.activation(ikt[:, 0:PAST], psf[:, 3072:3072 + PAST], ACT.Copy).then_inc(S["ik_copied"], 1)
            B_GRP = B_MAIN + 2 * (POOLW // 128)
            B_ZP = B_MAIN + POOLW // 128
            for n in range(B_MAIN + NX, B_ZP):
                split_hi(act, n + 1, 0)
                evacuate(act, n)
                store_block(act, n, proj[128 * (n - B_MAIN):128 * (n - B_MAIN) + 128, :])
                split_hi(act, n + 1, 1)
            with act.Fori(0, (B_GRP - B_ZP) // 2) as i:
                for n in (B_ZP, B_ZP + 1):
                    split_hi(act, n + 1, 0, i=i)
                    evacuate(act, n, i=i, func=ACT.Silu)
                    store_block(act, n, proj[bass.ds(i * 256 + 128 * (n - B_MAIN), 128), :], i=i)
                    split_hi(act, n + 1, 1, i=i)
            act.wait_ge(S["ul_turned"], 1)
            nc.scalar.activation(ulrow[:, :], psf[0:PAD + NSAMP, 3072:4096], ACT.Copy).then_inc(S["ul_kept"], 1)
            act.wait_ge(S["st_summed"], 1)
            nc.scalar.activation(sst[:, :, :], psf[:, 3072:3072 + 64].rearrange("p (c b) -> p c b", b=NSAMP),
                                 ACT.Copy).then_inc(S["st_kept"], 1)
            act.wait_ge(S["ul_kept"], 1)
            act.dma_start(io["new_pool_prompt"][0, 0, :, :], ulrow[0:PAD, :]).then_inc(S["ul_out"], 16)
            act.dma_start(io["new_pool_sample"][0, :, PAD - 1, :], ulrow[PAD:PAD + NSAMP, :]).then_inc(S["ul_out"], 16)

            def pool_group(g, i2, func, first=False):
                for q in range(4):
                    n = B_GRP + q
                    split_hi(act, n + 1, 0, i=i2)
                    evacuate(act, n, i=i2, func=func)
                    store_block(act, n, proj[bass.ds(g * 512 + 2 * POOLW + 128 * q, 128), :], i=i2)
                    split_hi(act, n + 1, 1, i=i2)
                    if q == 0:
                        if not first:
                            act.wait_ge(S["p_gated"], g)
                            act.wait_ge(S["p_stored"], g * 16)
                        act.wait_ge(S["ul_out"], 32)
                        nc.scalar.activation(psg[:, :], psc[:, bass.ds(g * 2, 2)], ACT.Copy).then_inc(S["psg_kept"], 1)
                        act.dma_start(pu[:, :, :], proj[bass.ds(g * GROUP, GROUP), :].rearrange("(c p) t -> p c t", p=128)
                                      ).then_inc(S["p_in"], 16)
                        act.dma_start(pz[:, :, :], proj[bass.ds(g * GROUP + C_ZP, GROUP), :]
                                      .rearrange("(c p) t -> p c t", p=128)).then_inc(S["p_in"], 16)
                        act.dma_start(pw[:, :, :], w_pool[0, bass.ds(g, 1), :, :].rearrange("o (c p) d -> p (o c) d", p=128)
                                      ).then_inc(S["p_in"], 16)
                act.wait_ge(S["psg_kept"], g + 1)
                for x in range(6):
                    m, c = divmod(x, 3)
                    t0, tn = CHUNKS[c]
                    act.wait_ge(S["p_mm"], g * 6 + x + 1)
                    nc.scalar.activation(pt[:, m, t0:t0 + tn], ps[:, 6 + x % 2, 0:tn], ACT.Identity,
                                         scale=psg[:, m:m + 1]).then_inc(S["p_scaled"], 1)

            groups = POOLW // GROUP
            pool_group(0, 0, ACT.Copy, first=True)
            with act.Fori(1, groups - 1) as g:
                pool_group(g, g * 2, ACT.Copy)
            for q in range(4):
                n = B_GRP + 4 * (groups - 1) + q
                split_hi(act, n + 1, 0)
                evacuate(act, n, func=ACT.Silu)
                r0 = (n - B_MAIN) * 128
                store_block(act, n, proj[r0:r0 + 128, :])
                split_hi(act, n + 1, 1)
                if q == 0:
                    g = groups - 1
                    act.wait_ge(S["p_gated"], g)
                    act.wait_ge(S["p_stored"], g * 16)
                    act.dma_start(pu[:, :, :], proj[g * GROUP:(g + 1) * GROUP, :].rearrange("(c p) t -> p c t", p=128)
                                  ).then_inc(S["p_in"], 16)
                    act.dma_start(pz[:, :, :], proj[C_ZP + g * GROUP:C_ZP + (g + 1) * GROUP, :]
                                  .rearrange("(c p) t -> p c t", p=128)).then_inc(S["p_in"], 16)
                    act.dma_start(pw[:, :, :], w_pool[0, g, :, :].rearrange("(c p) d -> p c d", p=128)
                                  ).then_inc(S["p_in"], 16)
            for x in range(6):
                m, c = divmod(x, 3)
                t0, tn = CHUNKS[c]
                act.wait_ge(S["p_mm"], g * 6 + x + 1)
                nc.scalar.activation(pt[:, m, t0:t0 + tn], ps[:, 6 + x % 2, 0:tn], ACT.Identity,
                                     scale=psc[:, g * 2 + m:g * 2 + m + 1]).then_inc(S["p_scaled"], 1)
            for n in range(B_GRP + 4 * groups, B_OUT):
                if n + 1 < B_OUT:
                    split_hi(act, n + 1, 0)
                evacuate(act, n, func=ACT.Silu)
                r0 = (n - B_MAIN) * 128
                store_block(act, n, proj[r0:r0 + 128, :])
                if n + 1 < B_OUT:
                    split_hi(act, n + 1, 1)

            act.wait_ge(S["kin_in"], 16)
            act.wait_ge(S["w_used"], 2 * B_OUT)
            nc.scalar.activation(akh[:, :, :], kin[:, :, 0:L], ACT.Copy).then_inc(S["ak_hi"], 1)

            def query_parts(s):
                act.wait_ge(S[f"aq_in{s % 2}"], 16 * (s // 2 + 1))
                if s >= 2:
                    act.wait_ge(S["aqk"], 8 * (s - 1))
                c = cols_of(ATILES[s])
                nc.scalar.activation(qh[:, s % 2, :, 0:c], qin[:, s % 2, :, 0:c], ACT.Copy,
                                     scale=HD ** -0.5).then_inc(S["aq_hi"], 1)

            query_parts(0)
            nc.scalar.activation(knew[:, :, :], kin[:, :, L:T], ACT.Copy).then_inc(S["knew_kept"], 1)
            for i in range(0, NTILE, 2):
                n = cols_of(i)
                act.wait_ge(S["kv_turned"], i + 1)
                nc.scalar.activation(kvtok[0:n, i, :], ps[0:n, i % 6, :], ACT.Copy).then_inc(S["kvtok_kept0"], 1)
            t = 0
            for k in range(NHEAD + LAG):
                for v, j in back_blocks(k):
                    i = AUNITS[v][0]
                    act.wait_ge(S["p_turned"], t + 1)
                    if t >= 2:
                        act.wait_ge(S["pv_mm"], t - 1)
                    kn = min(128, L - 128 * j)
                    w = 4 * rows_of(i)
                    nc.scalar.activation(pts[0:kn, t % 2, 0:w], ps[0:kn, 5 + t % 2, 0:w], ACT.Copy
                                         ).then_inc(S["pt_copied"], 1)
                    t += 1
                if k < NHEAD and k % (4 * KVH) == 4 * KVH - 3 and k // (4 * KVH) + 1 < NTILE:
                    query_parts(k // (4 * KVH) + 1)
                if 1 <= k <= NHEAD:
                    u, r = divmod(k - 1, 4)
                    n, w = rows_of(AUNITS[u][0]), keys_of(AUNITS[u][0])
                    act.wait_ge(S["amax"], k)
                    x = prob[0:n, u % NPROB, r, 0:w]
                    nc.scalar.activation(x, x, ACT.Exp, bias=ast[0:n, 0, u % NPROB, r:r + 1],
                                         accum_out=ast[0:n, 1, u % NPROB, r:r + 1]).then_inc(S["aexp"], 1)
                if k % 2 and 3 <= k < NHEAD + 2:
                    u, r = divmod(k - 2, 4)
                    n, w = rows_of(AUNITS[u][0]), keys_of(AUNITS[u][0])
                    act.wait_ge(S["inverse"], (k - 1) // 2)
                    x = prob[0:n, u % NPROB, r, 0:w]
                    nc.scalar.activation(x, x, ACT.Copy, scale=ast[0:n, 2, u % NPROB, r:r + 1]).then_inc(S["normed1"], 1)

            def operand_hi(k):
                act.wait_ge(S[f"o_in{k % 4}"], 16 * (k // 4 + 1))
                nc.scalar.activation(ohi[:, k, :], orow[:, k % 4, :], ACT.Copy).then_inc(S["o_hi"], 1)

            for m in range(NSAMP * KVH):
                b, g = divmod(m, KVH)
                act.wait_ge(S["sk_turned"], m + 1)
                if m == 0:
                    act.wait_ge(S["p_turned"], blocks_to(len(AUNITS)))
                if m >= 2:
                    act.wait_ge(S["sqk"], m - 1)
                nc.scalar.activation(skt[:, m % 2, :], psf[:, 2048 + 1024 * (m % 2):3072 + 1024 * (m % 2)],
                                     ACT.Copy).then_inc(S["sk_copied"], 1)
                if m == 8:
                    act.wait_ge(S["kv_out"], 16 * 6)
                    act.wait_ge(S["vnew_in"], 16)
                if m in (8, 10, 12, 14):
                    operand_hi((m - 8) // 2)
            act.wait_ge(S["smax"], 1)
            nc.scalar.activation(sprob[:, :], sprob[:, :], ACT.Exp, bias=sst64[:, 0:1],
                                 accum_out=sst64[:, 1:2]).then_inc(S["sexp"], 1)
            for s in range(2):
                split_hi(act, B_OUT, s)
            act.wait_ge(S["sp_turned"], 1)
            nc.scalar.activation(spt[:, 0:NPAGES, :], ps[:, 3, :].rearrange("p (j r) -> p j r", r=64), ACT.Copy)
            nc.scalar.activation(spt[0:1, NPAGES, :], ps[0:1, 4, 0:64], ACT.Copy).then_inc(S["spt_copied"], 1)
            for j in range(NSAMP // 2):
                act.wait_ge(S["sv_used"], 2 * j + 2)
                nc.scalar.activation(sout[:, j, :], ps[0:HEADS, SAMPLE_BANKS[j], :], ACT.Copy).then_inc(S["so_copied"], 1)
            act.wait_ge(S["so_turned"], NSAMP // 2)
            for k in range(4, KT):
                operand_hi(k)

            def squares(n, i=None):
                p = parity(n)
                add2 = 0 if i is None else 2 * i
                act.wait_ge(S["h_added"], n - B_OUT + 1 + add2)
                if n > B_OUT:
                    act.wait_ge(S["h_squared"], n - B_OUT + add2)
                for t in range(NTILE):
                    c = cols_of(t)
                    h = hblk[0:c, p, t, :]
                    if i is None and n >= B_OUT + NOUT - 2:
                        h = final_rows(t)[0:c, 128 * (n - B_OUT):128 * (n - B_OUT) + 128]
                    last = nc.scalar.activation(sqj[0:c, t, :], h, ACT.Square,
                                                accum_out=sq[0:c, p, t:t + 1])
                last.then_inc(S["h_squared"], 1)

            def store_h(n, c, i=None):
                p = parity(n)
                full = NTILE - 1
                act.dma_start(hbuf_d[0:128 * full, c].rearrange("(t p) d -> p t d", p=128),
                              hblk[:, p, 0:full, :]).then_inc(S[f"h_stored{p}"], 16)
                act.dma_start(hbuf_d[128 * full:T, c], hblk[0:T - 128 * full, p, full, :]
                              ).then_inc(S[f"h_stored{p}"], 16)

            def out_block(n, i=None, c=None):
                split_hi(act, n + 1, 0, i=i)
                evacuate(act, n, i=i, stored=False)
                split_hi(act, n + 1, 1, i=i)
                if c is not None:
                    squares(n - 1, i)
                    store_h(n - 1, c, i)

            out_block(B_OUT)
            out_block(B_OUT + 1, c=slice(0, 128))
            with act.Fori(0, NOUT // 2 - 2) as i:
                out_block(B_OUT + 2, i, bass.ds(i * 256 + 128, 128))
                out_block(B_OUT + 3, i, bass.ds(i * 256 + 256, 128))
            out_block(B_OUT + NOUT - 2, c=slice(D - 384, D - 256))
            n = B_OUT + NOUT - 1
            evacuate(act, n, stored=False)
            squares(n - 1)
            squares(n)
            act.wait_ge(S["f_rms"], 1)
            nc.scalar.activation(fst[:, 3, :], fst[:, 2, :], ACT.Sqrt).then_inc(S["f_sqrt"], 1)
            for at, i in enumerate(FTILES):
                act.wait_ge(S["f_done"], at + 1)
                for r0, n, _ in x_parts(i):
                    if i == 0 and r0 == 0:
                        continue
                    if i == NTILE - 1 and r0:
                        dst = io["y_sample"][:, 0, :]
                    else:
                        lo = 128 * i - META + r0
                        dst = io["y_prompt"][0, lo:lo + n, :]
                    act.dma_start(dst, final_rows(i)[r0:r0 + n, :]).then_inc(S["y_out"], 16)
            act.wait_ge(S["y_out"], 16 * (NTILE + 1))
            act.wait_ge(S["outs"], 16 * (3 + NSAMP))

        @block.vector
        def _(dve):
            tick = [0]

            def chain(ins):
                tick[0] += 1
                ins.then_inc(S["small"], 1)
                dve.wait_ge(S["small"], tick[0])

            dve.wait_ge(S["cst_in"], 16)

            def turned_lo(i):
                for q in range(4):
                    dve.wait_ge(S["a_hi"], 4 * i + q + 1)
                    c = cols_of(i)
                    out = slice(128 * i, 128 * i + c)
                    nc.vector.tensor_tensor(alo[:, 4 * q:4 * q + 4, out],
                                            ps[:, TBANKS[q], :].rearrange("p (k t) -> p k t", k=4)[:, :, 0:c],
                                            ahi[:, 4 * q:4 * q + 4, out].bitcast(F32),
                                            ALU.subtract).then_inc(S["a_lo"], 1)

            for i in range(NTILE):
                n = cols_of(i)
                col = [nst[0:n, r, i:i + 1] for r in range(6)]
                dve.wait_ge(S["x_sq"], i + 1)
                chain(nc.vector.tensor_scalar(col[1], col[0], 1.0 / D, EPS, ALU.mult, ALU.add))
                nc.vector.reciprocal(col[2], col[1]).then_inc(S["x_rms"], 1)
                dve.wait_ge(S["x_sqrt"], i + 1)
                chain(nc.vector.tensor_tensor(col[4], col[3], col[3], ALU.mult))
                chain(nc.vector.tensor_tensor(col[4], col[4], col[1], ALU.mult))
                chain(nc.vector.tensor_scalar(col[4], col[4], -0.5, 1.5, ALU.mult, ALU.add))
                chain(nc.vector.tensor_tensor(col[5], col[4], col[3], ALU.mult))
                if i == 0:
                    dve.wait_ge(S["g_in"], 16)
                x = xt[0:n, i % 3, 0:DSPLIT]
                nc.vector.scalar_tensor_tensor(out=x, in0=x, scalar=col[5], in1=gb[0:n, 0:DSPLIT], op0=ALU.mult,
                                               op1=ALU.mult).then_inc(S["x_scaled"], 1)
                if i:
                    turned_lo(i - 1)
                if i == 3:
                    for s in range(2):
                        split_lo(dve, 0, s, WIDTH0)
            turned_lo(NTILE - 1)
            for s in range(2):
                split_lo(dve, 1, s)
            nc.vector.memset(score[:, :], 0.0).then_inc(S["score_init"], 1)
            c = cols_of(NTILE - 1)
            chain(nc.vector.memset(kiw[:, NTILE - 1, :], 0.0))
            dve.wait_ge(S["kiw_turned"], 1)
            nc.vector.tensor_copy(kiw[:, 0:6, :], psf[:, 3072:3072 + 480].rearrange("p (t c) -> p t c", c=80))
            nc.vector.tensor_copy(kiw[:, 6:8, :], psf[:, 3584:3584 + 160].rearrange("p (t c) -> p t c", c=80))
            chain(nc.vector.tensor_copy(kiw[0:c, 8, :], psf[0:c, 3584 + 160:3584 + 240]))
            nc.vector.tensor_scalar(wsc[:, :, :], kiw[:, :, ID:ID + IH], ID ** -0.5 * IH ** -0.5, None,
                                    ALU.mult).then_inc(S["kiw_kept"], 1)
            with dve.Fori(0, NQI // 2) as i:
                for n in (2, 3):
                    for s in range(2):
                        split_lo(dve, n, s, i=i)

            dve.wait_ge(S["ki_hi"], 1)
            nc.vector.tensor_tensor(klo[:, :], relub[:, :], khi[:, :].bitcast(F32),
                                    ALU.subtract).then_inc(S["ki_lo"], 1)

            def query_lo(n):
                i, h = QUNITS[n]
                dve.wait_ge(S["q_hi"], n + 1)
                c = cols_of(i)
                if i == NTILE - 1:
                    nc.vector.tensor_copy(qlast[:, h, :, :], qraw[:, :, TAIL:TAIL + NSAMP])
                nc.vector.tensor_tensor(qst[64:128, n % 2, :, 0:c], qraw[64:128, :, 0:c],
                                        qst[64:128, n % 2, :, 0:c].bitcast(F32), ALU.subtract).then_inc(S["q_lo"], 1)

            query_lo(0)
            dve.wait_ge(S["score_init"], 1)
            for what, *x in indexer_order():
                if what == "step":
                    step_dve(dve, *x)
                    continue
                u = x[0]
                i, h, k = IUNITS[u]
                n = u // (IH // 2)
                if k == 4 and n + 1 < len(QUNITS):
                    query_lo(n + 1)
                rows = rows_of(i)
                dve.wait_ge(S["relu_done"], u + 1)
                if u:
                    dve.wait_ge(S["scored"], u)
                out = score_of(i)[0:rows, :]
                nc.vector.scalar_tensor_tensor(out=out, in0=relu_of(u)[0:rows, 0:keys_of(i)],
                                               scalar=wsc[0:rows, i, 8 * h + k:8 * h + k + 1], in1=out,
                                               op0=ALU.mult, op1=ALU.add).then_inc(S["scored"], 1)
            dve.wait_ge(S["logits"], len(IUNITS))
            chain(nc.vector.memset(qbd[:, :, :], 0.0))
            for b in range(NSAMP):
                r = 64 * (b % 2)
                for h in range(2):
                    last = nc.vector.tensor_copy(qbd[r:r + 64, b // 2, 16 * b + 8 * h:16 * b + 8 * h + 8],
                                                 qlast[r:r + 64, h, :, b])
                last.then_inc(S["qb_ready"], 1)
            def largest(count, tiles=TOPK_TILES):
                for m, t in enumerate(TOPK_TILES):
                    if t not in tiles:
                        continue
                    r = 128 if t < NTILE - 1 else 40
                    x = nc.vector.max(m8[0:r, m, :], score_of(t)[0:r, :])
                x.then_inc(S["maxed"], 1)
                dve.wait_ge(S["maxed"], count)

            def take(count, tiles=TOPK_TILES):
                for m, t in enumerate(TOPK_TILES):
                    if t not in tiles:
                        continue
                    r = 128 if t < NTILE - 1 else 40
                    x = nc.vector.match_replace(score_of(t)[0:r, :], m8[0:r, m, :], score_of(t)[0:r, :], NEG_TAKEN)
                x.then_inc(S["taken"], 1)
                dve.wait_ge(S["taken"], count)

            early = 0
            for what, *x in samples_order():
                if what == "sum":
                    break
                if what == "step":
                    step_dve(dve, *x)
                if what == "turn" and x[0] % 2 == 0:
                    dve.wait_ge(S["score_init"], 2)
                    early += 1
                    largest(early, TOPK_TILES[:-1])
                    take(early, TOPK_TILES[:-1])
            dve.wait_ge(S["slogits"], NSAMP // 2)
            dve.wait_ge(S["wcol_in"], 16 * NSAMP)
            nc.vector.tensor_scalar(rsc[:, :], psf[:, 1536:1536 + PAST + 1], 0.0, wcol[:, :], ALU.max,
                                    ALU.mult).then_inc(S["srelu"], 1)
            dve.wait_ge(S["ssum"], 1)
            last8 = score_of(NTILE - 1)
            nc.vector.tensor_scalar(last8[32:40, 0:PAST + 1], psf[32:40, 1536:1536 + PAST + 1],
                                    ID ** -0.5 * IH ** -0.5, None, ALU.mult).then_inc(S["ssum_kept"], 1)
            dve.wait_ge(S["ssum_kept"], 1)
            chain(nc.vector.memset(last8[32:40, PAST + 1:L], NEG_MASK))
            after = False
            for what, *x in samples_order():
                after = after or what == "sum"
                if after and what == "step":
                    step_dve(dve, *x)
            for r in range(early):
                largest(early + r + 1, TOPK_TILES[-1:])
                take(early + r + 1, TOPK_TILES[-1:])
            first = B_MAIN + NX + 1
            blocks = B_OUT - first
            assert early + blocks == ROUNDS and blocks % 2 == 0
            with dve.Fori(0, blocks // 2) as i:
                for q in range(2):
                    largest(2 * i + 2 * early + q + 1)
                    split_lo(dve, first + q, 0, i=i)
                    take(2 * i + 2 * early + q + 1)
                    split_lo(dve, first + q, 1, i=i)
            dve.wait_ge(S["spos_in"], 16)
            for t in TOPK_TILES:
                n = 128 if t < NTILE - 1 else 40
                x = score_of(t)[0:n, :]
                chain(nc.vector.tensor_scalar(x, x, (NEG_TAKEN + NEG_MASK) / 2, NEG_BIAS, ALU.is_gt, ALU.mult))
                chain(nc.vector.scalar_tensor_tensor(out=x, in0=x, scalar=cst[0:n, K_TQ + t:K_TQ + t + 1],
                                                     in1=spos[0:n, 0:keys_of(t)], op0=ALU.add, op1=ALU.add))
            for t in range(FIRST_TOPK):
                nc.vector.tensor_scalar(dist_of(t), spos[:, 0:keys_of(t)], cst[:, K_TQ + t:K_TQ + t + 1], None,
                                        ALU.add).then_inc(S["dist_made"], 1)
            dve.wait_ge(S["ak_hi"], 1)
            nc.vector.tensor_tensor(akl[:, :, :], kin[:, :, 0:L], akh[:, :, :].bitcast(F32),
                                    ALU.subtract).then_inc(S["ak_lo"], 1)

            def query_rest(s):
                dve.wait_ge(S["aq_hi"], s + 1)
                c = cols_of(ATILES[s])
                nc.vector.scalar_tensor_tensor(out=ql[:, s % 2, :, 0:c], in0=qin[:, s % 2, :, 0:c], scalar=HD ** -0.5,
                                               in1=qh[:, s % 2, :, 0:c].bitcast(F32), op0=ALU.mult,
                                               op1=ALU.subtract).then_inc(S["aq_lo"], 1)

            dve.wait_ge(S["aq_in0"], 16)
            nc.vector.tensor_scalar(qsamp[:, :, :], qin[:, 0, :, TAIL:TAIL + NSAMP], HD ** -0.5, None, ALU.mult)
            query_rest(0)
            for i in range(1, NTILE, 2):
                n = cols_of(i)
                dve.wait_ge(S["kv_turned"], i + 1)
                nc.vector.tensor_copy(kvtok[0:n, i, :], ps[0:n, i % 6, :]).then_inc(S["kvtok_kept1"], 1)
            dve.wait_ge(S["dist_masked"], FIRST_TOPK)

            def normalize(u, r):
                i, g = AUNITS[u]
                n, w = rows_of(i), keys_of(i)
                dve.wait_ge(S["aexp"], 4 * u + r + 1)
                inverse = nc.vector.reciprocal(ast[0:n, 2, u % NPROB, r:r + 1], ast[0:n, 1, u % NPROB, r:r + 1])
                if r % 2:
                    inverse.then_inc(S["inverse"], 1)
                    return
                chain(inverse)
                x = prob[0:n, u % NPROB, r, 0:w]
                nc.vector.tensor_scalar(x, x, ast[0:n, 2, u % NPROB, r:r + 1], None, ALU.mult).then_inc(S["normed0"], 1)

            def gate(u):
                i, g = AUNITS[u]
                n = rows_of(i)
                if g == 0:
                    dve.wait_ge(S[f"az_in{qbuf(u)}"], 16 * (u // KVH // 2 + 1))
                if u == 0:
                    nc.vector.tensor_copy(zsamp[:, :, :], zin[:, 0, :, TAIL:TAIL + NSAMP])
                dve.wait_ge(S["pv_mm"], blocks_to(u + 1))
                if u >= 2:
                    dve.wait_ge(S[f"o_stored{u % 2}"], 16 * (u // 2))
                nc.vector.tensor_tensor(osb[:, u % 2, :, 0:n],
                                        ps[:, out_bank(u), 0:4 * n].rearrange("p (h t) -> p h t", h=4),
                                        zin[:, qbuf(u), 4 * g:4 * g + 4, 0:n], ALU.mult).then_inc(S["gated"], 1)

            for k in range(NHEAD):
                u, r = divmod(k, 4)
                i, g = AUNITS[u]
                n, w = rows_of(i), keys_of(i)
                dve.wait_ge(S["aqk"], k + 1)
                if u >= NPROB and r == 0:
                    dve.wait_ge(S["p_turned"], blocks_to(u - NPROB + 1))
                x = prob[0:n, u % NPROB, r, 0:w]
                o = score_bank(k, w)
                nc.vector.scalar_tensor_tensor(out=x, in0=dist_of(i)[0:n, :], scalar=2.0 ** -(4 * g + r + 1),
                                               in1=psf[0:n, o:o + w], op0=ALU.mult, op1=ALU.add
                                               ).then_inc(S["abias"], 1)
                dve.wait_ge(S["abias"], k + 1)
                chain(nc.vector.tensor_reduce(ast[0:n, 0, u % NPROB, r:r + 1], x, AX.X, ALU.max))
                nc.vector.tensor_scalar(ast[0:n, 0, u % NPROB, r:r + 1], ast[0:n, 0, u % NPROB, r:r + 1], -1.0, None,
                                        ALU.mult).then_inc(S["amax"], 1)
                if k >= 2:
                    normalize(*divmod(k - 2, 4))
                if g == KVH - 1 and r == 2 and u // KVH + 1 < NTILE:
                    query_rest(u // KVH + 1)
                if r == 0 and u >= 3:
                    gate(u - 3)
            normalize(len(AUNITS) - 1, 2)
            normalize(len(AUNITS) - 1, 3)
            gate(len(AUNITS) - 3)
            gate(len(AUNITS) - 2)
            dve.wait_ge(S["p_turned"], blocks_to(len(AUNITS)))
            chain(nc.vector.memset(qz[:, :, :], 0.0))
            for m in range(NSAMP * KVH):
                b, g = divmod(m, KVH)
                x = nc.vector.tensor_copy(qz[:, m, 8 * b + 4 * g:8 * b + 4 * g + 4], qsamp[:, 4 * g:4 * g + 4, b])
            x.then_inc(S["qz_made"], 1)
            gate(len(AUNITS) - 1)
            dve.wait_ge(S["sdist"], 1)
            nc.vector.tensor_scalar(sbias[:, :], psf[0:64, 0:PAST + 1], cst[0:64, K_SLOPE:K_SLOPE + 1], None,
                                    ALU.mult).then_inc(S["sbias_made"], 1)

            def operand_lo(k):
                dve.wait_ge(S["o_hi"], k + 1)
                nc.vector.tensor_tensor(olo[:, k, :], orow[:, k % 4, :], ohi[:, k, :].bitcast(F32),
                                        ALU.subtract).then_inc(S["o_lo"], 1)

            for k in range(4):
                operand_lo(k)
            dve.wait_ge(S["sqk"], NSAMP * KVH)
            dve.wait_ge(S["sbias_made"], 1)
            chain(nc.vector.tensor_tensor(sprob[:, :], psf[0:64, 0:PAST + 1], sbias[:, :], ALU.add))
            chain(nc.vector.tensor_reduce(sst64[:, 0:1], sprob[:, :], AX.X, ALU.max))
            nc.vector.tensor_scalar(sst64[:, 0:1], sst64[:, 0:1], -1.0, None, ALU.mult).then_inc(S["smax"], 1)
            dve.wait_ge(S["sexp"], 1)
            chain(nc.vector.reciprocal(sst64[:, 2:3], sst64[:, 1:2]))
            nc.vector.tensor_scalar(sprob[:, :], sprob[:, :], sst64[:, 2:3], None, ALU.mult).then_inc(S["snormed"], 1)
            for s in range(2):
                split_lo(dve, B_OUT, s)
            dve.wait_ge(S["so_turned"], NSAMP // 2)
            for g in range(KVH):
                heads = slice(4 * g, 4 * g + 4)
                turned = ps[:, 6, 0:KVH * HEADS * NSAMP].rearrange("p (b x) -> p b x", b=NSAMP)
                last = nc.vector.tensor_tensor(osamp[:, heads, :].rearrange("p h b -> p b h"),
                                               turned[:, :, HEADS * g + 4 * g:HEADS * g + 4 * g + 4],
                                               zsamp[:, heads, :].rearrange("p h b -> p b h"), ALU.mult)
            last.then_inc(S["sgated"], 1)
            for k in range(4, KT):
                operand_lo(k)
            chain(nc.vector.memset(fst[:, 0, :], 0.0))

            def add_residual(n, part, i=None):
                p = parity(n)
                add1, add2 = (0, 0) if i is None else (i, 2 * i)
                if part == 0:
                    dve.wait_ge(S["h_turned"], 2 * (n - B_OUT) + 1 + 2 * add2)
                    dve.wait_ge(S[f"xb_in{p}"], 80 * ((n - B_OUT) // 2 + 1) + 80 * add1)
                    if n >= B_OUT + 2:
                        dve.wait_ge(S[f"h_stored{p}"], 32 * ((n - B_OUT) // 2) + 32 * add1)
                    nc.vector.tensor_tensor(hblk[:, p, 0:8, :], psf[:, 3072:4096].rearrange("p (t c) -> p t c", c=128),
                                            xblk[:, p, 0:8, :], ALU.add).then_inc(S["h_part"], 1)
                else:
                    dve.wait_ge(S["h_turned"], 2 * (n - B_OUT) + 2 + 2 * add2)
                    c = cols_of(NTILE - 1)
                    nc.vector.tensor_tensor(hblk[0:c, p, NTILE - 1, :], ps[0:c, 6, 0:128], xblk[0:c, p, NTILE - 1, :],
                                            ALU.add).then_inc(S["h_added"], 1)

            def add_last(n, part):
                p = parity(n)
                cols = slice(128 * (n - B_OUT), 128 * (n - B_OUT) + 128)
                dve.wait_ge(S["h_turned"], 2 * (n - B_OUT) + 1 + part)
                if part == 0:
                    dve.wait_ge(S[f"xb_in{p}"], 80 * ((n - B_OUT) // 2 + 1))
                    dve.wait_ge(S["w_used"], 2 * (B_OUT + NOUT) - 1)
                    for first, count, place in FPLACES:
                        count = min(count, NTILE - 1 - first)
                        o = 3072 + 128 * first
                        last = nc.vector.tensor_tensor(place[:, 0:count, cols],
                                                       psf[:, o:o + 128 * count].rearrange("p (t c) -> p t c", c=128),
                                                       xblk[:, p, first:first + count, :], ALU.add)
                    last.then_inc(S["h_part"], 1)
                else:
                    c = cols_of(NTILE - 1)
                    nc.vector.tensor_tensor(final_rows(NTILE - 1)[0:c, cols], ps[0:c, 6, 0:128],
                                            xblk[0:c, p, NTILE - 1, :], ALU.add).then_inc(S["h_added"], 1)

            def add_squares(n, i=None):
                p = parity(n)
                add2 = 0 if i is None else 2 * i
                dve.wait_ge(S["h_squared"], n - B_OUT + 1 + add2)
                nc.vector.tensor_tensor(fst[:, 0, 0:8], fst[:, 0, 0:8], sq[:, p, 0:8], ALU.add)
                c = cols_of(NTILE - 1)
                nc.vector.tensor_tensor(fst[0:c, 0, 8:9], fst[0:c, 0, 8:9], sq[0:c, p, 8:9], ALU.add
                                        ).then_inc(S["sq_added"], 1)
                dve.wait_ge(S["sq_added"], n - B_OUT + 1 + add2)

            def out_block(n, i=None):
                split_lo(dve, n + 1, 0, i=i)
                if n > B_OUT:
                    add_residual(n - 1, 0, i)
                split_lo(dve, n + 1, 1, i=i)
                if n > B_OUT:
                    add_residual(n - 1, 1, i)
                if n > B_OUT + 1:
                    add_squares(n - 2, i)

            for n in range(B_OUT, B_OUT + 4):
                out_block(n)
            with dve.Fori(0, (NOUT - 6) // 2) as i:
                out_block(B_OUT + 4, i)
                out_block(B_OUT + 5, i)
            n = B_OUT + NOUT - 2
            out_block(n)
            for n in (n, n + 1):
                add_last(n, 0)
                add_last(n, 1)
                add_squares(n - 1)
            add_squares(n)
            col = [fst[:, r, :] for r in range(6)]
            chain(nc.vector.tensor_scalar(col[1], col[0], 1.0 / D, EPS, ALU.mult, ALU.add))
            nc.vector.reciprocal(col[2], col[1]).then_inc(S["f_rms"], 1)
            dve.wait_ge(S["f_sqrt"], 1)
            chain(nc.vector.tensor_tensor(col[4], col[3], col[3], ALU.mult))
            chain(nc.vector.tensor_tensor(col[4], col[4], col[1], ALU.mult))
            chain(nc.vector.tensor_scalar(col[4], col[4], -0.5, 1.5, ALU.mult, ALU.add))
            chain(nc.vector.tensor_tensor(col[5], col[4], col[3], ALU.mult))
            dve.wait_ge(S["fg_in"], 16)
            for i in FTILES:
                n = cols_of(i)
                dve.wait_ge(S[f"fh_in{i}"], 16)
                x = final_rows(i)[0:n, :]
                nc.vector.scalar_tensor_tensor(out=x, in0=x, scalar=fst[0:n, 5, i:i + 1],
                                               in1=fg[0:n, :], op0=ALU.mult, op1=ALU.mult).then_inc(S["f_done"], 1)

        @block.tensor
        def _(pe):
            pe.wait_ge(S["cst_in"], 16)
            for i in range(NTILE):
                pe.wait_ge(S["x_scaled"], i + 1)
                n = cols_of(i)
                for q in range(4):
                    if 512 * (q + 1) > DSPLIT >= 512 * q:
                        pe.wait_ge(S["x_scaled_rest"], i + 1)
                    if i:
                        pe.wait_ge(S["a_lo"], 4 * (i - 1) + q + 1)
                    for k in range(4):
                        last = nc.tensor.transpose(ps[:, TBANKS[q], 128 * k:128 * k + n],
                                                   xt[0:n, i % 3, 128 * (4 * q + k):128 * (4 * q + k) + 128],
                                                   ident[0:n, 0:n])
                    last.then_inc(S["x_turned"], 1)
                if i == 3:
                    pe.wait_ge(S["w_lo"], 2)
                if i in EARLY:
                    c, first, end = EARLY[i]
                    if i % 3 == 0:
                        pe.wait_ge(S["a_lo"], 4 * i)
                    for a in range(first, end):
                        step(0, a, WIDTH0, chunks=[c])
            pe.wait_ge(S["a_lo"], 4 * NTILE)
            for a in range(KT):
                last = step(0, a, WIDTH0, chunks=[2])
                if a % HALF == HALF - 1:
                    last.then_inc(S["w_used"], 1)
            project(pe, 1, first=True)
            pe.wait_ge(S["evac"], 1)
            for i in range(NTILE):
                n = cols_of(i)
                at = 3072 + 80 * i if i < 6 else 3584 + 80 * (i - 6)
                last = nc.tensor.transpose(psf[0:n, at:at + WIDTH0], stage[0:WIDTH0, 1, 128 * i:128 * i + n],
                                           ident[0:WIDTH0, 0:WIDTH0])
            last.then_inc(S["kiw_turned"], 1)
            project(pe, 2)
            with pe.Fori(0, NQI // 2 - 1) as i:
                project(pe, 3, i=i)
                project(pe, 4, i=i)
            for what, *x in indexer_order():
                if what == "step":
                    step_among(pe, *x)
                    continue
                u = x[0]
                i = IUNITS[u][0]
                n, k = divmod(u, IH // 2)
                rows, w = rows_of(i), keys_of(i)
                if k == 0:
                    pe.wait_ge(S["q_lo"], n + 1)
                if u == 0:
                    pe.wait_ge(S["evac"], B_MAIN)
                    pe.wait_ge(S["ki_lo"], 1)
                if u >= 2:
                    pe.wait_ge(S["relu_done"], u - 1)
                o = logit_column(u, w)
                if o % BANK:
                    whole, rest = [(w % BANK + BANK * b, BANK) for b in range(w // BANK)], [(0, w % BANK)]
                else:
                    whole = [x for x in banks(w) if x[0] < 2 * BANK]
                    rest = [x for x in banks(w) if x[0] >= 2 * BANK]
                for part in (whole, rest):
                    if part is rest and rest:
                        pe.wait_ge(S["relu_done"], u)
                    for m in (khi, klo):
                        for c, cw in part:
                            last = nc.tensor.matmul(psf[0:rows, o + c:o + c + cw], qst[:, n % 2, k, 0:rows], m[:, c:c + cw],
                                                    start=m is khi, stop=m is klo)
                last.then_inc(S["logits"], 1)
            for what, *x in samples_order():
                if what == "step":
                    step_among(pe, *x)
                if what == "turn":
                    j = x[0]
                    for half in range(2):
                        pe.wait_ge(S[f"ik{half}_in{j % 2}"], 16 * NPAGES * (j // 2 + 1))
                    if j == 0:
                        pe.wait_ge(S["relu_done"], len(IUNITS))
                    else:
                        pe.wait_ge(S["ik_copied"], j)
                    for k in range(NPAGES):
                        last = nc.tensor.transpose(psf[:, 3072 + 128 * k:3072 + 128 * k + 128],
                                                   iload[:, j % 2, k, :, :].rearrange("p b d -> p (b d)"), ident)
                    last.then_inc(S["ik_turned"], 1)
                if what == "logit":
                    j = x[0]
                    pe.wait_ge(S["ik_copied"], j + 1)
                    pe.wait_ge(S["ikn_in"], 32 * (j + 1))
                    if j == 0:
                        pe.wait_ge(S["qb_ready"], 8)
                    for c, w in banks(PAST + 1):
                        last = nc.tensor.matmul(psf[:, 1536 + c:1536 + c + w], qbd[:, j, :], ikt[:, c:c + w],
                                                start=j == 0, stop=j == NSAMP // 2 - 1)
                    last.then_inc(S["slogits"], 1)
                if what == "sum":
                    pe.wait_ge(S["srelu"], 1)
                    for c, w in banks(PAST + 1):
                        last = nc.tensor.matmul(psf[32:40, 1536 + c:1536 + c + w], cst[:, K_ONEB:K_ONEB + 8], rsc[:, c:c + w],
                                                start=True, stop=True)
                    last.then_inc(S["ssum"], 1)
            pe.wait_ge(S["ssum_kept"], 1)
            B_ZP = B_MAIN + POOLW // 128
            for n in range(B_MAIN + NX, B_ZP):
                project(pe, n)
            with pe.Fori(0, POOLW // 256) as i:
                project(pe, B_ZP, i=i)
                project(pe, B_ZP + 1, i=i)
            pe.wait_ge(S["ul_in"], 16 * (POOLW // GROUP))
            for c in range(POOLW // 128):
                last = nc.tensor.transpose(psf[0:PAD + NSAMP, 3072 + 128 * c:3072 + 128 * c + 128], ulast[:, c, :], ident)
            last.then_inc(S["ul_turned"], 1)
            pe.wait_ge(S["state_in"], 32)
            pe.wait_ge(S["ul_kept"], 1)
            rows = NSAMP * PAD
            for c in range(POOLW // 128):
                g = c // 2
                last = nc.tensor.matmul(ps[:, 6, 8 * c:8 * c + 8], strow[:, 128 * c:128 * c + 128],
                                        cst[0:rows, K_STATE + 8 * g:K_STATE + 8 * g + 8], start=True, stop=True)
            last.then_inc(S["st_summed"], 1)
            B_GRP = B_MAIN + 2 * (POOLW // 128)
            with pe.Fori(0, POOLW // GROUP) as g:
                for q in range(4):
                    project(pe, B_GRP + q, i=g * 2)
                pe.wait_ge(S["p_mixed"], g + 1)
                pe.wait_ge(S["p_in"], g * 48 + 48)
                for x in range(6):
                    m, c = divmod(x, 3)
                    t0, tn = CHUNKS[c]
                    if x < 2:
                        pe.wait_ge(S["st_kept"], 1)
                    else:
                        pe.wait_ge(S["p_scaled"], g * 6 + x - 1)
                    for k in range(2):
                        last = nc.tensor.matmul(ps[:, 6 + x % 2, 0:tn], pw[:, k, 128 * m:128 * m + 128],
                                                pu[:, k, t0:t0 + tn], start=k == 0, stop=k == 1)
                    last.then_inc(S["p_mm"], 1)
            with pe.Fori(0, (B_OUT - B_GRP - 16) // 2) as i:
                project(pe, B_GRP + 16, i=i)
                project(pe, B_GRP + 17, i=i)
            pe.wait_ge(S["kin_in"], 16)
            pe.wait_ge(S["vin_in"], 32)
            for i in range(NTILE):
                n = cols_of(i)
                if i == 0:
                    pe.wait_ge(S["evac"], B_OUT - 1)
                if i == 3:
                    pe.wait_ge(S["evac"], B_OUT)
                if i >= 6:
                    pe.wait_ge(S[f"kvtok_kept{i % 2}"], (i - 6) // 2 + 1)
                for b in range(2 * KVH):
                    at = slice(128 * i, 128 * i + n)
                    src = kin[:, b, at] if b < KVH else vin[:, b - KVH, at] if i < NTILE - 1 else vtail[:, b - KVH, :]
                    last = nc.tensor.transpose(ps[0:n, i % 6, 128 * b:128 * b + 128], src, ident)
                last.then_inc(S["kv_turned"], 1)
            pe.wait_ge(S["kvtok_kept0"], (NTILE + 1) // 2)
            pe.wait_ge(S["kvtok_kept1"], NTILE // 2)
            pe.wait_ge(S["ak_lo"], 1)
            pe.wait_ge(S["p_scaled"], 24)

            def scores(k):
                u, r = divmod(k, 4)
                i, g = AUNITS[u]
                n, w = rows_of(i), keys_of(i)
                if g == 0 and r == 0:
                    pe.wait_ge(S["aq_lo"], u // KVH + 1)
                if k >= 2:
                    pe.wait_ge(S["abias"], k - 1)
                o = score_bank(k, w)
                pieces = banks(w) if o % BANK == 0 else [(BANK * b + w % BANK, BANK) for b in range(w // BANK)]
                rest = [x for x in pieces if x[1] < BANK] if w > 2 * BANK else []
                if o % BANK:
                    rest = [(0, w % BANK)]
                for part in ([x for x in pieces if x not in rest], rest):
                    if part is rest and rest and k:
                        pe.wait_ge(S["abias"], k)
                    for q, m in ((qh, akh), (qh, akl), (ql, akh)):
                        for c, cw in part:
                            last = nc.tensor.matmul(psf[0:n, o + c:o + c + cw], q[:, qbuf(u), 4 * g + r, 0:n],
                                                    m[:, g, c:c + cw], start=m is akh and q is qh, stop=q is ql)
                last.then_inc(S["aqk"], 1)

            def weighted(t, v, j):
                i, g = AUNITS[v]
                n = rows_of(i)
                kn = min(128, L - 128 * j)
                pe.wait_ge(S["pt_copied"], t + 1)
                if j == 0 and v > 1:
                    pe.wait_ge(S["gated"], v - 1)
                if j == 0 and v == 1:
                    pe.wait_ge(S["abias"], 4 * KVH)
                nc.tensor.matmul(ps[:, out_bank(v), 0:4 * n], kvtok[0:kn, j, 256 + 128 * g:256 + 128 * g + 128],
                                 pts[0:kn, t % 2, 0:4 * n], start=j == 0, stop=j == i).then_inc(S["pv_mm"], 1)

            t, waiting = 0, None
            for k in range(NHEAD + LAG):
                if k < NHEAD:
                    scores(k)
                if waiting:
                    weighted(*waiting)
                    waiting = None
                for v, j in back_blocks(k):
                    i, g = AUNITS[v]
                    n = rows_of(i)
                    kn = min(128, L - 128 * j)
                    if j == 0:
                        pe.wait_ge(S["normed0"], 2 * v + 2)
                        pe.wait_ge(S["normed1"], 2 * v + 2)
                    if t >= 2:
                        pe.wait_ge(S["pt_copied"], t - 1)
                    for h in range(4):
                        last = nc.tensor.transpose(ps[0:kn, 5 + t % 2, n * h:n * h + n],
                                                   prob[0:n, v % NPROB, h, 128 * j:128 * j + kn], ident[0:n, 0:n])
                    last.then_inc(S["p_turned"], 1)
                    if waiting:
                        weighted(*waiting)
                    waiting = (t, v, j)
                    t += 1
            if waiting:
                weighted(*waiting)

            pe.wait_ge(S["abias"], NHEAD)
            pe.wait_ge(S["pt_copied"], blocks_to(len(AUNITS)))
            for m in range(NSAMP * KVH + 1):
                if m < NSAMP * KVH:
                    b, g = divmod(m, KVH)
                    if g == 0 and b in (0, 6):
                        for half in range(2):
                            pe.wait_ge(S[f"ck_in{half}"], 8 * NPAGES * (6 if b == 0 else NSAMP))
                    if m == 1:
                        pe.wait_ge(S["gated"], len(AUNITS))
                        for c, w in banks(PAST + 1):
                            last = nc.tensor.matmul(psf[0:64, c:c + w], cst[32:40, K_ESEL:K_ESEL + 64],
                                                    score_of(NTILE - 1)[32:40, c:c + w], start=True, stop=True)
                        last.then_inc(S["sdist"], 1)
                    if m >= 2:
                        pe.wait_ge(S["sk_copied"], m - 1)
                    for k in range(NPAGES):
                        o = 2048 + 1024 * (m % 2) + 128 * k
                        last = nc.tensor.transpose(psf[:, o:o + 128], key_slot(b)[:, k, 128 * g:128 * g + 128], ident)
                    last.then_inc(S["sk_turned"], 1)
                if m == 1:
                    pe.wait_ge(S["qz_made"], 1)
                    pe.wait_ge(S["sbias_made"], 1)
                    pe.wait_ge(S["knew_kept"], 1)
                if m:
                    b, g = divmod(m - 1, KVH)
                    pe.wait_ge(S["sk_copied"], m)
                    q = qz[:, m - 1, :]
                    for c, w in banks(PAST):
                        nc.tensor.matmul(psf[0:64, c:c + w], q, skt[:, (m - 1) % 2, c:c + w], start=m == 1,
                                         stop=m == NSAMP * KVH)
                    nc.tensor.matmul(psf[0:64, PAST:PAST + 1], q, knew[:, g, b:b + 1], start=m == 1,
                                     stop=m == NSAMP * KVH).then_inc(S["sqk"], 1)
            pe.wait_ge(S["snormed"], 1)
            for k in range(NPAGES):
                nc.tensor.transpose(ps[:, 3, 64 * k:64 * k + 64], sprob[:, 128 * k:128 * k + 128], ident[0:64, 0:64])
            nc.tensor.transpose(ps[0:1, 4, 0:64], sprob[:, PAST:PAST + 1], ident[0:64, 0:64]).then_inc(S["sp_turned"], 1)
            pe.wait_ge(S["spt_copied"], 1)
            pe.wait_ge(S["vnew_in"], 16)

            def turn_samples(j):
                pe.wait_ge(S["so_copied"], j + 1)
                for x in range(2 * KVH):
                    o = HEADS * (2 * KVH * j + x)
                    last = nc.tensor.transpose(ps[:, 6, o:o + HEADS], sout[:, j, 128 * x:128 * x + 128],
                                               ident[0:HEADS, 0:HEADS])
                last.then_inc(S["so_turned"], 1)

            for b in range(NSAMP):
                for half in range(2):
                    if b == 0:
                        pe.wait_ge(S[f"cv_in{half}"], 16 * 4 * NPAGES // 2)
                    if b >= 4:
                        pe.wait_ge(S[f"cv{half}_in{b}"], 16 * NPAGES // 2)
                o = HEADS * b
                for k in range(NPAGES):
                    nc.tensor.matmul(sample_out(b), spt[:, k, o:o + HEADS],
                                     value_slot(b)[:, k, :], start=k == 0, stop=False)
                nc.tensor.matmul(sample_out(b), spt[0:1, NPAGES, o:o + HEADS], vnew[0:1, 256 * b:256 * b + 256],
                                 start=False, stop=True).then_inc(S["sv_used"], 1)
                if b >= 2 and b % 2 == 0:
                    turn_samples(b // 2 - 1)
            turn_samples(NSAMP // 2 - 1)

            def turn_h(n, part, i=None):
                p = parity(n)
                add2 = 0 if i is None else 2 * i
                if part == 0:
                    pe.wait_ge(S["evac"], n + 1 + add2)
                    if n > B_OUT:
                        pe.wait_ge(S["h_added"], n - B_OUT + add2)
                    else:
                        pe.wait_ge(S["sgated"], 1)
                    for t in range(NTILE - 1):
                        last = nc.tensor.transpose(psf[:, 3072 + 128 * t:3200 + 128 * t],
                                                   stage[:, p, 128 * t:128 * t + 128], ident)
                else:
                    pe.wait_ge(S["h_part"], n - B_OUT + 1 + add2)
                    c = cols_of(NTILE - 1)
                    last = nc.tensor.transpose(ps[0:c, 6, 0:128], stage[:, p, T - c:T], ident)
                last.then_inc(S["h_turned"], 1)

            def project_out(n, i=None, before=True):
                project(pe, n, i=i, src=(ohi, olo), first_out=n == B_OUT and i is None,
                        between=(lambda: turn_h(n - 1, 0, i)) if before else None)
                if before:
                    turn_h(n - 1, 1, i)

            project_out(B_OUT, before=False)
            project_out(B_OUT + 1)
            with pe.Fori(0, NOUT // 2 - 1) as i:
                project_out(B_OUT + 2, i)
                project_out(B_OUT + 3, i)
            turn_h(B_OUT + NOUT - 1, 0)
            turn_h(B_OUT + NOUT - 1, 1)

        @block.gpsimd
        def _(pool):
            tick = [0]

            def chain(ins):
                tick[0] += 1
                ins.then_inc(S["pool_step"], 1)
                pool.wait_ge(S["pool_step"], tick[0])

            for i in range(NTILE):
                n = cols_of(i)
                pool.wait_ge(S[f"x_in{i % 3}"], 16 * sum(X_PARTS[i % 3:i + 1:3]))
                if i == 0:
                    pool.wait_ge(S["g_in"], 16)
                pool.wait_ge(S["small"], 5 * (i + 1))
                x = xt[0:n, i % 3, DSPLIT:D]
                chain(nc.gpsimd.tensor_scalar(x, x, nst[0:n, 5, i:i + 1], None, ALU.mult))
                nc.gpsimd.tensor_tensor(x, x, gb[0:n, DSPLIT:D], ALU.mult).then_inc(S["x_scaled_rest"], 1)
            pool.wait_ge(S["pages_in"], 16)
            for j in range(2):
                load_index_keys(pool, j, 1)
            pool.wait_ge(S["scored"], len(TOPK_TILES) * IH)
            for i in TOPK_TILES:
                x = score_of(i)[0:rows_of(i), :]
                last = nc.gpsimd.affine_select(out=x, in_=x, compare_op=ALU.is_ge, fill=NEG_MASK, base=128 * i,
                                               pattern=[[-1, keys_of(i)]], channel_multiplier=1)
            last.then_inc(S["score_init"], 1)
            for j in range(2, NSAMP // 2):
                load_index_keys(pool, j, 1)
            for n in (B_MAIN + POOLW // 128 - 2, B_MAIN + POOLW // 128 - 1):
                pool.wait_ge(S[f"stored{parity(n)}"], 16 * uses(n))
            pool.wait_ge(S["srelu"], 1)
            pool.wait_ge(S["ssum"], 1)
            for g in range(POOLW // GROUP):
                pool.dma_start(ulast[:, 2 * g:2 * g + 2, :],
                               proj[GROUP * g:GROUP * g + GROUP, L - PAD:T].rearrange("(c p) t -> p c t", p=128)
                               ).then_inc(S["ul_in"], 16)
            for g in range(POOLW // GROUP):
                w = 2 << g
                pool.wait_ge(S["p_in"], 48 * (g + 1))
                pool.wait_ge(S["st_kept"], 1)
                for c in range(2):
                    u = pu[:, c, :]
                    a, b = pt[:, 0, :], pt[:, 1, :]
                    src, dst, step = u, a, 1
                    while step < w:
                        nc.gpsimd.tensor_copy(dst[:, 0:step], src[:, 0:step])
                        chain(nc.gpsimd.tensor_tensor(dst[:, step:L], src[:, step:L], src[:, 0:L - step], ALU.add))
                        src, dst, step = dst, (b if dst is a else a), 2 * step
                    nc.gpsimd.tensor_tensor(src[:, 0:16], src[:, 0:16], cst[:, K_CINV + 16 * g:K_CINV + 16 * g + 16], ALU.mult)
                    nc.gpsimd.tensor_scalar(src[:, 16:L], src[:, 16:L], 1.0 / w, None, ALU.mult)
                    chain(nc.gpsimd.tensor_tensor(dst[:, 0:NSAMP], sst[:, 2 * g + c, :], u[:, L:T], ALU.add))
                    chain(nc.gpsimd.tensor_scalar(dst[:, 0:NSAMP], dst[:, 0:NSAMP], 1.0 / w, None, ALU.mult))
                    nc.gpsimd.tensor_tensor(u[:, 0:L], src[:, 0:L], u[:, 0:L], ALU.subtract)
                    chain(nc.gpsimd.tensor_tensor(u[:, L:T], dst[:, 0:NSAMP], u[:, L:T], ALU.subtract))
                nc.gpsimd.engine_nop().then_inc(S["p_mixed"], 1)
                pool.wait_ge(S["p_scaled"], 6 * (g + 1))
                nc.gpsimd.tensor_tensor(pz[:, :, :], pz[:, :, :], pt[:, :, :], ALU.mult).then_inc(S["p_gated"], 1)
                pool.wait_ge(S["p_gated"], g + 1)
                pool.dma_start(mixt[GROUP * g:GROUP * (g + 1), :].rearrange("(c p) t -> p c t", p=128), pz[:, :, :]
                               ).then_inc(S["p_stored"], 16)
            for t in range(FIRST_TOPK):
                pool.wait_ge(S["dist_made"], FIRST_TOPK)
                nc.gpsimd.affine_select(out=dist_of(t), in_=dist_of(t), compare_op=ALU.is_ge, fill=NEG_BIAS,
                                        base=128 * t, pattern=[[-1, keys_of(t)]], channel_multiplier=1
                                        ).then_inc(S["dist_masked"], 1)
            pool.wait_ge(S["kv_turned"], NTILE)
            pool.wait_ge(S["pages_in"], 16)
            for b in range(NSAMP):
                load_keys(pool, b, 1)
            pool.wait_ge(S["p_turned"], blocks_to(len(AUNITS)))
            for b in range(NSAMP):
                load_values(pool, b, 1)


_INS = ["x_prompt", "x_sample", "cache_k", "cache_v", "cache_idx_k", "state_pool", "page_table",
        "meta_tokens", "norm_g", "w_in", "w_pool", "pool_scale", "w_out", "final_norm_g"]
_OUTS = [("y_prompt", (1, SEQ, D)), ("y_sample", (NSAMP, 1, D)),
         ("new_k_prompt", (1, 1, L, KVH, HD)), ("new_v_prompt", (1, 1, L, KVH, HD)),
         ("new_idx_k_prompt", (1, 1, L, ID)), ("new_pool_prompt", (1, 1, PAD, POOLW)),
         ("new_k_sample", (1, NSAMP, 1, KVH, HD)), ("new_v_sample", (1, NSAMP, 1, KVH, HD)),
         ("new_idx_k_sample", (1, NSAMP, 1, ID)), ("new_pool_sample", (1, NSAMP, PAD, POOLW))]


def kernel(**inputs):
    import concourse.bacc as _bacc
    from concourse.bass_utils import run_bass_kernel_spmd as _run

    nc = _bacc.Bacc("TRN2", target_bir_lowering=False, num_devices=1, dynamic_dma_scratch_size=1024)
    arrays = {n: np.ascontiguousarray(inputs[n]) for n in _INS}
    arrays["consts"] = constants()
    io = {n: nc.dram_tensor(n, a.shape, mybir.dt.from_np(a.dtype), kind="ExternalInput").ap()
          for n, a in arrays.items()}
    for n, shape in _OUTS:
        io[n] = nc.dram_tensor(n, shape, F32, kind="ExternalOutput").ap()
    build(nc, io)
    r = _run(nc, [arrays], core_ids=[0])
    return tuple(r.results[0][n] for n, _ in _OUTS)
```
